# Optimizing a Trainium2 kernel written in Bass

```python
import math
import jax, jax.numpy as jnp
from jax import lax
import numpy as np

D_MODEL = 1024
BATCH = 1
SEQ = 1024
DEPTH = 1

CHUNK = 64
Q_BLOCK = 128
MLA_WIDTH = D_MODEL // 2
MLA_V_DIM = 64
MLA_HEADS = MLA_WIDTH // MLA_V_DIM
MLA_QK_NOPE = 64
MLA_QK_ROPE = 32
MLA_Q_RANK = D_MODEL // 4
MLA_KV_RANK = D_MODEL // 8
ROPE_THETA = 10000.0
GDN_WIDTH = D_MODEL // 4
GDN_HEAD_DIM = 64
GDN_HEADS = GDN_WIDTH // GDN_HEAD_DIM
GDN_CONV = 4
POOL_WIDTH = D_MODEL - MLA_WIDTH - GDN_WIDTH
POOL_WINDOWS = (2, 4, 8, 16)
POOL_GROUPS = 4
POOL_GROUP_DIM = POOL_WIDTH // POOL_GROUPS
MIX_WIDTH = MLA_WIDTH + GDN_WIDTH + POOL_WIDTH
IN_SIZES = (MLA_Q_RANK, MLA_KV_RANK, MLA_QK_ROPE, GDN_WIDTH, GDN_WIDTH, GDN_WIDTH, GDN_WIDTH, GDN_HEADS, GDN_HEADS, POOL_WIDTH)
IN_PROJ_DIM = sum(IN_SIZES)
N_GROUPS = 4
EXPERTS_PER_GROUP = 8
N_EXPERTS = N_GROUPS * EXPERTS_PER_GROUP
TOP_K = 2
EXPERT_FF = D_MODEL // 4
MOE_BLOCK = 128
DEEPNORM_ALPHA = (2 * DEPTH) ** 0.25
DEEPNORM_BETA = (8 * DEPTH) ** -0.25
LN_EPS = 1e-5
RMS_EPS = 1e-6


F32 = jnp.float32

def layer_norm(x, g, b):
    xf = x.astype(F32)
    mu = jnp.mean(xf, axis=-1, keepdims=True)
    var = jnp.mean(jnp.square(xf - mu), axis=-1, keepdims=True)
    return ((xf - mu) * lax.rsqrt(var + LN_EPS)).astype(x.dtype) * g + b

def rms_norm(x, g):
    xf = x.astype(F32)
    return (xf * lax.rsqrt(jnp.mean(xf * xf, axis=-1, keepdims=True) + RMS_EPS)).astype(x.dtype) * g

def l2_norm(x):
    xf = x.astype(F32)
    return xf * lax.rsqrt(jnp.sum(xf * xf, axis=-1, keepdims=True) + RMS_EPS)

def split_sizes(x, sizes):
    offs, acc = [], 0
    for s in sizes[:-1]:
        acc += s
        offs.append(acc)
    return jnp.split(x, offs, axis=-1)

def rope_tables(seq):
    inv_freq = jnp.power(ROPE_THETA, -jnp.arange(0, MLA_QK_ROPE, 2, dtype=F32) / MLA_QK_ROPE)
    ang = jnp.arange(seq, dtype=F32)[:, None] * inv_freq[None, :]
    return jnp.cos(ang), jnp.sin(ang)

def apply_rope(x, cos, sin):
    xf = x.astype(F32)
    x1, x2 = jnp.split(xf, 2, axis=-1)
    return jnp.concatenate([x1 * cos - x2 * sin, x2 * cos + x1 * sin], axis=-1).astype(x.dtype)

def mla_attention(c_q, c_kv, k_rope, q_norm_g, kv_norm_g, w_uq, w_ukv, cos, sin):
    B, S, _ = c_q.shape
    q = (rms_norm(c_q, q_norm_g) @ w_uq).reshape(B, S, MLA_HEADS, MLA_QK_NOPE + MLA_QK_ROPE)
    q_nope, q_rope = q[..., :MLA_QK_NOPE], q[..., MLA_QK_NOPE:]
    q_rope = apply_rope(q_rope, cos[:, None, :], sin[:, None, :])
    kv = (rms_norm(c_kv, kv_norm_g) @ w_ukv).reshape(B, S, MLA_HEADS, MLA_QK_NOPE + MLA_V_DIM)
    k_nope, v = kv[..., :MLA_QK_NOPE], kv[..., MLA_QK_NOPE:]
    k_rope = apply_rope(k_rope, cos, sin)
    scale = (MLA_QK_NOPE + MLA_QK_ROPE) ** -0.5
    outs = []
    for qb in range(S // Q_BLOCK):
        q0, kend = qb * Q_BLOCK, (qb + 1) * Q_BLOCK
        s = (jnp.einsum('bqhd,bkhd->bhqk', q_nope[:, q0:kend], k_nope[:, :kend])
             + jnp.einsum('bqhd,bkd->bhqk', q_rope[:, q0:kend], k_rope[:, :kend]))
        s = s.astype(F32) * scale
        q_chunk = jnp.arange(q0, kend) // CHUNK
        k_chunk = jnp.arange(kend) // CHUNK
        allowed = k_chunk[None, :] <= q_chunk[:, None]
        p = jax.nn.softmax(jnp.where(allowed, s, -jnp.inf), axis=-1).astype(v.dtype)
        outs.append(jnp.einsum('bhqk,bkhd->bqhd', p, v[:, :kend]))
    return jnp.concatenate(outs, axis=1).reshape(B, S, MLA_WIDTH)

def causal_depthwise_conv(x, w):
    C = x.shape[-1]
    return lax.conv_general_dilated(x, w[:, None, :].astype(x.dtype), window_strides=(1,),
                                    padding=[(GDN_CONV - 1, 0)],
                                    dimension_numbers=('NWC', 'WIO', 'NWC'),
                                    feature_group_count=C)

def gated_delta_rule(q, k, v, g, beta):
    B, S, H, dk = q.shape
    dv = v.shape[-1]
    nc = S // CHUNK

    def to_chunks(t):
        t = t.astype(F32).reshape((B, nc, CHUNK, H) + t.shape[3:])
        return jnp.moveaxis(t, 3, 1)

    qc = to_chunks(q) * dk ** -0.5
    kc, vc = to_chunks(k), to_chunks(v)
    gc = jnp.cumsum(to_chunks(g), axis=-1)
    bc = to_chunks(beta)
    idx = jnp.arange(CHUNK)
    incl = idx[:, None] >= idx[None, :]
    strict = idx[:, None] > idx[None, :]
    diff = gc[..., :, None] - gc[..., None, :]
    decay = jnp.where(incl, jnp.exp(jnp.where(incl, diff, 0.0)), 0.0)
    kb = kc * bc[..., None]
    a_mat = jnp.where(strict, jnp.einsum('bhnid,bhnjd->bhnij', kb, kc) * decay, 0.0)
    lower = a_mat + jnp.eye(CHUNK, dtype=F32)
    rhs = jnp.concatenate([vc * bc[..., None], kb * jnp.exp(gc)[..., None]], axis=-1)
    sol = lax.linalg.triangular_solve(lower, rhs, left_side=True, lower=True, unit_diagonal=True)
    u, w = sol[..., :dv], sol[..., dv:]
    qk = jnp.where(incl, jnp.einsum('bhnid,bhnjd->bhnij', qc, kc) * decay, 0.0)
    q_dec = qc * jnp.exp(gc)[..., None]
    k_dec = kc * jnp.exp(gc[..., -1:] - gc)[..., None]
    g_last = jnp.exp(gc[..., -1])

    def step(state, inp):
        q_i, k_i, u_i, w_i, qk_i, gl_i = inp
        v_new = u_i - jnp.einsum('bhck,bhkv->bhcv', w_i, state)
        o_i = jnp.einsum('bhck,bhkv->bhcv', q_i, state) + jnp.einsum('bhij,bhjv->bhiv', qk_i, v_new)
        state = state * gl_i[..., None, None] + jnp.einsum('bhck,bhcv->bhkv', k_i, v_new)
        return state, o_i

    xs = tuple(jnp.moveaxis(t, 2, 0) for t in (q_dec, k_dec, u, w, qk, g_last))
    _, o = lax.scan(step, jnp.zeros((B, H, dk, dv), F32), xs)
    o = jnp.moveaxis(o, 0, 2).reshape(B, H, S, dv)
    return jnp.transpose(o, (0, 2, 1, 3))

def gdn_mixer(q, k, v, z, a, b, conv_w, a_log, dt_bias, out_g):
    B, S, _ = q.shape
    qkv = jax.nn.silu(causal_depthwise_conv(jnp.concatenate([q, k, v], axis=-1), conv_w))
    q, k, v = jnp.split(qkv, 3, axis=-1)
    shp = (B, S, GDN_HEADS, GDN_HEAD_DIM)
    q, k, v = l2_norm(q.reshape(shp)), l2_norm(k.reshape(shp)), v.reshape(shp)
    g = -jnp.exp(a_log.astype(F32)) * jax.nn.softplus(a.astype(F32) + dt_bias.astype(F32))
    beta = jax.nn.sigmoid(b.astype(F32))
    o = gated_delta_rule(q, k, v, g, beta).astype(z.dtype)
    o = rms_norm(o, out_g) * jax.nn.silu(z.reshape(shp))
    return o.reshape(B, S, GDN_WIDTH)

def pool_mixer(p, pool_w, pool_scale):
    B, S, _ = p.shape
    pg = p.reshape(B, S, POOL_GROUPS, POOL_GROUP_DIM).astype(F32)
    cs = jnp.cumsum(pg, axis=1)
    cs = jnp.concatenate([jnp.zeros_like(cs[:, :1]), cs], axis=1)
    t = jnp.arange(S)
    means = []
    for gi, win in enumerate(POOL_WINDOWS):
        start = jnp.maximum(t + 1 - win, 0)
        cnt = (t + 1 - start).astype(F32)
        cs_g = cs[:, :, gi, :]
        means.append((cs_g[:, 1:] - cs_g[:, start]) / cnt[None, :, None])
    delta = (jnp.stack(means, axis=2) - pg).astype(p.dtype)
    mixed = jnp.einsum('bsgc,gcd->bsgd', delta, pool_w)
    return mixed.reshape(B, S, POOL_WIDTH) * pool_scale

def hybrid_mixer(h, w_in, q_norm_g, kv_norm_g, w_uq, w_ukv, conv_w, a_log, dt_bias, gdn_g,
                 pool_w, pool_scale, w_out, cos, sin):
    proj = h @ w_in
    c_q, c_kv, k_rope, gq, gk, gv, gz, ga, gb, p = split_sizes(proj, IN_SIZES)
    y_mla = mla_attention(c_q, c_kv, k_rope, q_norm_g, kv_norm_g, w_uq, w_ukv, cos, sin)
    y_gdn = gdn_mixer(gq, gk, gv, gz, ga, gb, conv_w, a_log, dt_bias, gdn_g)
    y_pool = pool_mixer(p, pool_w, pool_scale)
    return jnp.concatenate([y_mla, y_gdn, y_pool], axis=-1) @ w_out

def grouped_expert_ffn(hf, expert, weights, w_gate, w_up, w_down):
    T, D = hf.shape
    A = T * TOP_K
    flat_e = expert.reshape(A)
    flat_tok = jnp.arange(A, dtype=jnp.int32) // TOP_K
    flat_w = weights.reshape(A).astype(hf.dtype)
    order = jnp.argsort(flat_e)
    se = flat_e[order]
    counts = jax.ops.segment_sum(jnp.ones((A,), jnp.int32), flat_e, num_segments=N_EXPERTS)
    padded = (counts + MOE_BLOCK - 1) // MOE_BLOCK * MOE_BLOCK
    pad_end = jnp.cumsum(padded)
    pad_start = pad_end - padded
    start = jnp.cumsum(counts) - counts
    dest = pad_start[se] + (jnp.arange(A, dtype=jnp.int32) - start[se])
    nb = (A + N_EXPERTS * (MOE_BLOCK - 1) + MOE_BLOCK - 1) // MOE_BLOCK
    P = nb * MOE_BLOCK
    buf_tok = jnp.full((P,), T, jnp.int32).at[dest].set(flat_tok[order])
    buf_w = jnp.zeros((P,), hf.dtype).at[dest].set(flat_w[order])
    block_expert = jnp.clip(jnp.searchsorted(pad_end, jnp.arange(nb) * MOE_BLOCK, side='right'), 0, N_EXPERTS - 1)
    xpad = jnp.concatenate([hf, jnp.zeros((1, D), hf.dtype)], axis=0)
    xb = xpad[buf_tok].reshape(nb, MOE_BLOCK, D)

    def block_ffn(args):
        xb_i, e = args
        return (jax.nn.silu(xb_i @ w_gate[e]) * (xb_i @ w_up[e])) @ w_down[e]

    yb = lax.map(block_ffn, (xb, block_expert)).reshape(P, D)
    out = jnp.zeros((T + 1, D), yb.dtype).at[buf_tok].add(yb * buf_w[:, None])
    return out[:T]

def hierarchical_moe(h, w_rg, b_rg, w_re, b_re, w_gate, w_up, w_down):
    B, S, D = h.shape
    hf = h.reshape(B * S, D)
    g_prob = jax.nn.softmax((hf @ w_rg + b_rg).astype(F32), axis=-1)
    g_p, g_sel = lax.top_k(g_prob, 1)
    e_logit = (hf @ w_re + b_re).astype(F32).reshape(-1, N_GROUPS, EXPERTS_PER_GROUP)
    e_logit = jnp.take_along_axis(e_logit, g_sel[:, :, None], axis=1)[:, 0]
    e_p, e_idx = lax.top_k(jax.nn.softmax(e_logit, axis=-1), TOP_K)
    weights = g_p * e_p / jnp.sum(e_p, axis=-1, keepdims=True)
    expert = g_sel * EXPERTS_PER_GROUP + e_idx
    return grouped_expert_ffn(hf, expert, weights, w_gate, w_up, w_down).reshape(B, S, D)

def first_inputs(seed: int = 0) -> dict:
    key = jax.random.key(seed)
    ks = jax.random.split(key, 32)
    L, D = DEPTH, D_MODEL

    def nrm(k, shape, scale):
        return jax.random.normal(k, shape, F32) * scale

    dt = jnp.exp(jax.random.uniform(ks[9], (L, GDN_HEADS), F32, math.log(1e-3), math.log(1e-1)))
    return {
        'x': nrm(ks[0], (BATCH, SEQ, D), 1.0),
        'c': nrm(ks[1], (BATCH, D), 1.0),
        'w_in': nrm(ks[2], (L, D, IN_PROJ_DIM), D ** -0.5),
        'mla_q_norm': 1.0 + nrm(ks[3], (L, MLA_Q_RANK), 0.05),
        'mla_kv_norm': 1.0 + nrm(ks[4], (L, MLA_KV_RANK), 0.05),
        'mla_w_uq': nrm(ks[5], (L, MLA_Q_RANK, MLA_HEADS * (MLA_QK_NOPE + MLA_QK_ROPE)), MLA_Q_RANK ** -0.5),
        'mla_w_ukv': nrm(ks[6], (L, MLA_KV_RANK, MLA_HEADS * (MLA_QK_NOPE + MLA_V_DIM)), MLA_KV_RANK ** -0.5),
        'gdn_conv': nrm(ks[7], (L, GDN_CONV, 3 * GDN_WIDTH), GDN_CONV ** -0.5),
        'gdn_a_log': jnp.log(jax.random.uniform(ks[8], (L, GDN_HEADS), F32, 1.0, 16.0)),
        'gdn_dt_bias': dt + jnp.log(-jnp.expm1(-dt)),
        'gdn_out_norm': 1.0 + nrm(ks[10], (L, GDN_HEAD_DIM), 0.05),
        'pool_w': nrm(ks[11], (L, POOL_GROUPS, POOL_GROUP_DIM, POOL_GROUP_DIM), POOL_GROUP_DIM ** -0.5),
        'pool_scale': 1.0 + nrm(ks[12], (L, POOL_WIDTH), 0.05),
        'w_out': nrm(ks[13], (L, MIX_WIDTH, D), MIX_WIDTH ** -0.5 * DEEPNORM_BETA),
        'w_mod': nrm(ks[14], (L, D, 6 * D), 0.2 * D ** -0.5),
        'b_mod': nrm(ks[15], (L, 6 * D), 0.02),
        'ln1_g': 1.0 + nrm(ks[16], (L, D), 0.05),
        'ln1_b': nrm(ks[17], (L, D), 0.02),
        'ln2_g': 1.0 + nrm(ks[18], (L, D), 0.05),
        'ln2_b': nrm(ks[19], (L, D), 0.02),
        'router_w_group': nrm(ks[20], (L, D, N_GROUPS), D ** -0.5),
        'router_b_group': nrm(ks[21], (L, N_GROUPS), 0.01),
        'router_w_expert': nrm(ks[22], (L, D, N_EXPERTS), D ** -0.5),
        'router_b_expert': nrm(ks[23], (L, N_EXPERTS), 0.01),
        'moe_w_gate': nrm(ks[24], (L, N_EXPERTS, D, EXPERT_FF), D ** -0.5),
        'moe_w_up': nrm(ks[25], (L, N_EXPERTS, D, EXPERT_FF), D ** -0.5),
        'moe_w_down': nrm(ks[26], (L, N_EXPERTS, EXPERT_FF, D), EXPERT_FF ** -0.5 * DEEPNORM_BETA),
    }

def first_block(x, c, w_in, mla_q_norm, mla_kv_norm, mla_w_uq, mla_w_ukv, gdn_conv, gdn_a_log,
              gdn_dt_bias, gdn_out_norm, pool_w, pool_scale, w_out, w_mod, b_mod, ln1_g, ln1_b,
              ln2_g, ln2_b, router_w_group, router_b_group, router_w_expert, router_b_expert,
              moe_w_gate, moe_w_up, moe_w_down):
    cos, sin = rope_tables(x.shape[1])
    c_act = jax.nn.silu(c)
    for l in range(DEPTH):
        mod = c_act @ w_mod[l] + b_mod[l]
        sh1, sc1, gt1, sh2, sc2, gt2 = [m[:, None, :] for m in jnp.split(mod, 6, axis=-1)]
        h = x * (1.0 + sc1) + sh1
        y = hybrid_mixer(h, w_in[l], mla_q_norm[l], mla_kv_norm[l], mla_w_uq[l], mla_w_ukv[l],
                         gdn_conv[l], gdn_a_log[l], gdn_dt_bias[l], gdn_out_norm[l],
                         pool_w[l], pool_scale[l], w_out[l], cos, sin)
        x = layer_norm(DEEPNORM_ALPHA * x + (1.0 + gt1) * y, ln1_g[l], ln1_b[l])
        h = x * (1.0 + sc2) + sh2
        y = hierarchical_moe(h, router_w_group[l], router_b_group[l], router_w_expert[l],
                             router_b_expert[l], moe_w_gate[l], moe_w_up[l], moe_w_down[l])
        x = layer_norm(DEEPNORM_ALPHA * x + (1.0 + gt2) * y, ln2_g[l], ln2_b[l])
    return x


GRID_W = 64
N_HEADS = 8
HEAD_DIM = 64
ATTN_W = N_HEADS * HEAD_DIM
NA_WIN_H = 8
NA_WIN_W = 16
SSM_W = 512
SSM_GROUP = 16
SSM_GROUPS = SSM_W // SSM_GROUP
SSM_STATE = 64
N_DIR = 2
DT_MIN = 1e-3
DT_MAX = 1e-1
LAMBDA_RE_MAX = -1e-4
N_BRANCH = 2
IN_COLS = 3 * ATTN_W + SSM_W + N_BRANCH * D_MODEL
D_FF = 2816
PLE_DIM = 256


def rms_norm_2(x, g):
    xf = x.astype(jnp.float32)
    y = xf * lax.rsqrt(jnp.mean(xf * xf, axis=-1, keepdims=True) + RMS_EPS)
    return (y * g.astype(jnp.float32)).astype(x.dtype)

def swiglu(x, w_gate, w_up, w_down):
    return (jax.nn.silu(x @ w_gate) * (x @ w_up)) @ w_down

def neighbourhood_attention(q, k, v, rpb):
    bn, s, h, hd = q.shape
    rows = s // GRID_W
    wh = min(NA_WIN_H, rows)
    ww = NA_WIN_W
    scale = hd ** -0.5
    qg = q.reshape(bn, rows, GRID_W, h, hd)
    kg = k.reshape(bn, rows, GRID_W, h, hd)
    vg = v.reshape(bn, rows, GRID_W, h, hd)
    cols = jnp.arange(GRID_W)
    col_start = jnp.clip(cols - ww // 2, 0, GRID_W - ww)
    col_idx = col_start[:, None] + jnp.arange(ww)[None, :]
    dc_idx = col_idx - cols[:, None] + (NA_WIN_W - 1)

    def row_block(r):
        rs = jnp.clip(r - wh // 2, 0, rows - wh)
        kr = lax.dynamic_slice_in_dim(kg, rs, wh, axis=1)
        vr = lax.dynamic_slice_in_dim(vg, rs, wh, axis=1)
        kn = kr[:, :, col_idx]
        vn = vr[:, :, col_idx]
        qr = lax.dynamic_index_in_dim(qg, r, axis=1, keepdims=False)
        dr_idx = rs + jnp.arange(wh) - r + (NA_WIN_H - 1)
        bias = rpb[:, dr_idx[:, None, None], dc_idx[None]]
        bias = bias.transpose(0, 2, 1, 3)
        sc = jnp.einsum('bchd,brcwhd->bhcrw', qr, kn) * scale + bias[None]
        sc = sc.reshape(bn, h, GRID_W, wh * ww).astype(jnp.float32)
        pr = jax.nn.softmax(sc, axis=-1).astype(v.dtype).reshape(bn, h, GRID_W, wh, ww)
        return jnp.einsum('bhcrw,brcwhd->bchd', pr, vn)

    out = lax.map(row_block, jnp.arange(rows))
    return out.transpose(1, 0, 2, 3, 4).reshape(bn, s, h * hd)

def _ssm_combine(ei, ej):
    a_i, b_i = ei
    a_j, b_j = ej
    return a_j * a_i, a_j * b_i + b_j

def s5_scan(u, lam_re, lam_im, log_dt, b_re, b_im, c_re, c_im, reverse):
    f32 = jnp.float32
    s = u.shape[1]
    lam = lax.complex(jnp.minimum(lam_re.astype(f32), LAMBDA_RE_MAX), lam_im.astype(f32))
    dt = jnp.exp(log_dt.astype(f32))[:, None]
    lam_bar = jnp.exp(lam * dt)
    b_bar = ((lam_bar - 1.0) / lam)[..., None] * lax.complex(b_re.astype(f32), b_im.astype(f32))
    bu = lax.complex(jnp.einsum('bsgi,gpi->bsgp', u, b_bar.real),
                     jnp.einsum('bsgi,gpi->bsgp', u, b_bar.imag))
    a = jnp.broadcast_to(lam_bar, (1, s) + lam_bar.shape)
    _, states = lax.associative_scan(_ssm_combine, (a, bu), reverse=reverse, axis=1)
    return (jnp.einsum('bsgp,gop->bsgo', states.real, c_re.astype(f32))
            - jnp.einsum('bsgp,gop->bsgo', states.imag, c_im.astype(f32)))

def s5_branch(s_in, lam_re, lam_im, log_dt, b_re, b_im, c_re, c_im, d_skip, glu_w, glu_b):
    f32 = jnp.float32
    bn, s, _ = s_in.shape
    u = s_in.astype(f32).reshape(bn, s, SSM_GROUPS, SSM_GROUP)
    y = d_skip.astype(f32).reshape(SSM_GROUPS, SSM_GROUP) * u
    for direction in range(N_DIR):
        y = y + s5_scan(u, lam_re[direction], lam_im[direction], log_dt[direction],
                        b_re[direction], b_im[direction], c_re[direction], c_im[direction],
                        reverse=(direction == 1))
    y = jax.nn.gelu(y.reshape(bn, s, SSM_W))
    y = y * jax.nn.sigmoid(y @ glu_w.astype(f32) + glu_b.astype(f32))
    return y.astype(s_in.dtype)

def second_inputs(seed: int = 0) -> dict:
    key = jax.random.key(seed)
    ks = iter(jax.random.split(key, 48))
    L = DEPTH
    f32 = jnp.float32

    def nrm(shape, fan_in):
        return jax.random.normal(next(ks), shape, f32) * fan_in ** -0.5

    def gain(shape):
        return 1.0 + 0.05 * jax.random.normal(next(ks), shape, f32)

    def small(shape, scale):
        return scale * jax.random.normal(next(ks), shape, f32)

    G, P, GC = SSM_GROUPS, SSM_STATE, SSM_GROUP
    return {
        "x": jax.random.normal(next(ks), (BATCH, SEQ, D_MODEL), f32),
        "p": jax.random.normal(next(ks), (DEPTH, BATCH, SEQ, PLE_DIM), f32),
        "ffn1_norm": gain((L, D_MODEL)),
        "ffn1_w_gate": nrm((L, D_MODEL, D_FF), D_MODEL),
        "ffn1_w_up": nrm((L, D_MODEL, D_FF), D_MODEL),
        "ffn1_w_down": nrm((L, D_FF, D_MODEL), D_FF),
        "mix_norm": gain((L, D_MODEL)),
        "w_in": nrm((L, D_MODEL, IN_COLS), D_MODEL),
        "na_rpb": small((L, N_HEADS, 2 * NA_WIN_H - 1, 2 * NA_WIN_W - 1), 0.02),
        "ssm_lam_re": -0.5 + small((L, N_DIR, G, P), 0.01),
        "ssm_lam_im": math.pi * jnp.arange(P, dtype=f32) + small((L, N_DIR, G, P), 0.01),
        "ssm_log_dt": jax.random.uniform(next(ks), (L, N_DIR, G), f32,
                                         minval=math.log(DT_MIN), maxval=math.log(DT_MAX)),
        "ssm_b_re": nrm((L, N_DIR, G, P, GC), 2 * GC),
        "ssm_b_im": nrm((L, N_DIR, G, P, GC), 2 * GC),
        "ssm_c_re": nrm((L, N_DIR, G, GC, P), 2 * P),
        "ssm_c_im": nrm((L, N_DIR, G, GC, P), 2 * P),
        "ssm_d": jax.random.normal(next(ks), (L, SSM_W), f32),
        "ssm_glu_w": nrm((L, SSM_W, SSM_W), SSM_W),
        "ssm_glu_b": small((L, SSM_W), 0.01),
        "w_attn_out": nrm((L, ATTN_W, D_MODEL), ATTN_W),
        "w_ssm_out": nrm((L, SSM_W, D_MODEL), SSM_W),
        "w_out": nrm((L, D_MODEL, D_MODEL), D_MODEL),
        "ffn2_norm": gain((L, D_MODEL)),
        "ffn2_w_gate": nrm((L, D_MODEL, D_FF), D_MODEL),
        "ffn2_w_up": nrm((L, D_MODEL, D_FF), D_MODEL),
        "ffn2_w_down": nrm((L, D_FF, D_MODEL), D_FF),
        "ple_norm": gain((L, D_MODEL)),
        "ple_w_gate": nrm((L, D_MODEL, D_MODEL), D_MODEL),
        "ple_w_proj": nrm((L, PLE_DIM, D_MODEL), PLE_DIM),
        "final_norm": gain((D_MODEL,)),
    }

def second_block(x, p, ffn1_norm, ffn1_w_gate, ffn1_w_up, ffn1_w_down, mix_norm, w_in, na_rpb,
              ssm_lam_re, ssm_lam_im, ssm_log_dt, ssm_b_re, ssm_b_im, ssm_c_re, ssm_c_im,
              ssm_d, ssm_glu_w, ssm_glu_b, w_attn_out, w_ssm_out, w_out,
              ffn2_norm, ffn2_w_gate, ffn2_w_up, ffn2_w_down,
              ple_norm, ple_w_gate, ple_w_proj, final_norm):
    bn, s, _ = x.shape
    splits = [ATTN_W, 2 * ATTN_W, 3 * ATTN_W, 3 * ATTN_W + SSM_W]
    h = x
    for i in range(DEPTH):
        h = h + 0.5 * swiglu(rms_norm_2(h, ffn1_norm[i]), ffn1_w_gate[i], ffn1_w_up[i], ffn1_w_down[i])
        u = rms_norm_2(h, mix_norm[i])
        z = u @ w_in[i]
        q, k, v, s_in, gates = jnp.split(z, splits, axis=-1)
        y_attn = neighbourhood_attention(q.reshape(bn, s, N_HEADS, HEAD_DIM),
                                         k.reshape(bn, s, N_HEADS, HEAD_DIM),
                                         v.reshape(bn, s, N_HEADS, HEAD_DIM),
                                         na_rpb[i]) @ w_attn_out[i]
        y_ssm = s5_branch(s_in, ssm_lam_re[i], ssm_lam_im[i], ssm_log_dt[i],
                          ssm_b_re[i], ssm_b_im[i], ssm_c_re[i], ssm_c_im[i],
                          ssm_d[i], ssm_glu_w[i], ssm_glu_b[i]) @ w_ssm_out[i]
        g_attn, g_ssm = jnp.split(jax.nn.sigmoid(gates), N_BRANCH, axis=-1)
        h = h + (g_attn * y_attn + g_ssm * y_ssm) @ w_out[i]
        h = h + 0.5 * swiglu(rms_norm_2(h, ffn2_norm[i]), ffn2_w_gate[i], ffn2_w_up[i], ffn2_w_down[i])
        h = h + (p[i] @ ple_w_proj[i]) * jax.nn.sigmoid(rms_norm_2(h, ple_norm[i]) @ ple_w_gate[i])
    return rms_norm_2(h, final_norm)


def setup_inputs(seed=0):
    out = dict(first_inputs(seed))
    for name, value in second_inputs(seed + 1).items():
        if name != "x":
            out[name + "_2"] = value
    return out


def reference(
    x, c, w_in, mla_q_norm, mla_kv_norm, mla_w_uq, mla_w_ukv, gdn_conv, gdn_a_log, gdn_dt_bias,
    gdn_out_norm, pool_w, pool_scale, w_out, w_mod, b_mod, ln1_g, ln1_b, ln2_g, ln2_b,
    router_w_group, router_b_group, router_w_expert, router_b_expert, moe_w_gate, moe_w_up,
    moe_w_down, p_2, ffn1_norm_2, ffn1_w_gate_2, ffn1_w_up_2, ffn1_w_down_2, mix_norm_2, w_in_2,
    na_rpb_2, ssm_lam_re_2, ssm_lam_im_2, ssm_log_dt_2, ssm_b_re_2, ssm_b_im_2, ssm_c_re_2,
    ssm_c_im_2, ssm_d_2, ssm_glu_w_2, ssm_glu_b_2, w_attn_out_2, w_ssm_out_2, w_out_2,
    ffn2_norm_2, ffn2_w_gate_2, ffn2_w_up_2, ffn2_w_down_2, ple_norm_2, ple_w_gate_2,
    ple_w_proj_2, final_norm_2,
):
    x = first_block(
        x, c, w_in, mla_q_norm, mla_kv_norm, mla_w_uq, mla_w_ukv, gdn_conv, gdn_a_log,
        gdn_dt_bias, gdn_out_norm, pool_w, pool_scale, w_out, w_mod, b_mod, ln1_g, ln1_b, ln2_g,
        ln2_b, router_w_group, router_b_group, router_w_expert, router_b_expert, moe_w_gate,
        moe_w_up, moe_w_down,
    )
    return second_block(
        x, p_2, ffn1_norm_2, ffn1_w_gate_2, ffn1_w_up_2, ffn1_w_down_2, mix_norm_2, w_in_2,
        na_rpb_2, ssm_lam_re_2, ssm_lam_im_2, ssm_log_dt_2, ssm_b_re_2, ssm_b_im_2, ssm_c_re_2,
        ssm_c_im_2, ssm_d_2, ssm_glu_w_2, ssm_glu_b_2, w_attn_out_2, w_ssm_out_2, w_out_2,
        ffn2_norm_2, ffn2_w_gate_2, ffn2_w_up_2, ffn2_w_down_2, ple_norm_2, ple_w_gate_2,
        ple_w_proj_2, final_norm_2,
    )


_drawn_inputs = setup_inputs


def setup_inputs(seed=0):
    import zlib

    import numpy as np

    out = dict(_drawn_inputs(seed))
    spreads = {}
    factors = {'mla_q_norm': 8.0,
     'mla_kv_norm': 6.065,
     'gdn_out_norm': 3.46,
     'pool_scale': 3.654,
     'router_b_group': 8.0,
     'router_b_expert': 8.0,
     'ffn1_norm_2': 2.93,
     'mix_norm_2': 4.642,
     'na_rpb_2': 8.0,
     'ssm_lam_re_2': 64.0,
     'ssm_lam_im_2': 18.203,
     'ssm_log_dt_2': 18.929,
     'ssm_b_re_2': 35.968,
     'ssm_b_im_2': 37.375,
     'ssm_c_re_2': 35.597,
     'ssm_c_im_2': 35.936,
     'ssm_glu_b_2': 64.0,
     'ffn2_norm_2': 3.345,
     'ple_norm_2': 51.744}
    for name, (base, spread) in spreads.items():
        noise = np.random.default_rng([zlib.crc32(name.encode()), seed]).standard_normal(out[name].shape)
        drawn = base * np.exp(spread * noise) if base else spread * noise
        out[name] = __import__('jax').numpy.asarray(drawn.astype(out[name].dtype))
    for name, factor in factors.items():
        out[name] = (out[name] * factor).astype(out[name].dtype)
    return out
```

```python
from contextlib import ExitStack
import concourse.bass as bass
from concourse import mybir

P = 128
F32 = mybir.dt.float32
I32 = mybir.dt.int32
U32 = mybir.dt.uint32
ALU = mybir.AluOpType
ACT = mybir.ActivationFunctionType
AX = mybir.AxisListType.X

SEQ, D = 1024, 1024
TT = SEQ // P
KT = D // P
NW = 512


class Steps:

    def __init__(self, eng, sem, at=0):
        self.eng, self.sem, self.at, self.n = eng, sem, at, 0

    def __call__(self, ins):
        self.n += 1
        ins.then_inc(self.sem, 1)
        self.eng.wait_ge(self.sem, self.at + self.n)


class Stage:

    def __init__(self, nc, name):
        self.nc, self.name, self.ctx, self.sems = nc, name, ExitStack(), []

    def __enter__(self):
        return self

    def __exit__(self, *what):
        self.ctx.close()
        self.nc.clear_and_free_semaphores(self.sems)
        self.nc.all_engine_barrier()

    def sb(self, name, shape, dt=F32):
        return self.ctx.enter_context(self.nc.sbuf_tensor(f"{self.name}_{name}", shape, dt))

    def ps(self, name, shape, dt=F32):
        return self.ctx.enter_context(self.nc.psum_tensor(f"{self.name}_{name}", shape, dt))

    def sem(self, name):
        self.sems.append(self.nc.alloc_semaphore(f"{self.name}_{name}"))
        return self.sems[-1]


def stage_modulation(nc, I, mod):
    CH = 6 * D // NW
    SL = 4
    with Stage(nc, "mod") as s:
        ccol, cact = s.sb("ccol", [P, KT]), s.sb("cact", [P, KT])
        crep = s.sb("crep", [P, KT, P])
        ones = s.sb("ones", [1, P])
        bias = s.sb("bias", [1, 6 * D])
        w = s.sb("w", [P, SL, KT, NW])
        acc = s.ps("acc", [P, SL, NW])
        c_in, b_in, act_c, rep_c, ones_c = (s.sem(x) for x in ("c_in", "b_in", "act_c", "rep_c", "ones_c"))
        w_in = [s.sem(f"w_in{j}") for j in range(SL)]
        w_free, acc_ready, acc_free = s.sem("w_free"), s.sem("acc_ready"), s.sem("acc_free")
        wv = I["w_mod"][0].rearrange("(k p) n -> p k n", p=P)
        block = s.ctx.enter_context(nc.Block())

        @block.sync
        def _(sp):
            sp.dma_start(ccol[:], I["c"][0].rearrange("(k p) -> p k", p=P)).then_inc(c_in, 16)
            sp.dma_start(bias[:], I["b_mod"]).then_inc(b_in, 16)
            with sp.Fori(0, CH // SL) as i:
                for j in range(SL):
                    sp.wait_ge(w_free, i * SL + j + 1)
                    sp.dma_start(w[:, j], wv[:, :, bass.ds(i * (SL * NW) + j * NW, NW)]).then_inc(w_in[j], 16)

        @block.scalar
        def _(act):
            act.wait_ge(c_in, 16)
            act.activation(cact[:], ccol[:], ACT.Silu).then_inc(act_c, 1)

        @block.gpsimd
        def _(pool):
            pool.memset(ones[:], 1.0).then_inc(ones_c, 1)
            pool.wait_ge(act_c, 1)
            pool.tensor_copy(crep[:], cact[:].unsqueeze(2).broadcast_to([P, KT, P])).then_inc(rep_c, 1)

        @block.tensor
        def _(pe):
            pe.sem_inc(w_free, SL)
            pe.wait_ge(rep_c, 1)
            pe.wait_ge(ones_c, 1)
            pe.wait_ge(b_in, 16)
            with pe.Fori(0, CH // SL) as i:
                for j in range(SL):
                    pe.wait_ge(acc_free, i * SL + j + 1)
                    pe.wait_ge(w_in[j], i * 16 + 16)
                    for k in range(KT):
                        mm = pe.matmul(acc[:, j], crep[:, k], w[:, j, k], start=(k == 0), stop=False)
                    mm.then_inc(w_free, 1)
                    pe.matmul(acc[:, j], ones[:], bias[:, bass.ds(i * (SL * NW) + j * NW, NW)],
                              start=False, stop=True).then_inc(acc_ready, 1)

        @block.vector
        def _(dve):
            dve.sem_inc(acc_free, SL)
            with dve.Fori(0, CH // SL) as i:
                for j in range(SL):
                    dve.wait_ge(acc_ready, i * SL + j + 1)
                    dve.tensor_copy(mod[:, bass.ds(i * (SL * NW) + j * NW, NW)], acc[:, j]).then_inc(acc_free, 1)


def stage_features(nc, name, src, dst, ident, scale=None, bias=None, spread=False):
    kt = src.shape[2] // P
    n = kt * 2
    with Stage(nc, name) as s:
        turned = s.ps("turned", [P, 4, NW])
        ready, free_a, free_d = s.sem("turned_ready"), s.sem("act_took"), s.sem("dve_took")
        block = s.ctx.enter_context(nc.Block())

        @block.tensor
        def _(pe):
            for g in range(n):
                k, half = g // 2, g % 2
                if g >= 4:
                    pe.wait_ge((free_a, free_d)[g % 2], (g - 4) // 2 + 1)
                for q in range(4):
                    mm = pe.transpose(turned[:, g % 4, q * P:(q + 1) * P],
                                      src[:, 4 * half + q].rearrange("p (c k) -> p k c", k=kt)[:, k] if spread
                                      else src[:, 4 * half + q, k * P:(k + 1) * P], ident)
                mm.then_inc(ready, 1)

        @block.scalar
        def _(act):
            for g in range(0, n, 2):
                act.wait_ge(ready, g + 1)
                k = g // 2
                act.activation(dst[:, k, 0:NW], turned[:, g % 4], ACT.Identity,
                               bias=0.0 if bias is None else bias[:, k:k + 1],
                               scale=1.0 if scale is None else scale[:, k:k + 1]).then_inc(free_a, 1)

        @block.vector
        def _(dve):
            for g in range(1, n, 2):
                dve.wait_ge(ready, g + 1)
                k = g // 2
                o, i = dst[:, k, NW:2 * NW], turned[:, g % 4]
                if scale is None:
                    ins = dve.tensor_copy(o, i)
                elif bias is None:
                    ins = dve.tensor_scalar(o, i, scale[:, k:k + 1], None, ALU.mult)
                else:
                    ins = dve.tensor_scalar(o, i, scale[:, k:k + 1], bias[:, k:k + 1], ALU.mult, ALU.add)
                ins.then_inc(free_d, 1)


def stage_load(nc, name, pairs):
    with Stage(nc, name) as s:
        loaded = s.sem("loaded")
        block = s.ctx.enter_context(nc.Block())

        @block.sync
        def _(sp):
            for dst, src in pairs:
                sp.dma_start(dst, src).then_inc(loaded, 16)
            sp.wait_ge(loaded, 16 * len(pairs))


def stage_columns(nc, name, rows, ones, cols):
    with Stage(nc, name) as s:
        n = sum(r.shape[1] // P for r, _ in rows)
        acc = s.ps("acc", [P, NW])
        turned, done = s.sem("turned"), s.sem("done")
        block = s.ctx.enter_context(nc.Block())

        @block.tensor
        def _(pe):
            c = 0
            for r, _ in rows:
                for k in range(r.shape[1] // P):
                    mm = pe.matmul(acc[:, c:c + 1], r[:, k * P:(k + 1) * P], ones[0:1, 0:1],
                                   start=True, stop=True, skip_group_check=True)
                    c += 1
            mm.then_inc(turned, 1)

        @block.vector
        def _(dve):
            dve.wait_ge(turned, 1)
            c = 0
            for r, one in rows:
                k = r.shape[1] // P
                dve.tensor_scalar(cols[:, c:c + k], acc[:, c:c + k], float(one), None, ALU.add).then_inc(done, 1)
                c += k


Q_RANK, KV_RANK, ROPE = 256, 128, 32
LAT = Q_RANK + KV_RANK + ROPE
GW = 256
GH, GD = 4, 64
CONV = 4
O_G, O_Z, O_P = LAT, LAT + 3 * GW, LAT + 4 * GW + 2 * GH
ZAB = GW + 2 * GH
PADW = 16


def stage_projections(nc, I, hT, ident, kc, lat, zab, gqkv, yT):
    NC = 8
    with Stage(nc, "proj") as s:
        wt = s.sb("w_tokens", [P, KT, LAT + ZAB])
        wf = s.sb("w_features", [P, 2, KT, P])
        cin = s.sb("conv_in", [P, PADW + SEQ])
        cout = s.sb("conv_out", [P, PADW + SEQ])
        cact = s.sb("conv_act", [P, SEQ])
        psum2 = s.sb("pool_sum", [P, PADW + SEQ])
        s_bufs = (cout, psum2)
        cw = s.sb("conv_w", [P, 6, CONV])
        pw = s.sb("pool_w", [P, 2, P])
        psc = s.sb("pool_scale", [P, 2])
        rc = s.sb("rc", [P, 2, PADW])
        tok = s.ps("tok", [P, 2, 2, NW])
        feat = s.ps("feat", [P, 2, NW])
        turn = s.ps("turn", [P, TT, P])
        wt_in, par_in, tok_ready, tok_free = s.sem("wt_in"), s.sem("par_in"), s.sem("tok_ready"), s.sem("tok_free")
        wf_in = [s.sem("wf_in0"), s.sem("wf_in1")]
        feat_ready, feat_free = s.sem("feat_ready"), s.sem("feat_free")
        conv_done, act_done, turn_ready, turn_free = s.sem("conv_done"), s.sem("act_done"), s.sem("turn_ready"), s.sem("turn_free")
        zeroed = s.sem("zeroed")
        cin_ready, dchain, delta_done, mix_ready, mix_free = s.sem("cin_ready"), s.sem("dchain"), s.sem("delta_done"), s.sem("mix_ready"), s.sem("mix_free")
        w = I["w_in"][0].rearrange("(k p) n -> p k n", p=P)
        block = s.ctx.enter_context(nc.Block())
        offs = [O_G + j * P for j in range(6)] + [O_P, O_P + P]

        @block.sync
        def _(sp):
            sp.dma_start(wt[:, :, 0:LAT], w[:, :, 0:LAT]).then_inc(wt_in, 16)
            sp.dma_start(wt[:, :, LAT:], w[:, :, O_Z:O_Z + ZAB]).then_inc(wt_in, 16)
            for i in range(CONV):
                sp.dma_start(cw[:, :, i], I["gdn_conv"][0, i].rearrange("(j p) -> p j", p=P)).then_inc(par_in, 16)
            sp.wait_ge(zeroed, 1)
            for g in range(2):
                r = slice(64 * g, 64 * g + 64)
                sp.dma_start(pw[r, :, r], I["pool_w"][0].rearrange("(j h) c d -> h c j d", h=2)[g]).then_inc(par_in, 16)
            sp.dma_start(psc[:], I["pool_scale"][0].rearrange("(j p) -> p j", p=P)).then_inc(par_in, 16)
            sp.dma_start(rc[:], kc["pool_rc"]).then_inc(par_in, 16)
            for j in range(NC):
                if j >= 2:
                    sp.wait_ge(feat_ready, j - 1)
                sp.dma_start(wf[:, j % 2], w[:, :, offs[j]:offs[j] + P]).then_inc(wf_in[j % 2], 16)

        @block.tensor
        def _(pe):
            def features(j):
                pe.wait_ge(wf_in[j % 2], 16 * (j // 2 + 1))
                if j:
                    pe.wait_ge(feat_free, j)
                for half in range(2):
                    for k in range(KT):
                        mm = pe.matmul(feat[:, half], wf[:, j % 2, k], hT[:, k, half * NW:(half + 1) * NW],
                                       start=(k == 0), stop=(k == KT - 1))
                mm.then_inc(feat_ready, 1)

            def turned(j):
                pe.wait_ge(act_done, j + 1)
                if j:
                    pe.wait_ge(turn_free, j)
                for t in range(TT):
                    mm = pe.transpose(turn[:, t], cact[:, t * P:(t + 1) * P], ident)
                mm.then_inc(turn_ready, 1)

            def tokens(t):
                if t == 0:
                    pe.wait_ge(wt_in, 32)
                if t >= 2:
                    pe.wait_ge(tok_free, t - 1)
                for c, (a, b) in enumerate(((0, LAT), (LAT, LAT + ZAB))):
                    for k in range(KT):
                        mm = pe.matmul(tok[:, t % 2, c, 0:b - a], hT[:, k, t * P:(t + 1) * P], wt[:, k, a:b],
                                       start=(k == 0), stop=(k == KT - 1))
                mm.then_inc(tok_ready, 1)

            def mix(j):
                pe.wait_ge(delta_done, j + 1)
                pe.wait_ge(par_in, 16 * (CONV + 4))
                if j:
                    pe.wait_ge(mix_free, j)
                else:
                    pe.wait_ge(turn_free, 6)
                for half in range(2):
                    mm = pe.matmul(turn[:, :, :].rearrange("p t c -> p (t c)")[:, half * NW:(half + 1) * NW],
                                   pw[:, j], cact[:, half * NW:(half + 1) * NW], start=True, stop=True)
                mm.then_inc(mix_ready, 1)

            for j in range(NC):
                features(j)
                tokens(j)
                if j < 6:
                    turned(j)
                else:
                    mix(j - 6)

        @block.scalar
        def _(act):
            def tokens(t):
                act.wait_ge(tok_ready, t + 1)
                act.copy(lat[:, t], tok[:, t % 2, 0, 0:LAT])
                act.copy(zab[:, t], tok[:, t % 2, 1, 0:ZAB]).then_inc(tok_free, 1)

            act.wait_ge(par_in, 16 * (CONV + 4))
            for j in range(NC):
                act.wait_ge(feat_ready, j + 1)
                if j:
                    act.wait_ge(conv_done, j)
                else:
                    act.wait_ge(cin_ready, 1)
                act.copy(cin[:, PADW:], feat[:, :, :].rearrange("p h c -> p (h c)")).then_inc(feat_free, 1)
                tokens(j)
                if j < 6:
                    act.wait_ge(conv_done, j + 1)
                    if j:
                        act.wait_ge(turn_ready, j)
                    act.activation(cact[:], cout[:, PADW:], ACT.Silu).then_inc(act_done, 1)
                    act.wait_ge(turn_ready, j + 1)
                    act.copy(gqkv[:, :, j * P:(j + 1) * P], turn[:]).then_inc(turn_free, 1)
                else:
                    act.wait_ge(mix_ready, j - 5)
                    act.activation(yT[:, j, :], turn[:, :, :].rearrange("p t c -> p (t c)"), ACT.Copy,
                                   scale=psc[:, j - 6:j - 5]).then_inc(mix_free, 1)

        @block.vector
        def _(dve):
            st = Steps(dve, dchain)
            dve.memset(pw[:], 0.0).then_inc(zeroed, 1)
            st(dve.memset(cout[:, 0:PADW], 0.0))
            dve.memset(cin[:, 0:PADW], 0.0).then_inc(cin_ready, 1)
            dve.wait_ge(par_in, 16 * (CONV + 4))
            for j in range(NC):
                dve.wait_ge(feat_free, j + 1)
                if j < 6:
                    if j:
                        dve.wait_ge(act_done, j)
                    st(dve.tensor_scalar(cout[:, PADW:], cin[:, PADW:], cw[:, j, CONV - 1:CONV], None, ALU.mult))
                    for i in range(CONV - 1):
                        a = PADW - (CONV - 1) + i
                        ins = dve.scalar_tensor_tensor(out=cout[:, PADW:], in0=cin[:, a:a + SEQ], scalar=cw[:, j, i:i + 1],
                                                       in1=cout[:, PADW:], op0=ALU.mult, op1=ALU.add)
                        if i < CONV - 2:
                            st(ins)
                    ins.then_inc(conv_done, 1)
                else:
                    jj = j - 6
                    if jj == 0:
                        dve.wait_ge(act_done, 6)
                        dve.wait_ge(turn_ready, 6)
                    else:
                        dve.wait_ge(mix_ready, 1)
                    lo, hi = slice(0, 64), slice(64, 128)
                    X, Y = cin, cout
                    plan = [(slice(0, 128), 1), (hi, 2)] if jj == 0 else [(slice(0, 128), 1), (slice(0, 128), 2), (slice(0, 128), 4), (hi, 8)]
                    bufs = s_bufs
                    cur = cin
                    for n, (r, sh) in enumerate(plan):
                        nxt = bufs[n % 2]
                        st(dve.memset(nxt[:, 0:PADW], 0.0))
                        st(dve.tensor_tensor(nxt[r, PADW:], cur[r, PADW:], cur[r, PADW - sh:PADW - sh + SEQ], ALU.add))
                        last = nxt
                        prev, cur = cur, nxt
                    for r, src in ((lo, prev), (hi, cur)):
                        g = 2 * jj + (0 if r is lo else 1)
                        win = 2 << g
                        st(dve.tensor_tensor(cact[r, 0:PADW], src[r, PADW:2 * PADW], rc[r, jj], ALU.mult))
                        st(dve.tensor_scalar(cact[r, PADW:], src[r, 2 * PADW:], 1.0 / win, None, ALU.mult))
                    dve.tensor_tensor(cact[:], cact[:], cin[:, PADW:], ALU.subtract).then_inc(delta_done, 1)
                    dve.wait_ge(delta_done, jj + 1)
                    dve.sem_inc(conv_done, 1)


def stage_delta_gates(nc, I, zab, gqkv, M, g, beta, gc, egc, kdf, rs):
    with Stage(nc, "gates") as s:
        alog, dtb, ea = s.sb("alog", [P, GH]), s.sb("dtb", [P, GH]), s.sb("ea", [P, GH])
        xa, nab, e, l = (s.sb(n, [P, TT, GH]) for n in ("xa", "nab", "e", "l"))
        sq = s.sb("sq", [P, TT, 2 * GW])
        diff = s.sb("diff", [P, TT, GH])
        ps = s.ps("sums", [P, 2, TT * GH])
        par_in, x_ready, act_done, g_ready, sums = (s.sem(n) for n in ("par_in", "x_ready", "act_done", "g_ready", "sums"))
        chain, ss_ready, root, diff_ready, achain = (s.sem(n) for n in ("chain", "ss_ready", "root", "diff_ready", "achain"))
        block = s.ctx.enter_context(nc.Block())
        flat = lambda x: x[:, :, :].rearrange("p t h -> p (t h)")

        @block.sync
        def _(sp):
            sp.dma_start(alog[:], I["gdn_a_log"].partition_broadcast(P).rearrange("p a h -> p (a h)")).then_inc(par_in, 16)
            sp.dma_start(dtb[:], I["gdn_dt_bias"].partition_broadcast(P).rearrange("p a h -> p (a h)")).then_inc(par_in, 16)

        @block.scalar
        def _(act):
            a = Steps(act, achain)
            act.activation(sq[:], gqkv[:, :, 0:2 * GW], ACT.Square).then_inc(act_done, 1)
            a(act.activation(beta[:], zab[:, :, GW + GH:], ACT.Sigmoid))
            act.wait_ge(par_in, 32)
            a(act.activation(ea[:], alog[:], ACT.Exp))
            act.wait_ge(x_ready, 1)
            a(act.activation(e[:], nab[:], ACT.Exp))
            act.activation(l[:], e[:], ACT.Ln, bias=1.0).then_inc(act_done, 1)
            act.wait_ge(sums, 1)
            act.activation(flat(egc), ps[:, 0], ACT.Exp).then_inc(act_done, 1)
            act.wait_ge(diff_ready, 1)
            act.activation(flat(kdf), flat(diff), ACT.Exp).then_inc(act_done, 1)
            act.wait_ge(ss_ready, 1)
            act.activation(rs[:], rs[:], ACT.Sqrt).then_inc(root, 1)

        @block.vector
        def _(dve):
            st = Steps(dve, chain)
            dve.wait_ge(par_in, 32)
            st(dve.tensor_tensor(xa[:], zab[:, :, GW:GW + GH], dtb[:].unsqueeze(1).broadcast_to([P, TT, GH]), ALU.add))
            dve.scalar_tensor_tensor(out=nab[:], in0=xa[:], scalar=-1.0, in1=xa[:], op0=ALU.mult, op1=ALU.min).then_inc(x_ready, 1)
            dve.wait_ge(act_done, 2)
            st(dve.scalar_tensor_tensor(out=l[:], in0=xa[:], scalar=0.0, in1=l[:], op0=ALU.max, op1=ALU.add))
            dve.scalar_tensor_tensor(out=g[:], in0=l[:], scalar=-1.0, in1=ea[:].unsqueeze(1).broadcast_to([P, TT, GH]),
                                     op0=ALU.mult, op1=ALU.mult).then_inc(g_ready, 1)
            st(dve.tensor_reduce(rs[:], sq[:, :, :].rearrange("p t (h d) -> p (t h) d", d=GD), AX, ALU.add))
            dve.tensor_scalar(rs[:], rs[:], 1e-6, None, ALU.add).then_inc(ss_ready, 1)
            dve.wait_ge(sums, 1)
            dve.wait_ge(act_done, 3)
            st(dve.tensor_copy(flat(gc), ps[:, 0]))
            dve.tensor_tensor(flat(diff), ps[:, 1], flat(gc), ALU.subtract).then_inc(diff_ready, 1)
            dve.wait_ge(root, 1)
            st(dve.reciprocal(rs[:], rs[:]))
            q = rs[:].rearrange("p (t a) -> p t a", a=2 * GH)[:, :, 0:GH]
            st(dve.tensor_scalar(q, q, GD ** -0.5, None, ALU.mult))

        @block.tensor
        def _(pe):
            pe.wait_ge(g_ready, 1)
            pe.matmul(ps[:, 0], M["cum"], flat(g), start=True, stop=True, skip_group_check=True)
            pe.matmul(ps[:, 1], M["same"], flat(g), start=False, stop=True, skip_group_check=True).then_inc(sums, 1)


def stage_delta_rule(nc, gqkv, M, lv, g, beta, gc, egc, kdf, rs, o_tok):
    W = GH * P
    with Stage(nc, "delta") as s:
        qk, bv, bke, qd, kd = s.sb("qk", [P, 2 * GH, GD]), *(s.sb(n, [P, GH, GD]) for n in ("bv", "bke", "qd", "kd"))
        rsb = s.sb("rsb", [P, 2 * GH])
        bg = s.sb("bg", [P, GH])
        grep, brep = s.sb("g_rep", [P, GH, P]), s.sb("beta_rep", [P, GH, P])
        kT, qT, qdT, wT = (s.sb(n, [GD, GH, P]) for n in ("kT", "qT", "qdT", "wT"))
        dec, decI, decB, AT, qkT, X, XT, T1 = (s.sb(n, [P, GH, P]) for n in ("dec", "decI", "decB", "AT", "qkT", "X", "XT", "T1"))
        LT = s.sb("LT", [P, 6, GH, P])
        u, vn, o1 = s.sb("u", [P, GH, GD]), s.sb("vn", [P, GH, GD]), s.sb("o1", [P, GH, GD])
        gl = s.sb("gl", [GD, GH, 2])
        S = s.sb("S", [GD, GH, GD])
        bank = [s.ps(f"bank{n}", [P, GH, P]) for n in range(8)]
        names = ("staged kT_ps kT_sb rows_ps kk_ps dmin expd at_done t1_ps t1_sb t2_ps x_sb masks uw_ps uw_sb gl_sb "
                 "ws_ps vn_sb so_ps s_sb o_sb tile_done prep_done init init_p").split()
        m = {n: s.sem(n) for n in names}
        chain, pchain = s.sem("chain"), s.sem("pchain")
        N_DVE = 30
        block = s.ctx.enter_context(nc.Block())
        bc = lambda x, shape: x.unsqueeze(1).broadcast_to(shape)
        full = [P, GH, P]

        @block.gpsimd
        def _(pool):
            pool.memset(S[:], 0.0).then_inc(m["init_p"], 1)
            with pool.Fori(0, TT) as i:
                pool.wait_ge(m["tile_done"], i)
                gi = g[:, bass.ds(i, 1), :].rearrange("p a h -> p (a h)").unsqueeze(2).broadcast_to(full)
                bi = beta[:, bass.ds(i, 1), :].rearrange("p a h -> p (a h)").unsqueeze(2).broadcast_to(full)
                pool.tensor_copy(grep[:], gi)
                pool.tensor_copy(brep[:], bi).then_inc(m["prep_done"], 1)
                pool.wait_ge(m["at_done"], i + 1)
                for n in range(6):
                    pool.tensor_tensor(LT[:, n], AT[:], bc(lv[n], full), ALU.mult).then_inc(m["masks"], 1)

        @block.tensor
        def _(pe):
            pe.wait_ge(m["init_p"], 1)
            with pe.Fori(0, TT) as i:
                pe.wait_ge(m["staged"], i + 1)
                for h in range(GH):
                    pe.matmul(bank[0][0:GD, h], qk[:, GH + h], M["ident"], start=True, stop=True, skip_group_check=True)
                    pe.matmul(bank[1][0:GD, h], qk[:, h], M["ident"], start=True, stop=True, skip_group_check=True)
                    mm = pe.matmul(bank[2][0:GD, h], qd[:, h], M["ident"], start=True, stop=True, skip_group_check=True)
                mm.then_inc(m["kT_ps"], 1)
                pe.wait_ge(m["prep_done"], i + 1)
                for h in range(GH):
                    pe.matmul(bank[3][:, h], grep[:, h], M["cum"], start=True, stop=True, skip_group_check=True)
                    mm = pe.matmul(bank[4][:, h], brep[:, h], M["ident"], start=True, stop=True, skip_group_check=True)
                mm.then_inc(m["rows_ps"], 1)
                pe.wait_ge(m["kT_sb"], i + 1)
                for h in range(GH):
                    pe.matmul(bank[5][:, h], kT[:, h], kT[:, h], start=True, stop=True, skip_group_check=True)
                    mm = pe.matmul(bank[6][:, h], kT[:, h], qT[:, h], start=True, stop=True, skip_group_check=True)
                mm.then_inc(m["kk_ps"], 1)
                for n in range(6):
                    pe.wait_ge(m["masks"], i * 6 + n + 1)
                    if n:
                        pe.wait_ge(m["x_sb"], i * 6 + n)
                    for h in range(GH):
                        mm = pe.matmul(bank[0][:, h], LT[:, n, h], X[:, h] if n else M["ident"], start=True, stop=True, skip_group_check=True)
                    mm.then_inc(m["t1_ps"], 1)
                    if n:
                        pe.wait_ge(m["t1_sb"], i * 5 + n)
                        for h in range(GH):
                            pe.matmul(bank[1][:, h], XT[:, h], T1[:, h], start=True, stop=True, skip_group_check=True)
                            mm = pe.matmul(bank[2][:, h], T1[:, h], XT[:, h], start=True, stop=True, skip_group_check=True)
                        mm.then_inc(m["t2_ps"], 1)
                pe.wait_ge(m["x_sb"], i * 6 + 6)
                for h in range(GH):
                    pe.matmul(bank[3][:, h, 0:GD], XT[:, h], bv[:, h], start=True, stop=True, skip_group_check=True)
                    mm = pe.matmul(bank[4][0:GD, h], bke[:, h], XT[:, h], start=True, stop=True, skip_group_check=True)
                mm.then_inc(m["uw_ps"], 1)
                pe.wait_ge(m["uw_sb"], i + 1)
                for c in range(2):
                    r = slice(64 * c, 64 * c + 64)
                    pe.wait_ge(m["s_sb"], i * 2 + c)
                    for h in range(GH):
                        pe.matmul(bank[5][:, h, 0:GD], wT[:, h], S[:, h], start=True, stop=True, skip_group_check=True)
                        mm = pe.matmul(bank[6][:, h, 0:GD], qdT[:, h], S[:, h], start=True, stop=True, skip_group_check=True)
                    mm.then_inc(m["ws_ps"], 1)
                    pe.wait_ge(m["vn_sb"], i * 2 + c + 1)
                    for h in range(GH):
                        pe.matmul(bank[0][:, h, 0:GD], qkT[r, h], vn[r, h], start=True, stop=True, skip_group_check=True)
                    for h in range(GH):
                        mm = pe.matmul(bank[7][0:GD, h, 0:GD], kd[r, h], vn[r, h], start=True, stop=True, skip_group_check=True)
                    mm.then_inc(m["so_ps"], 1)

        @block.scalar
        def _(act):
            with act.Fori(0, TT) as i:
                act.wait_ge(m["kT_ps"], i + 1)
                act.copy(kT[:], bank[0][0:GD])
                act.copy(qT[:], bank[1][0:GD])
                act.copy(qdT[:], bank[2][0:GD]).then_inc(m["kT_sb"], 1)
                act.wait_ge(m["rows_ps"], i + 1)
                act.activation(gl[:], bank[3][0:GD, :, :].rearrange("p h (c j) -> p h c j", c=2)[:, :, :, 63], ACT.Exp).then_inc(m["gl_sb"], 1)
                act.wait_ge(m["dmin"], i + 1)
                act.activation(dec[:], dec[:], ACT.Exp).then_inc(m["expd"], 1)
                for n in range(1, 6):
                    act.wait_ge(m["t1_ps"], i * 6 + n + 1)
                    act.copy(T1[:], bank[0][:]).then_inc(m["t1_sb"], 1)
                act.wait_ge(m["uw_ps"], i + 1)
                act.copy(wT[:], bank[4][0:GD])
                act.copy(u[:], bank[3][:, :, 0:GD]).then_inc(m["uw_sb"], 1)

        @block.vector
        def _(dve):
            with dve.Fori(0, TT) as i:
                st = Steps(dve, chain, at=i * N_DVE)
                row = lambda x: x[:, bass.ds(i, 1), :].rearrange("p a h -> p (a h)")
                wide = lambda x, n=GH: x.unsqueeze(2).broadcast_to([P, n, GD])
                src = gqkv[:, bass.ds(i, 1), :].rearrange("p a (h d) -> p (a h) d", d=GD)
                rsi = rs[:, bass.ds(i * (2 * GH), 2 * GH)]
                st(dve.tensor_tensor(qk[:], src[:, 0:2 * GH], wide(rsi, 2 * GH), ALU.mult))
                st(dve.tensor_tensor(bg[:], row(beta), row(egc), ALU.mult))
                dve.tensor_tensor(bv[:], src[:, 2 * GH:], wide(row(beta)), ALU.mult)
                dve.tensor_tensor(bke[:], qk[:, GH:], wide(bg[:]), ALU.mult)
                dve.tensor_tensor(kd[:], qk[:, GH:], wide(row(kdf)), ALU.mult)
                dve.tensor_tensor(qd[:], qk[:, 0:GH], wide(row(egc)), ALU.mult).then_inc(m["staged"], 1)
                dve.wait_ge(m["rows_ps"], i + 1)
                dve.wait_ge(m["gl_sb"], i + 1)
                for h in range(GH):
                    ins = dve.tensor_scalar(dec[:, h], bank[3][:, h], gc[:, bass.ds(i, 1), h], 0.0, ALU.subtract, ALU.min)
                ins.then_inc(m["dmin"], 1)
                dve.wait_ge(m["expd"], i + 1)
                dve.tensor_tensor(decI[:], dec[:], bc(M["cum"], full), ALU.mult)
                st(dve.tensor_tensor(decB[:], dec[:], bc(M["strict"], full), ALU.mult))
                st(dve.tensor_tensor(decB[:], decB[:], bank[4][:], ALU.mult))
                dve.wait_ge(m["kk_ps"], i + 1)
                dve.tensor_tensor(AT[:], decB[:], bank[5][:], ALU.mult).then_inc(m["at_done"], 1)
                dve.tensor_tensor(qkT[:], decI[:], bank[6][:], ALU.mult)
                for n in range(6):
                    dve.wait_ge(m["masks"], i * 6 + n + 1)
                    if n == 0:
                        dve.wait_ge(m["t1_ps"], i * 6 + 1)
                        dve.tensor_tensor(XT[:], bc(M["ident"], full), LT[:, 0], ALU.subtract)
                        dve.tensor_tensor(X[:], bc(M["ident"], full), bank[0][:], ALU.subtract).then_inc(m["x_sb"], 1)
                    else:
                        dve.wait_ge(m["t2_ps"], i * 5 + n)
                        dve.tensor_tensor(X[:], X[:], bank[1][:], ALU.subtract)
                        dve.tensor_tensor(XT[:], XT[:], bank[2][:], ALU.subtract).then_inc(m["x_sb"], 1)
                for c in range(2):
                    r = slice(64 * c, 64 * c + 64)
                    dve.wait_ge(m["ws_ps"], i * 2 + c + 1)
                    dve.wait_ge(m["uw_sb"], i + 1)
                    dve.tensor_tensor(vn[r], u[r], bank[5][r, :, 0:GD], ALU.subtract).then_inc(m["vn_sb"], 1)
                    dve.tensor_copy(o1[r], bank[6][r, :, 0:GD])
                    st(dve.tensor_tensor(S[:], S[:], gl[:, :, c].unsqueeze(2).broadcast_to([GD, GH, GD]), ALU.mult))
                    dve.wait_ge(m["so_ps"], i * 2 + c + 1)
                    dve.tensor_tensor(S[:], S[:], bank[7][0:GD, :, 0:GD], ALU.add).then_inc(m["s_sb"], 1)
                    ot = o_tok[r, bass.ds(i, 1), :].rearrange("p a (h d) -> p (a h) d", d=GD)
                    ins = dve.tensor_tensor(ot, o1[r], bank[0][r, :, 0:GD], ALU.add)
                ins.then_inc(m["tile_done"], 1)
                while st.n < N_DVE:
                    dve.sem_inc(chain, 1)
                    st.n += 1
                dve.wait_ge(m["tile_done"], i + 1)


def stage_delta_out(nc, I, o_tok, zab, yg):
    with Stage(nc, "dout") as s:
        sq, sz = s.sb("sq", [P, TT, GW]), s.sb("sz", [P, TT, GW])
        ss = s.sb("ss", [P, TT * GH])
        gain = s.sb("gain", [P, GD])
        gin, sq_ready, ss_ready, root, chain, silu = (s.sem(n) for n in ("gin", "sq_ready", "ss_ready", "root", "chain", "silu"))
        block = s.ctx.enter_context(nc.Block())
        hd = lambda x: x[:, :, :].rearrange("p t (h d) -> p (t h) d", d=GD)

        @block.sync
        def _(sp):
            sp.dma_start(gain[:], I["gdn_out_norm"].partition_broadcast(P).rearrange("p a h -> p (a h)")).then_inc(gin, 16)

        @block.scalar
        def _(act):
            act.activation(sq[:], o_tok[:], ACT.Square).then_inc(sq_ready, 1)
            act.activation(sz[:], zab[:, :, 0:GW], ACT.Silu).then_inc(silu, 1)
            act.wait_ge(ss_ready, 1)
            act.activation(ss[:], ss[:], ACT.Sqrt).then_inc(root, 1)

        @block.vector
        def _(dve):
            st = Steps(dve, chain)
            dve.wait_ge(sq_ready, 1)
            st(dve.tensor_reduce(ss[:], hd(sq), AX, ALU.add))
            dve.tensor_scalar(ss[:], ss[:], 1.0 / GD, 1e-6, ALU.mult, ALU.add).then_inc(ss_ready, 1)
            dve.wait_ge(root, 1)
            st(dve.reciprocal(ss[:], ss[:]))
            st(dve.tensor_tensor(hd(yg), hd(o_tok), ss[:].unsqueeze(2).broadcast_to([P, TT * GH, GD]), ALU.mult))
            dve.wait_ge(gin, 16)
            st(dve.tensor_tensor(hd(yg), hd(yg), gain[:].unsqueeze(1).broadcast_to([P, TT * GH, GD]), ALU.mult))
            dve.wait_ge(silu, 1)
            st(dve.tensor_tensor(yg[:], yg[:], sz[:], ALU.mult))


HEADS, NOPE, VD = 8, 64, 64
QKD = NOPE + ROPE
HR = ROPE // 2
MASKED = -1.0e30


def stage_latent_norms(nc, lat, rope, kr):
    with Stage(nc, "latent") as s:
        sq = s.sb("sq", [P, TT, Q_RANK + KV_RANK])
        ss = s.sb("ss", [P, 2, TT])
        t1, t2 = s.sb("t1", [P, TT, HR]), s.sb("t2", [P, TT, HR])
        sq_ready, ss_ready, root, chain = (s.sem(n) for n in ("sq_ready", "ss_ready", "root", "chain"))
        block = s.ctx.enter_context(nc.Block())

        @block.scalar
        def _(act):
            act.activation(sq[:], lat[:, :, 0:Q_RANK + KV_RANK], ACT.Square).then_inc(sq_ready, 1)
            act.wait_ge(ss_ready, 1)
            act.activation(ss[:], ss[:], ACT.Sqrt).then_inc(root, 1)

        @block.vector
        def _(dve):
            st = Steps(dve, chain)
            x1, x2 = lat[:, :, LAT - ROPE:LAT - HR], lat[:, :, LAT - HR:LAT]
            cos, sin = rope[:, :, 0], rope[:, :, 1]
            st(dve.tensor_tensor(t1[:], x1, cos, ALU.mult))
            st(dve.tensor_tensor(t2[:], x2, sin, ALU.mult))
            st(dve.tensor_tensor(kr[:, :, 0:HR], t1[:], t2[:], ALU.subtract))
            st(dve.tensor_tensor(t1[:], x2, cos, ALU.mult))
            st(dve.tensor_tensor(t2[:], x1, sin, ALU.mult))
            st(dve.tensor_tensor(kr[:, :, HR:], t1[:], t2[:], ALU.add))
            dve.wait_ge(sq_ready, 1)
            st(dve.tensor_reduce(ss[:, 0], sq[:, :, 0:Q_RANK], AX, ALU.add))
            st(dve.tensor_reduce(ss[:, 1], sq[:, :, Q_RANK:], AX, ALU.add))
            st(dve.tensor_scalar(ss[:, 0], ss[:, 0], 1.0 / Q_RANK, 1e-6, ALU.mult, ALU.add))
            dve.tensor_scalar(ss[:, 1], ss[:, 1], 1.0 / KV_RANK, 1e-6, ALU.mult, ALU.add).then_inc(ss_ready, 1)
            dve.wait_ge(root, 1)
            st(dve.reciprocal(ss[:], ss[:]))
            for a, b, n in ((0, Q_RANK, 0), (Q_RANK, Q_RANK + KV_RANK, 1)):
                st(dve.tensor_tensor(lat[:, :, a:b], lat[:, :, a:b], ss[:, n].unsqueeze(2).broadcast_to([P, TT, b - a]), ALU.mult))


def stage_latent_attention(nc, I, cT, rope, kr, ident, y_tok, y_dram, filler):
    scale = QKD ** -0.5
    with Stage(nc, "mla") as s:
        wq = s.sb("wq", [P, 2, HEADS * QKD])
        wkv = s.sb("wkv", [P, HEADS * (NOPE + VD)])
        qs, ks, vs = s.sb("q_tok", [P, TT, QKD]), s.sb("k_tok", [P, TT, QKD]), s.sb("v_tok", [P, TT, VD])
        r1, r2 = s.sb("r1", [P, TT, HR]), s.sb("r2", [P, TT, HR])
        qT, kT = s.sb("qT", [QKD, SEQ]), s.sb("kT", [QKD, SEQ])
        pr, prT = s.sb("probs", [P, 2, SEQ]), s.sb("probsT", [P, 2, SEQ])
        mx, nm, rsum, rinv = (s.sb(n, [P, 2, 1]) for n in ("mx", "nm", "rsum", "rinv"))
        A = [s.ps(f"A{n}", [P, 2 * NW]) for n in range(4)]
        w_in, qkv_ps, kr_set, q_rot, qk_sb, turn_ps, turn_sb = (s.sem(n) for n in ("w_in", "qkv_ps", "kr_set", "q_rot", "qk_sb", "turn_ps", "turn_sb"))
        s_ps, nm_sb, p_sb, pT_ps, pT_a, pT_d, o_ps, y_sb, chain, achain = (s.sem(n) for n in (
            "s_ps", "nm_sb", "p_sb", "pT_ps", "pT_a", "pT_d", "o_ps", "y_sb", "chain", "achain"))
        filled = s.sem("filled")
        tiles = lambda x, w: x[:, :].rearrange("p (t c) -> p t c", t=TT)[:, :, 0:w]
        block = s.ctx.enter_context(nc.Block())

        @block.sync
        def _(sp):
            sp.dma_start(wq[:], I["mla_w_uq"][0].rearrange("(k p) n -> p k n", p=P)).then_inc(w_in, 16)
            sp.dma_start(wkv[:], I["mla_w_ukv"][0]).then_inc(w_in, 16)
            rows = y_dram.rearrange("(b p) d -> p b d", p=P)
            for b in range(0, BLOCKS, 8):
                sp.dma_start(rows[:, b:b + 8], filler.unsqueeze(1).broadcast_to([P, 8, D])).then_inc(filled, 16)
            sp.wait_ge(filled, 16 * (BLOCKS // 8))

        @block.gpsimd
        def _(pool):
            pool.tensor_copy(ks[:, :, NOPE:], kr[:]).then_inc(kr_set, 1)

        @block.tensor
        def _(pe):
            pe.wait_ge(w_in, 32)
            pe.wait_ge(kr_set, 1)
            with pe.Fori(0, HEADS) as h:
                pe.wait_ge(y_sb, h * TT)
                for t in range(TT):
                    for k in range(2):
                        pe.matmul(tiles(A[0], P)[:, t, 0:QKD], cT[:, k, t * P:(t + 1) * P],
                                  wq[:, k, bass.ds(h * QKD, QKD)], start=(k == 0), stop=(k == 1), skip_group_check=True)
                    mm = pe.matmul(tiles(A[1], P)[:, t], cT[:, 2, t * P:(t + 1) * P], wkv[:, bass.ds(h * P, P)],
                                   start=True, stop=True, skip_group_check=True)
                mm.then_inc(qkv_ps, 1)
                pe.wait_ge(qk_sb, h + 1)
                pe.wait_ge(q_rot, h + 1)
                for t in range(TT):
                    pe.transpose(A[2][0:QKD, t * P:(t + 1) * P], qs[:, t], ident)
                    mm = pe.transpose(A[3][0:QKD, t * P:(t + 1) * P], ks[:, t], ident)
                mm.then_inc(turn_ps, 1)
                pe.wait_ge(turn_sb, h * 2 + 2)

                def scores(b):
                    if b >= 2:
                        pe.wait_ge(p_sb, h * TT + b - 1)
                    n = (b + 1) * P
                    for a in range(0, n, NW):
                        mm = pe.matmul(A[b % 2][:, a:min(a + NW, n)], qT[:, b * P:n], kT[:, a:min(a + NW, n)], start=True, stop=True)
                    mm.then_inc(s_ps, 1)

                scores(0)
                for b in range(TT):
                    if b + 1 < TT:
                        scores(b + 1)
                    pe.wait_ge(p_sb, h * TT + b + 1)
                    if b:
                        pe.wait_ge(pT_a, h * TT + b)
                        pe.wait_ge(pT_d, h * TT + b)
                    for n in range(b + 1):
                        mm = pe.transpose(A[2][:, n * P:(n + 1) * P], pr[:, b % 2, n * P:(n + 1) * P], ident)
                    mm.then_inc(pT_ps, 1)
                    pe.wait_ge(pT_a, h * TT + b + 1)
                    pe.wait_ge(pT_d, h * TT + b + 1)
                    if b >= 2:
                        pe.wait_ge(y_sb, h * TT + b - 1)
                    for n in range(b + 1):
                        mm = pe.matmul(A[3][:, (b % 2) * NW:(b % 2) * NW + VD], prT[:, b % 2, n * P:(n + 1) * P], vs[:, n],
                                       start=(n == 0), stop=(n == b))
                    mm.then_inc(o_ps, 1)

        @block.scalar
        def _(act):
            with act.Fori(0, HEADS) as h:
                act.wait_ge(qkv_ps, h + 1)
                act.copy(ks[:, :, 0:NOPE], tiles(A[1], NOPE))
                act.copy(vs[:], A[1][:, :].rearrange("p (t c) -> p t c", t=TT)[:, :, NOPE:])
                act.copy(qs[:, :, 0:NOPE], tiles(A[0], NOPE)).then_inc(qk_sb, 1)
                act.wait_ge(turn_ps, h + 1)
                act.copy(qT[:], A[2][0:QKD]).then_inc(turn_sb, 1)
                for b in range(TT):
                    n = (b + 1) * P
                    act.wait_ge(nm_sb, h * TT + b + 1)
                    act.activation(pr[:, b % 2, 0:n], A[b % 2][:, 0:n], ACT.Exp, bias=nm[:, b % 2], scale=scale,
                                   accum_out=rsum[:, b % 2]).then_inc(p_sb, 1)
                    act.wait_ge(pT_ps, h * TT + b + 1)
                    act.copy(prT[:, b % 2, 0:min(n, NW)], A[2][:, 0:min(n, NW)]).then_inc(pT_a, 1)

        @block.vector
        def _(dve):
            N = 5 + 3 * TT
            with dve.Fori(0, HEADS) as h:
                st = Steps(dve, chain, at=h * N)
                dve.wait_ge(qkv_ps, h + 1)
                dve.wait_ge(qk_sb, h + 1)
                x1, x2 = tiles(A[0], P)[:, :, NOPE:NOPE + HR], tiles(A[0], P)[:, :, NOPE + HR:QKD]
                cos, sin = rope[:, :, 0], rope[:, :, 1]
                st(dve.tensor_tensor(r1[:], x1, cos, ALU.mult))
                st(dve.tensor_tensor(r2[:], x2, sin, ALU.mult))
                st(dve.tensor_tensor(qs[:, :, NOPE:NOPE + HR], r1[:], r2[:], ALU.subtract))
                st(dve.tensor_tensor(r1[:], x2, cos, ALU.mult))
                st(dve.tensor_tensor(r2[:], x1, sin, ALU.mult))
                dve.tensor_tensor(qs[:, :, NOPE + HR:], r1[:], r2[:], ALU.add).then_inc(q_rot, 1)
                dve.wait_ge(turn_ps, h + 1)
                dve.tensor_copy(kT[:], A[3][0:QKD]).then_inc(turn_sb, 1)

                def largest(b):
                    n = (b + 1) * P
                    dve.wait_ge(s_ps, h * TT + b + 1)
                    st(dve.memset(A[b % 2][0:64, n - 64:n], MASKED))
                    st(dve.reduce_max(mx[:, b % 2], A[b % 2][:, 0:n], AX))
                    dve.tensor_scalar(nm[:, b % 2], mx[:, b % 2], -scale, None, ALU.mult).then_inc(nm_sb, 1)

                largest(0)
                for b in range(TT):
                    if b + 1 < TT:
                        if b:
                            dve.wait_ge(p_sb, h * TT + b)
                        largest(b + 1)
                    dve.wait_ge(p_sb, h * TT + b + 1)
                    st(dve.reciprocal(rinv[:, b % 2], rsum[:, b % 2]))
                    dve.wait_ge(pT_ps, h * TT + b + 1)
                    n = (b + 1) * P
                    if n > NW:
                        dve.tensor_copy(prT[:, b % 2, NW:n], A[2][:, NW:n]).then_inc(pT_d, 1)
                    else:
                        dve.sem_inc(pT_d, 1)
                    dve.wait_ge(o_ps, h * TT + b + 1)
                    dve.tensor_scalar(y_tok[:, b, bass.ds(h * VD, VD)], A[3][:, (b % 2) * NW:(b % 2) * NW + VD],
                                      rinv[:, b % 2], None, ALU.mult).then_inc(y_sb, 1)
                assert st.n == N, st.n


ALPHA = 2.0 ** 0.25
LN_EPS = 1e-5


def stage_mix_out(nc, I, yT, gate, v, nmean, ss):
    with Stage(nc, "mixout") as s:
        w = s.sb("w", [P, KT, D])
        tmp, junk = s.sb("tmp", [P, 2, D]), s.sb("junk", [P, D])
        sm = s.sb("sum", [P, TT])
        acc = s.ps("acc", [P, 2, D])
        w_in, x_in, acc_ready, acc_free, v_ready, sum_ready, mean_ready, chain, sq_done = (s.sem(n) for n in (
            "w_in", "x_in", "acc_ready", "acc_free", "v_ready", "sum_ready", "mean_ready", "chain", "sq_done"))
        block = s.ctx.enter_context(nc.Block())

        @block.sync
        def _(sp):
            sp.dma_start(w[:], I["w_out"][0].rearrange("(k p) n -> p k n", p=P)).then_inc(w_in, 16)
            sp.dma_start(v[:], I["x"][0].rearrange("(t p) d -> p t d", p=P)).then_inc(x_in, 16)

        @block.tensor
        def _(pe):
            pe.wait_ge(w_in, 16)
            for t in range(TT):
                if t >= 2:
                    pe.wait_ge(acc_free, t - 1)
                for c in range(2):
                    for k in range(KT):
                        mm = pe.matmul(acc[:, t % 2, c * NW:(c + 1) * NW], yT[:, k, t * P:(t + 1) * P],
                                       w[:, k, c * NW:(c + 1) * NW], start=(k == 0), stop=(k == KT - 1))
                mm.then_inc(acc_ready, 1)

        @block.vector
        def _(dve):
            dve.wait_ge(x_in, 16)
            for t in range(TT):
                dve.wait_ge(acc_ready, t + 1)
                dve.scalar_tensor_tensor(out=tmp[:, t % 2], in0=gate, scalar=1.0, in1=acc[:, t % 2],
                                         op0=ALU.add, op1=ALU.mult).then_inc(acc_free, 1)
                dve.wait_ge(acc_free, t + 1)
                dve.scalar_tensor_tensor(out=v[:, t], in0=v[:, t], scalar=ALPHA, in1=tmp[:, t % 2],
                                         op0=ALU.mult, op1=ALU.add).then_inc(v_ready, 1)
                if t:
                    dve.wait_ge(sum_ready, t)
                    dve.tensor_scalar(nmean[:, t - 1:t], sm[:, t - 1:t], -1.0 / D, None, ALU.mult).then_inc(mean_ready, 1)
            dve.wait_ge(sum_ready, TT)
            dve.tensor_scalar(nmean[:, TT - 1:], sm[:, TT - 1:], -1.0 / D, None, ALU.mult).then_inc(mean_ready, 1)

        @block.scalar
        def _(act):
            moments(act, v, v_ready, sm, sum_ready, nmean, mean_ready, junk, chain, ss)


def moments(act, v, v_ready, sm, sum_ready, nmean, mean_ready, junk, chain, ss):
    st = Steps(act, chain)
    for t in range(TT + 1):
        if t < TT:
            act.wait_ge(v_ready, t + 1)
            if t:
                st(act.activation(junk[:], v[:, t], ACT.Copy, accum_out=sm[:, t:t + 1]))
            else:
                act.activation(junk[:], v[:, t], ACT.Copy, accum_out=sm[:, t:t + 1]).then_inc(chain, 1)
                st.n += 1
                act.wait_ge(chain, 1)
            act.sem_inc(sum_ready, 1)
        if t:
            act.wait_ge(mean_ready, t)
            st(act.activation(junk[:], v[:, t - 1], ACT.Square, bias=nmean[:, t - 1:t], accum_out=ss[:, t - 1:t]))


def stage_layer_norm(nc, name, gain, bias, v, nmean, ss, factor=None, shift=None, h=None, stores=()):
    with Stage(nc, name) as s:
        g, b = s.sb("g", [P, D]), s.sb("b", [P, D])
        rstd = s.sb("rstd", [P, TT])
        par, var_ready, root, chain, norm_done, v_done, hm, h_done, stored = (s.sem(n) for n in (
            "par", "var_ready", "root", "chain", "norm_done", "v_done", "hm", "h_done", "stored"))
        block = s.ctx.enter_context(nc.Block())

        @block.sync
        def _(sp):
            sp.dma_start(g[:], gain.partition_broadcast(P).rearrange("p a d -> p (a d)")).then_inc(par, 16)
            sp.dma_start(b[:], bias.partition_broadcast(P).rearrange("p a d -> p (a d)")).then_inc(par, 16)
            for t in range(TT):
                for dram, src in stores:
                    sp.wait_ge(h_done if h is not None and src is h else v_done, t + 1)
                    sp.dma_start(dram[t], src[:, t]).then_inc(stored, 16)
            if stores:
                sp.wait_ge(stored, 16 * TT * len(stores))

        @block.scalar
        def _(act):
            act.wait_ge(var_ready, 1)
            act.activation(rstd[:], rstd[:], ACT.Sqrt).then_inc(root, 1)

        @block.vector
        def _(dve):
            st = Steps(dve, chain)
            dve.tensor_scalar(rstd[:], ss[:], 1.0 / D, LN_EPS, ALU.mult, ALU.add).then_inc(var_ready, 1)
            dve.wait_ge(root, 1)
            st(dve.reciprocal(rstd[:], rstd[:]))
            dve.wait_ge(par, 32)
            for t in range(TT):
                dve.tensor_scalar(v[:, t], v[:, t], nmean[:, t:t + 1], rstd[:, t:t + 1], ALU.add, ALU.mult).then_inc(norm_done, 1)
                dve.wait_ge(norm_done, t + 1)
                st(dve.tensor_tensor(v[:, t], v[:, t], g[:], ALU.mult))
                dve.tensor_tensor(v[:, t], v[:, t], b[:], ALU.add).then_inc(v_done, 1)
                if h is not None:
                    dve.wait_ge(v_done, t + 1)
                    dve.scalar_tensor_tensor(out=h[:, t], in0=factor, scalar=1.0, in1=v[:, t], op0=ALU.add,
                                             op1=ALU.mult).then_inc(hm, 1)

        @block.gpsimd
        def _(pool):
            if h is not None:
                for t in range(TT):
                    pool.wait_ge(hm, t + 1)
                    pool.tensor_tensor(h[:, t], h[:, t], shift, ALU.add).then_inc(h_done, 1)


NG, EG = 4, 8
NE = NG * EG
TOPK = 2
FF = 256
BLOCKS = (SEQ * TOPK + NE * (P - 1) + P - 1) // P
BIG = 1.0e30


def stage_route(nc, I, K, M, h2T, wts, dest, be, idx_dram):
    NR = NG + NE
    with Stage(nc, "route") as s:
        w, bias = s.sb("w", [P, KT, NR]), s.sb("bias", [P, NR])
        iota = s.sb("iota", [P, 64])
        bstart = s.sb("bstart", [1, BLOCKS])
        tok = s.sb("tok", [P, TT], I32)
        zero = s.sb("zero", [P, BLOCKS], I32)
        lg = s.sb("lg", [P, TT, NR])
        gl = s.sb("gl", [P, TT, 8])
        gmax, gidx, gf = s.sb("gmax", [P, TT, 8]), s.sb("gidx", [P, TT, 8], U32), s.sb("gf", [P, TT])
        gm, gmb = s.sb("gm", [P, TT, NG]), s.sb("gmb", [P, TT, NG])
        el = s.sb("el", [P, TT, NE])
        emax, eidx, ef = s.sb("emax", [P, TT, 8]), s.sb("eidx", [P, TT, 8], U32), s.sb("ef", [P, TT, 2])
        ge, gs = s.sb("ge", [P, TT, NG]), s.sb("gs", [P, TT])
        d, de, den = s.sb("d", [P, TT]), s.sb("de", [P, TT]), s.sb("den", [P, TT])
        oh = s.sb("oh", [P, 2, TT, NE])
        both = s.sb("both", [P, TT, NE])
        cf, ci, padded, pend, pstart, one = (s.sb("cf", [P, NE]), s.sb("ci", [P, NE], I32), s.sb("padded", [P, NE]),
                                             s.sb("pend", [P, NE]), s.sb("pstart", [P, NE]), s.sb("one", [P, NE]))
        place, pick = s.sb("place", [P, TT, NE]), s.sb("pick", [P, TT, NE])
        df = s.sb("df", [P, 2, TT])
        bl, bef = s.sb("bl", [1, BLOCKS, NE]), s.sb("bef", [1, BLOCKS + 1])
        ps, ranks = s.ps("logits", [P, TT, 64]), s.ps("ranks", [P, 16, NE])
        par, lg_ps, chain, e_ready, e_done, both_done, rk_ps, placed, zeroed, zstore, scattered = (s.sem(n) for n in (
            "par", "lg_ps", "chain", "e_ready", "e_done", "both_done", "rk_ps", "placed", "zeroed", "zstore", "scattered"))
        block = s.ctx.enter_context(nc.Block())

        @block.sync
        def _(sp):
            kv = lambda a: a.rearrange("(p k) n -> p k n", p=P)
            sp.dma_start(w[:, :, 0:NG], kv(I["router_w_group"][0])).then_inc(par, 16)
            sp.dma_start(w[:, :, NG:], kv(I["router_w_expert"][0])).then_inc(par, 16)
            sp.dma_start(bias[:, 0:NG], I["router_b_group"].partition_broadcast(P).rearrange("p a d -> p (a d)")).then_inc(par, 16)
            sp.dma_start(bias[:, NG:], I["router_b_expert"].partition_broadcast(P).rearrange("p a d -> p (a d)")).then_inc(par, 16)
            sp.dma_start(iota[:], K["iota"]).then_inc(par, 16)
            sp.dma_start(bstart[:], K["bstart"]).then_inc(par, 16)
            sp.dma_start(tok[:], K["tokens"]).then_inc(par, 16)
            sp.wait_ge(zeroed, 1)
            sp.dma_start(idx_dram.rearrange("(p b) a -> p (b a)", p=P), zero[:]).then_inc(zstore, 16)

        @block.tensor
        def _(pe):
            pe.wait_ge(par, 16 * 7)
            for t in range(TT):
                for k in range(KT):
                    mm = pe.matmul(ps[:, t, 0:NR], h2T[:, k, t * P:(t + 1) * P], w[:, k], start=(k == 0), stop=(k == KT - 1),
                                   skip_group_check=True)
            mm.then_inc(lg_ps, 1)
            pe.wait_ge(both_done, 1)
            for t in range(TT + 1):
                for q in range(t):
                    mm = pe.matmul(ranks[:, t], M["ones"], both[:, q], start=(q == 0), stop=(q == t - 1 and t == TT), skip_group_check=True)
                if t < TT:
                    mm = pe.matmul(ranks[:, t], M["before"], both[:, t], start=(t == 0), stop=True, skip_group_check=True)
            mm.then_inc(rk_ps, 1)

        @block.scalar
        def _(act):
            act.wait_ge(e_ready, 1)
            act.activation(ge[:], ge[:], ACT.Exp)
            act.activation(de[:], d[:], ACT.Exp).then_inc(e_done, 1)

        @block.gpsimd
        def _(pool):
            pool.memset(zero[:], 0).then_inc(zeroed, 1)
            pool.wait_ge(zstore, 16)
            pool.wait_ge(placed, 1)
            for c in range(2):
                for t in range(TT):
                    pool.indirect_dma_start(out=idx_dram, out_offset=bass.IndirectOffsetOnAxis(ap=dest[:, c * TT + t:c * TT + t + 1], axis=0),
                                            in_=tok[:, t:t + 1], in_offset=None).then_inc(scattered, 16)
            pool.wait_ge(scattered, 16 * 2 * TT)

        @block.vector
        def _(dve):
            st = Steps(dve, chain)
            wide = lambda x, n: x.unsqueeze(2).broadcast_to([P, TT, n])
            dve.wait_ge(par, 16 * 7)
            st(dve.memset(gl[:], -BIG))
            st(dve.memset(one[:], 1.0))
            dve.wait_ge(lg_ps, 1)
            st(dve.tensor_tensor(lg[:], ps[:, :, 0:NR], bias[:].unsqueeze(1).broadcast_to([P, TT, NR]), ALU.add))
            st(dve.tensor_copy(gl[:, :, 0:NG], lg[:, :, 0:NG]))
            for t in range(TT):
                st(dve.max(gmax[:, t], gl[:, t]))
                st(dve.max_index(gidx[:, t], gmax[:, t], gl[:, t]))
            st(dve.tensor_copy(gf[:], gidx[:, :, 0]))
            st(dve.tensor_tensor(gm[:], iota[:, 0:NG].unsqueeze(1).broadcast_to([P, TT, NG]), wide(gf[:], NG), ALU.is_equal))
            st(dve.tensor_scalar(gmb[:], gm[:], -1.0, BIG, ALU.add, ALU.mult))
            grouped = lambda x: x.rearrange("p t (g e) -> p t g e", g=NG)
            for t in range(TT):
                w3 = lambda x: x[:, t].unsqueeze(2).broadcast_to([P, NG, EG])
                e3 = lambda x: x.rearrange("p (g e) -> p g e", g=NG)
                st(dve.tensor_tensor(e3(el[:, t]), e3(lg[:, t, NG:]), w3(gm), ALU.mult))
                st(dve.tensor_tensor(e3(el[:, t]), e3(el[:, t]), w3(gmb), ALU.add))
                st(dve.max(emax[:, t], el[:, t]))
                st(dve.max_index(eidx[:, t], emax[:, t], el[:, t]))
            st(dve.tensor_copy(ef[:], eidx[:, :, 0:2]))
            st(dve.tensor_tensor(ge[:], lg[:, :, 0:NG], wide(gmax[:, :, 0], NG), ALU.subtract))
            dve.tensor_tensor(d[:], emax[:, :, 1], emax[:, :, 0], ALU.subtract).then_inc(e_ready, 1)
            for c in range(2):
                st(dve.tensor_tensor(oh[:, c], iota[:, 0:NE].unsqueeze(1).broadcast_to([P, TT, NE]), wide(ef[:, :, c], NE), ALU.is_equal))
            dve.tensor_tensor(both[:], oh[:, 0], oh[:, 1], ALU.add).then_inc(both_done, 1)
            dve.wait_ge(e_done, 1)
            st(dve.tensor_reduce(gs[:], ge[:], AX, ALU.add))
            st(dve.tensor_scalar(den[:], de[:], 1.0, None, ALU.add))
            st(dve.tensor_tensor(den[:], den[:], gs[:], ALU.mult))
            st(dve.reciprocal(wts[:, 0:TT], den[:]))
            st(dve.tensor_tensor(wts[:, TT:], wts[:, 0:TT], de[:], ALU.mult))
            dve.wait_ge(rk_ps, 1)
            st(dve.tensor_scalar(cf[:], ranks[:, TT], float(P - 1), None, ALU.add))
            st(dve.tensor_copy(ci[:], cf[:]))
            sh = P.bit_length() - 1
            st(dve.tensor_scalar(ci[:], ci[:], sh, sh, ALU.logical_shift_right, ALU.logical_shift_left))
            st(dve.tensor_copy(padded[:], ci[:]))
            st(dve.tensor_tensor_scan(pend[:], one[:], padded[:], 0.0, ALU.mult, ALU.add))
            st(dve.tensor_tensor(pstart[:], pend[:], padded[:], ALU.subtract))
            st(dve.tensor_tensor(place[:], ranks[:, 0:TT], pstart[:].unsqueeze(1).broadcast_to([P, TT, NE]), ALU.add))
            for c in range(2):
                st(dve.tensor_tensor(pick[:], place[:], oh[:, c], ALU.mult))
                st(dve.tensor_reduce(df[:, c], pick[:], AX, ALU.add))
            dve.tensor_copy(dest[:], df[:, :, :].rearrange("p c t -> p (c t)")).then_inc(placed, 1)
            st(dve.tensor_tensor(bl[:], pend[0:1].unsqueeze(1).broadcast_to([1, BLOCKS, NE]),
                                 bstart[:].unsqueeze(2).broadcast_to([1, BLOCKS, NE]), ALU.is_le))
            st(dve.tensor_reduce(bef[:, 0:BLOCKS], bl[:], AX, ALU.add))
            st(dve.tensor_scalar(bef[:, 0:BLOCKS], bef[:, 0:BLOCKS], float(NE - 1), None, ALU.min))
            st(dve.tensor_scalar(bef[:, BLOCKS:], pend[0:1, NE - 1:], 1.0 / P, 1.0, ALU.mult, ALU.add))
            st(dve.tensor_copy(be[:], bef[:]))
            st(dve.tensor_scalar(be[:, BLOCKS:], be[:, BLOCKS:], 1, None, ALU.logical_shift_right))


def stage_experts(nc, I, M, h_dram, idx_dram, be, y_dram):
    with Stage(nc, "moe") as s:
        idx = s.sb("idx", [P, BLOCKS], I32)
        one_idx = s.sb("one_idx", [P, 2], I32)
        xg, xT = s.sb("xg", [P, 2, D]), s.sb("xT", [P, 2, KT, P])
        wgu, wd = s.sb("w_gate_up", [P, 2, KT, 2 * FF]), s.sb("w_down", [P, 2, 2, D])
        sg, hh, hT = s.sb("sg", [P, FF]), s.sb("hh", [P, FF]), s.sb("hT", [P, 2, P])
        y = s.sb("y", [P, 2, D])
        turn, gu, th, yo = s.ps("turn", [P, D]), s.ps("gu", [P, 2, NW]), s.ps("th", [P, NW]), s.ps("yo", [P, D])
        idx_in, ix_set, turn_ps, xT_sb, gu_ps, sg_sb, hh_sb, th_ps, hT_sb, y_ps, y_sb = (s.sem(n) for n in (
            "idx_in", "ix_set", "turn_ps", "xT_sb", "gu_ps", "sg_sb", "hh_sb", "th_ps", "hT_sb", "y_ps", "y_sb"))
        gathers = s.sem("gathers")
        w_in, x_in, y_out, w_free, y_free = ([s.sem("w_in0"), s.sem("w_in1")], [s.sem("x_in0"), s.sem("x_in1")],
                                             [s.sem("y_out0"), s.sem("y_out1")], s.sem("w_free"), s.sem("y_free"))
        block = s.ctx.enter_context(nc.Block())
        pairs = lambda eng: eng.value_load(be[0:1, BLOCKS:BLOCKS + 1], min_val=1, max_val=BLOCKS // 2)
        ident = M["ident"]

        @block.sync
        def _(sp):
            sp.dma_start(idx[:], idx_dram.rearrange("(b p) a -> p (b a)", p=P)).then_inc(idx_in, 16)
            n = pairs(sp)
            with sp.Fori(0, n) as i:
                for j in range(2):
                    e = sp.value_load(be[0:1, bass.ds(i * 2 + j, 1)], min_val=0, max_val=NE - 1)
                    sp.wait_ge(w_free, i * 2 + j + 1)
                    for c, name in enumerate(("moe_w_gate", "moe_w_up")):
                        src = I[name][0][bass.ds(e, 1)].rearrange("a (p k) n -> p (a k) n", p=P)
                        sp.dma_start(wgu[:, j, :, c * FF:(c + 1) * FF], src).then_inc(w_in[j], 16)
                    src = I["moe_w_down"][0][bass.ds(e, 1)].rearrange("a (k p) n -> p (a k) n", p=P)
                    sp.dma_start(wd[:, j], src).then_inc(w_in[j], 16)

        @block.gpsimd
        def _(pool):
            pool.wait_ge(idx_in, 16)
            n = pairs(pool)
            with pool.Fori(0, n) as i:
                for j in range(2):
                    pool.wait_ge(xT_sb, i * 2 + j)
                    pool.tensor_copy(one_idx[:, j:j + 1], idx[:, bass.ds(i * 2 + j, 1)]).then_inc(ix_set, 1)
                    pool.wait_ge(ix_set, i * 2 + j + 1)
                    pool.sem_inc(gathers, 1)
                    pool.indirect_dma_start(out=xg[:, j], out_offset=None, in_=h_dram,
                                            in_offset=bass.IndirectOffsetOnAxis(ap=one_idx[:, j:j + 1], axis=0)).then_inc(x_in[j], 16)

        @block.tensor
        def _(pe):
            pe.sem_inc(w_free, 2)
            n = pairs(pe)
            with pe.Fori(0, n) as i:
                for j in range(2):
                    pe.wait_ge(x_in[j], i * 16 + 16)
                    pe.wait_ge(xT_sb, i * 2 + j)
                    for k in range(KT):
                        mm = pe.transpose(turn[:, k * P:(k + 1) * P], xg[:, j].rearrange("p (q k) -> p k q", k=KT)[:, k], ident)
                    mm.then_inc(turn_ps, 1)
                    pe.wait_ge(w_in[j], i * 48 + 48)
                    pe.wait_ge(xT_sb, i * 2 + j + 1)
                    for k in range(KT):
                        mm = pe.matmul(gu[:, j], xT[:, j, k], wgu[:, j, k], start=(k == 0), stop=(k == KT - 1))
                    mm.then_inc(gu_ps, 1)
                    pe.wait_ge(hh_sb, i * 2 + j + 1)
                    for k in range(2):
                        mm = pe.transpose(th[:, k * P:(k + 1) * P], hh[:, k * P:(k + 1) * P], ident)
                    mm.then_inc(th_ps, 1)
                    pe.wait_ge(hT_sb, i * 2 + j + 1)
                    pe.wait_ge(y_sb, (i * 2 + j) * 2)
                    for c in range(2):
                        for k in range(2):
                            mm = pe.matmul(yo[:, c * NW:(c + 1) * NW], hT[:, k], wd[:, j, k, c * NW:(c + 1) * NW], start=(k == 0), stop=(k == 1))
                    mm.then_inc(y_ps, 1)
                    pe.wait_ge(y_sb, (i * 2 + j) * 2 + 2)
                    pe.sem_inc(w_free, 1)

        @block.scalar
        def _(act):
            n = pairs(act)
            with act.Fori(0, n) as i:
                for j in range(2):
                    act.wait_ge(turn_ps, i * 2 + j + 1)
                    act.copy(xT[:, j, :, :].rearrange("p k c -> p (k c)"), turn[:]).then_inc(xT_sb, 1)
                    act.wait_ge(gu_ps, i * 2 + j + 1)
                    act.activation(sg[:], gu[:, j, 0:FF], ACT.Silu).then_inc(sg_sb, 1)
                    act.wait_ge(y_ps, i * 2 + j + 1)
                    act.wait_ge(y_out[j], i * 16)
                    act.copy(y[:, j, 0:NW], yo[:, 0:NW]).then_inc(y_sb, 1)
                    act.wait_ge(y_sb, (i * 2 + j) * 2 + 2)
                    act.dma_start(y_dram[bass.ds((i * 2 + j) * P, P)], y[:, j]).then_inc(y_out[j], 16)
            for j in range(2):
                act.wait_ge(y_out[j], n * 16)
                act.sem_inc(gathers, 1)

        @block.vector
        def _(dve):
            n = pairs(dve)
            with dve.Fori(0, n) as i:
                for j in range(2):
                    dve.wait_ge(sg_sb, i * 2 + j + 1)
                    dve.tensor_tensor(hh[:], sg[:], gu[:, j, FF:], ALU.mult).then_inc(hh_sb, 1)
                    dve.wait_ge(th_ps, i * 2 + j + 1)
                    dve.tensor_copy(hT[:, :, :].rearrange("p k c -> p (k c)"), th[:, 0:2 * P]).then_inc(hT_sb, 1)
                    dve.wait_ge(y_ps, i * 2 + j + 1)
                    dve.wait_ge(y_out[j], i * 16)
                    dve.tensor_copy(y[:, j, NW:], yo[:, NW:]).then_inc(y_sb, 1)


def stage_combine(nc, y_dram, dest, wts, gate, v, nmean, ss):
    with Stage(nc, "combine") as s:
        a, b = s.sb("a", [P, 2, D]), s.sb("b", [P, 2, D])
        junk, sm = s.sb("junk", [P, D]), s.sb("sum", [P, TT])
        rows = [s.sem("rows0"), s.sem("rows1")]
        chain, v_ready, sum_ready, mean_ready, achain = (s.sem(n) for n in ("chain", "v_ready", "sum_ready", "mean_ready", "achain"))
        block = s.ctx.enter_context(nc.Block())

        @block.gpsimd
        def _(pool):
            for t in range(TT):
                if t >= 2:
                    pool.wait_ge(v_ready, t - 1)
                for c, dst in ((0, a), (1, b)):
                    pool.indirect_dma_start(out=dst[:, t % 2], out_offset=None, in_=y_dram, in_offset=bass.IndirectOffsetOnAxis(
                        ap=dest[:, c * TT + t:c * TT + t + 1], axis=0)).then_inc(rows[t % 2], 16)

        @block.vector
        def _(dve):
            st = Steps(dve, chain)
            for t in range(TT):
                j = t % 2
                dve.wait_ge(rows[j], 32 * (t // 2 + 1))
                st(dve.tensor_scalar(a[:, j], a[:, j], wts[:, t:t + 1], None, ALU.mult))
                st(dve.scalar_tensor_tensor(out=a[:, j], in0=b[:, j], scalar=wts[:, TT + t:TT + t + 1], in1=a[:, j], op0=ALU.mult, op1=ALU.add))
                st(dve.scalar_tensor_tensor(out=a[:, j], in0=gate, scalar=1.0, in1=a[:, j], op0=ALU.add, op1=ALU.mult))
                dve.scalar_tensor_tensor(out=v[:, t], in0=v[:, t], scalar=ALPHA, in1=a[:, j], op0=ALU.mult, op1=ALU.add).then_inc(v_ready, 1)
                if t:
                    dve.wait_ge(sum_ready, t)
                    dve.tensor_scalar(nmean[:, t - 1:t], sm[:, t - 1:t], -1.0 / D, None, ALU.mult).then_inc(mean_ready, 1)
            dve.wait_ge(sum_ready, TT)
            dve.tensor_scalar(nmean[:, TT - 1:], sm[:, TT - 1:], -1.0 / D, None, ALU.mult).then_inc(mean_ready, 1)

        @block.scalar
        def _(act):
            moments(act, v, v_ready, sm, sum_ready, nmean, mean_ready, junk, achain, ss)


RMS_EPS = 1e-6
D_FF = 2816
FT = D_FF // P


def stage_rms_features(nc, name, hT, gain, ones, uT, out=None, ident=None):
    with Stage(nc, name) as s:
        g = s.sb("gain", [P, KT])
        sq = s.sb("sq", [P, 2, SEQ])
        r = s.sb("rms", [P, SEQ])
        acc = s.ps("acc", [P, SEQ])
        gin, sq_ready, sq_used, sums, var_ready, root, chain, done = (s.sem(n) for n in (
            "gin", "sq_ready", "sq_used", "sums", "var_ready", "root", "chain", "done"))
        block = s.ctx.enter_context(nc.Block())

        @block.sync
        def _(sp):
            sp.dma_start(g[:], gain.rearrange("(k p) -> p k", p=P)).then_inc(gin, 16)

        @block.scalar
        def _(act):
            for k in range(KT):
                if k >= 2:
                    act.wait_ge(sq_used, k - 1)
                act.activation(sq[:, k % 2], hT[:, k], ACT.Square).then_inc(sq_ready, 1)
            act.wait_ge(var_ready, 1)
            act.activation(r[:], r[:], ACT.Sqrt).then_inc(root, 1)

        @block.tensor
        def _(pe):
            for k in range(KT):
                pe.wait_ge(sq_ready, k + 1)
                for c in range(2):
                    mm = pe.matmul(acc[:, c * NW:(c + 1) * NW], ones, sq[:, k % 2, c * NW:(c + 1) * NW], start=(k == 0), stop=(k == KT - 1))
                mm.then_inc(sq_used, 1)

        @block.vector
        def _(dve):
            dve.wait_ge(sq_used, KT)
            dve.tensor_scalar(r[:], acc[:], 1.0 / D, RMS_EPS, ALU.mult, ALU.add).then_inc(var_ready, 1)
            dve.wait_ge(root, 1)
            dve.reciprocal(r[:], r[:]).then_inc(chain, 1)
            dve.wait_ge(chain, 1)
            dve.wait_ge(gin, 16)
            for k in range(KT):
                dve.scalar_tensor_tensor(out=uT[:, k], in0=hT[:, k], scalar=g[:, k:k + 1], in1=r[:],
                                         op0=ALU.mult, op1=ALU.mult).then_inc(done, 1)


def stage_linear(nc, name, groups, tiles, act_part, dve_part, steps=0, bufs=2, scratch=None):
    kt = sum(src.shape[1] for g in groups for _, src in g)
    n = len(groups)
    with Stage(nc, name) as s:
        w = s.sb("w", [P, 2, kt, P])
        tmp = s.sb("tmp", scratch) if scratch else None
        acc = s.ps("acc", [P, bufs, n, SEQ])
        w_in = [s.sem("w_in0"), s.sem("w_in1")]
        acc_ready, acc_free, act_ready, chain = (s.sem(x) for x in ("acc_ready", "acc_free", "act_ready", "chain"))
        per = sum(len(g) for g in groups)
        block = s.ctx.enter_context(nc.Block())

        @block.sync
        def _(sp):
            with sp.Fori(0, tiles // 2) as i:
                for j in range(2):
                    sp.wait_ge(acc_ready, i * 2 + j)
                    k0 = 0
                    for g in groups:
                        for wd, src in g:
                            k1 = k0 + src.shape[1]
                            sp.dma_start(w[:, j, k0:k1], wd[:, :, bass.ds((i * 2 + j) * P, P)]).then_inc(w_in[j], 16)
                            k0 = k1

        @block.tensor
        def _(pe):
            pe.sem_inc(acc_ready, 1)
            with pe.Fori(0, tiles // 2) as i:
                for j in range(2):
                    b = j % bufs
                    pe.wait_ge(acc_free, i * 2 + j + 1)
                    pe.wait_ge(w_in[j], i * (16 * per) + 16 * per)
                    k0 = 0
                    for q, g in enumerate(groups):
                        kg = sum(src.shape[1] for _, src in g)
                        for c in range(2):
                            k = k0
                            for wd, src in g:
                                for kk in range(src.shape[1]):
                                    mm = pe.matmul(acc[:, b, q, c * NW:(c + 1) * NW], w[:, j, k], src[:, kk, c * NW:(c + 1) * NW],
                                                   start=(k == k0), stop=(k == k0 + kg - 1))
                                    k += 1
                        k0 += kg
                    mm.then_inc(acc_ready, 1)

        @block.scalar
        def _(act):
            if act_part is not None:
                with act.Fori(0, tiles // 2) as i:
                    for j in range(2):
                        act.wait_ge(acc_ready, i * 2 + j + 2)
                        act.wait_ge(acc_free, i * 2 + j + (bufs - 1))
                        act_part(act, i * 2 + j, j, [acc[:, j % bufs, q] for q in range(n)], tmp).then_inc(act_ready, 1)

        @block.vector
        def _(dve):
            dve.sem_inc(acc_free, bufs)
            with dve.Fori(0, tiles // 2) as i:
                for j in range(2):
                    st = Steps(dve, chain, at=(i * 2 + j) * steps)
                    dve.wait_ge(acc_ready, i * 2 + j + 2)
                    if act_part is not None:
                        dve.wait_ge(act_ready, i * 2 + j + 1)
                    dve_part(dve, i * 2 + j, j, [acc[:, j % bufs, q] for q in range(n)], tmp, st).then_inc(acc_free, 1)
                    assert st.n == steps


def tile_of(x, m):
    return x[:, bass.ds(m, 1), :].rearrange("p a t -> p (a t)")


def stage_ffn(nc, name, wg, wu, wd, uT, aT, hT):
    rows = lambda x: x.rearrange("(k p) n -> p k n", p=P)

    def silu_gate(act, m, j, acc, tmp):
        return act.activation(tmp[:, j], acc[0], ACT.Silu)

    def times_up(dve, m, j, acc, tmp, st):
        return dve.tensor_tensor(tile_of(aT, m), tmp[:, j], acc[1], ALU.mult)

    stage_linear(nc, name + "_in", [[(rows(wg), uT)], [(rows(wu), uT)]], FT, silu_gate, times_up, scratch=[P, 2, SEQ])
    SL = FT // 2
    with Stage(nc, name + "_out") as s:
        w = s.sb("w", [P, SL, NW])
        acc = s.ps("acc", [P, 4, SEQ])
        w_in = [s.sem(f"w_in{j}") for j in range(SL)]
        w_used, acc_free = s.sem("w_used"), s.sem("acc_free")
        block = s.ctx.enter_context(nc.Block())

        @block.sync
        def _(sp):
            with sp.Fori(0, 4) as i:
                for j in range(SL):
                    sp.wait_ge(w_used, i * SL + j + 1)
                    row = (i % 2) * (SL * P) + j * P
                    sp.dma_start(w[:, j], wd[bass.ds(row, P), bass.ds((i // 2) * NW, NW)]).then_inc(w_in[j], 16)

        @block.tensor
        def _(pe):
            pe.sem_inc(w_used, SL)
            for c in range(2):
                if c:
                    pe.wait_ge(acc_free, 4)
                for half in range(2):
                    for j in range(SL):
                        pe.wait_ge(w_in[j], 16 * (2 * c + half + 1))
                        f = half * SL + j
                        for q in range(4):
                            for t in range(2):
                                mm = pe.matmul(acc[:, q, t * NW:(t + 1) * NW], w[:, j, q * P:(q + 1) * P],
                                               aT[:, f, t * NW:(t + 1) * NW], start=(f == 0), stop=(f == FT - 1))
                        mm.then_inc(w_used, 1)

        @block.vector
        def _(dve):
            for c in range(2):
                dve.wait_ge(w_used, SL + FT * (c + 1))
                for q in range(4):
                    k = 4 * c + q
                    dve.scalar_tensor_tensor(out=hT[:, k], in0=acc[:, q], scalar=0.5, in1=hT[:, k],
                                             op0=ALU.mult, op1=ALU.add).then_inc(acc_free, 1)


def stage_store(nc, uT, ident, out):
    with Stage(nc, "store") as s:
        o = s.sb("o", [P, 4, D])
        turned = s.ps("turned", [P, 4, D])
        ready, free_a, free_d = (s.sem(n) for n in ("ready", "free_a", "free_d"))
        stored = [s.sem(f"stored{n}") for n in range(4)]
        view = out[0].rearrange("(t p) d -> t p d", p=P)
        block = s.ctx.enter_context(nc.Block())

        @block.tensor
        def _(pe):
            for t in range(TT):
                if t >= 4:
                    pe.wait_ge(free_a, t - 3)
                    pe.wait_ge(free_d, t - 3)
                for k in range(KT):
                    mm = pe.transpose(turned[:, t % 4, k * P:(k + 1) * P], uT[:, k, t * P:(t + 1) * P], ident)
                mm.then_inc(ready, 1)

        def take(eng, copy, half, free):
            for t in range(TT):
                eng.wait_ge(ready, t + 1)
                if t >= 4:
                    eng.wait_ge(stored[t % 4], 16 * (t // 4))
                c = slice(half * NW, half * NW + NW)
                copy(o[:, t % 4, c], turned[:, t % 4, c]).then_inc(free, 1)

        @block.scalar
        def _(act):
            take(act, act.copy, 0, free_a)

        @block.vector
        def _(dve):
            take(dve, dve.tensor_copy, 1, free_d)

        @block.sync
        def _(sp):
            for t in range(TT):
                sp.wait_ge(free_a, t + 1)
                sp.wait_ge(free_d, t + 1)
                sp.dma_start(view[t], o[:, t % 4]).then_inc(stored[t % 4], 16)
            for n in range(4):
                sp.wait_ge(stored[n], 16 * (TT // 4))


PLE = 256
GRID = 64
NAH, NAW = 8, 16
HD = 64
PAIRS = SEQ // (2 * GRID)
PADR = 128
EDGE, INNER = 14, 9
SLOTS = EDGE + INNER


def pair_window(p):
    rows = SEQ // GRID
    clip = lambda r: min(max(r - NAH // 2, 0), rows - NAH)
    a, b = clip(2 * p), clip(2 * p + 1)
    if a == b:
        return a, NAH * GRID, NAH - 1 + a - 2 * p - 1
    return a, (NAH + 1) * GRID, EDGE


def stage_bias_rows(nc, I, shift_dram):
    with Stage(nc, "biasrows") as s:
        z = s.sb("z", [8 * (2 * NAH - 1), PADR])
        n = 2 * NAW - 1
        zeroed, filled, stored = s.sem("zeroed"), s.sem("filled"), s.sem("stored")
        block = s.ctx.enter_context(nc.Block())

        @block.gpsimd
        def _(pool):
            pool.memset(z[:], 0.0).then_inc(zeroed, 1)

        @block.sync
        def _(sp):
            sp.wait_ge(zeroed, 1)
            lo = GRID - NAW
            sp.dma_start(z[:, lo:lo + n], I["na_rpb_2"][0].rearrange("h r c -> (h r) c")).then_inc(filled, 16)
            sp.wait_ge(filled, 16)
            with sp.Fori(0, GRID) as i:
                sp.dma_start(shift_dram[bass.ds(GRID - 1 - i, 1)].rearrange("c r k -> (c r) k"), z[:, bass.ds(i, GRID)]).then_inc(stored, 16)
            sp.wait_ge(stored, 16 * GRID)


def stage_neighbourhood(nc, I, K, ident, uT, naT, shift_dram):
    R = 2 * NAH - 1
    scale = HD ** -0.5
    U = PAIRS * 2
    with Stage(nc, "na") as s:
        w = s.sb("w", [P, 3, KT, P])
        mask = s.sb("mask", [P, SLOTS, GRID])
        tb = s.sb("bias", [P, 2, SLOTS, GRID])
        qT, kT, V = s.sb("qT", [P, SEQ]), s.sb("kT", [P, SEQ]), s.sb("V", [P, TT, P])
        KW = (NAH + 1) * GRID
        pr, prT = s.sb("probs", [P, 2, KW]), s.sb("probsT", [P, 2, 5, P])
        yt = s.sb("y_tok", [P, 2, P])
        mx, nm, rsum, rinv = (s.sb(n, [P, 2, 1]) for n in ("mx", "nm", "rsum", "rinv"))
        S = [s.ps("S0", [P, SEQ]), s.ps("S1", [P, SEQ])]
        T, O = s.ps("T", [P, SEQ]), s.ps("O", [P, 2, NW])
        names = ("mask_in w_in w_used b_in zeroed tb_ready qkv_ps q_sb k_sb v_sb s_ps m_set nm_set p_sb pT_ps pT_a pT_d o_ps y_sb yT_ps yT_sb "
                 "chain units").split()
        m = {n: s.sem(n) for n in names}
        win = I["w_in_2"][0].rearrange("(k p) n -> p k n", p=P)
        block = s.ctx.enter_context(nc.Block())

        def shifted(i, hh, dr, n):
            return shift_dram[:, bass.ds((i * 2 + hh) * R + dr, n)]

        @block.sync
        def _(sp):
            sp.dma_start(mask[:], K["na_mask"]).then_inc(m["mask_in"], 16)
            sp.wait_ge(m["zeroed"], 1)
            with sp.Fori(0, 4) as i:
                sp.wait_ge(m["w_used"], i)
                for c in range(3):
                    sp.dma_start(w[:, c], win[:, :, bass.ds(i * P + c * NW, P)]).then_inc(m["w_in"], 16)
                sp.wait_ge(m["y_sb"], i * U)
                for hh in range(2):
                    for r, dr, n, at in ((0, 1, EDGE, 0), (64, 0, EDGE, 0), (0, 3, NAH, EDGE), (64, 3, NAH, EDGE + 1)):
                        sp.dma_start(tb[r:r + GRID, hh, at:at + n], shifted(i, hh, dr, n)).then_inc(m["b_in"], 16)

        @block.gpsimd
        def _(pool):
            pool.memset(tb[0:64, :, SLOTS - 1], 0.0)
            pool.memset(tb[64:128, :, EDGE], 0.0).then_inc(m["zeroed"], 1)

        def window(u):
            p, hh = u // 2, u % 2
            row, n, slot = pair_window(p)
            return p, hh, row, n, slot

        @block.tensor
        def _(pe):
            with pe.Fori(0, 4) as i:
                pe.wait_ge(m["w_in"], i * 48 + 48)
                pe.wait_ge(m["yT_sb"], i * PAIRS)
                for c, dst in ((0, S[0]), (1, S[1])):
                    for t in range(2):
                        for k in range(KT):
                            pe.matmul(dst[:, t * NW:(t + 1) * NW], w[:, c, k], uT[:, k, t * NW:(t + 1) * NW], start=(k == 0), stop=(k == KT - 1))
                for t in range(TT):
                    for k in range(KT):
                        mm = pe.matmul(T[:, t * P:(t + 1) * P], uT[:, k, t * P:(t + 1) * P], w[:, 2, k], start=(k == 0), stop=(k == KT - 1),
                                       skip_group_check=True)
                mm.then_inc(m["qkv_ps"], 1)
                pe.wait_ge(m["qkv_ps"], i + 1)
                pe.sem_inc(m["w_used"], 1)
                pe.wait_ge(m["q_sb"], i + 1)
                pe.wait_ge(m["k_sb"], i + 1)
                pe.wait_ge(m["v_sb"], i + 1)

                def scores(u):
                    p, hh, row, n, slot = window(u)
                    if u >= 2:
                        pe.wait_ge(m["m_set"], i * U + u - 1)
                    r = slice(64 * hh, 64 * hh + 64)
                    for a in range(0, n, NW):
                        b = min(n, a + NW)
                        mm = pe.matmul(S[hh][:, a:b], qT[r, p * P:(p + 1) * P], kT[r, row * GRID + a:row * GRID + b], start=True, stop=True)
                    mm.then_inc(m["s_ps"], 1)

                def turn_out(p):
                    pe.wait_ge(m["y_sb"], i * U + 2 * p + 2)
                    if p:
                        pe.wait_ge(m["yT_sb"], i * PAIRS + p)
                    pe.transpose(T[:, 768:768 + P], yt[:, p % 2], ident).then_inc(m["yT_ps"], 1)

                scores(0)
                for u in range(U):
                    p, hh, row, n, slot = window(u)
                    if u + 1 < U:
                        scores(u + 1)
                    pe.wait_ge(m["p_sb"], i * U + u + 1)
                    if u:
                        pe.wait_ge(m["pT_a"], i * U + u)
                        pe.wait_ge(m["pT_d"], i * U + u)
                    if u % 2 == 0 and u >= 4:
                        pe.wait_ge(m["yT_sb"], i * PAIRS + p - 1)
                    if u % 2 == 1 and u >= 3:
                        turn_out(p - 1)
                    for q in range(4):
                        mm = pe.transpose(T[:, q * P:(q + 1) * P], pr[:, u % 2, q * P:(q + 1) * P], ident)
                    if n > NW:
                        mm = pe.matmul(T[0:64, NW:NW + P], pr[:, u % 2, NW:n], ident, start=True, stop=True, skip_group_check=True)
                    mm.then_inc(m["pT_ps"], 1)
                    pe.wait_ge(m["pT_a"], i * U + u + 1)
                    pe.wait_ge(m["pT_d"], i * U + u + 1)
                    if u >= 2:
                        pe.wait_ge(m["y_sb"], i * U + u - 1)
                    t0 = row * GRID // P
                    for q in range(4):
                        mm = pe.matmul(O[:, u % 2, 0:HD], prT[:, u % 2, q], V[:, t0 + q, hh * HD:(hh + 1) * HD],
                                       start=(q == 0), stop=(q == 3 and n == NW))
                    if n > NW:
                        mm = pe.matmul(O[:, u % 2, 0:HD], prT[0:64, u % 2, 4], V[0:64, t0 + 4, hh * HD:(hh + 1) * HD], start=False, stop=True)
                    mm.then_inc(m["o_ps"], 1)
                turn_out(PAIRS - 1)

        @block.scalar
        def _(act):
            with act.Fori(0, 4) as i:
                act.wait_ge(m["qkv_ps"], i + 1)
                act.copy(qT[:], S[0][:]).then_inc(m["q_sb"], 1)
                act.copy(V[:, :, :].rearrange("p t c -> p (t c)"), T[:]).then_inc(m["v_sb"], 1)
                for u in range(U):
                    p, hh, row, n, slot = window(u)
                    act.wait_ge(m["nm_set"], i * U + u + 1)
                    act.activation(pr[:, u % 2, 0:n], pr[:, u % 2, 0:n], ACT.Exp, bias=nm[:, u % 2], scale=scale,
                                   accum_out=rsum[:, u % 2]).then_inc(m["p_sb"], 1)
                    act.wait_ge(m["pT_ps"], i * U + u + 1)
                    act.copy(prT[:, u % 2, 0:4, :].rearrange("p q c -> p (q c)"), T[:, 0:NW]).then_inc(m["pT_a"], 1)

        @block.vector
        def _(dve):
            N = 1 + 2 * U - U + U
            dve.wait_ge(m["mask_in"], 16)
            with dve.Fori(0, 4) as i:
                st = Steps(dve, m["chain"], at=i * N)
                dve.wait_ge(m["b_in"], i * 128 + 128)
                for hh in range(2):
                    ins = dve.scalar_tensor_tensor(out=tb[:, hh], in0=tb[:, hh], scalar=1.0 / scale, in1=mask[:],
                                                   op0=ALU.mult, op1=ALU.add)
                st(ins)
                dve.wait_ge(m["qkv_ps"], i + 1)
                dve.tensor_copy(kT[:], S[1][:]).then_inc(m["k_sb"], 1)

                def largest(u):
                    p, hh, row, n, slot = window(u)
                    dve.wait_ge(m["s_ps"], i * U + u + 1)
                    if u >= 2:
                        dve.wait_ge(m["pT_ps"], i * U + u - 1)
                    dve.sem_inc(m["units"], 1)
                    dve.tensor_tensor_reduce(out=pr[:, u % 2, 0:n], in0=S[hh][:, 0:n],
                                             in1=tb[:, hh, slot:slot + n // GRID, :].rearrange("p s c -> p (s c)"),
                                             scale=1.0, scalar=-3.0e38, op0=ALU.add, op1=ALU.max,
                                             accum_out=mx[:, u % 2]).then_inc(m["m_set"], 1)
                    dve.wait_ge(m["m_set"], i * U + u + 1)
                    dve.tensor_scalar(nm[:, u % 2], mx[:, u % 2], -scale, None, ALU.mult).then_inc(m["nm_set"], 1)

                largest(0)
                for u in range(U):
                    p, hh, row, n, slot = window(u)
                    if u + 1 < U:
                        largest(u + 1)
                    dve.wait_ge(m["p_sb"], i * U + u + 1)
                    st(dve.reciprocal(rinv[:, u % 2], rsum[:, u % 2]))
                    dve.wait_ge(m["pT_ps"], i * U + u + 1)
                    if n > NW:
                        dve.tensor_copy(prT[0:64, u % 2, 4], T[0:64, NW:NW + P]).then_inc(m["pT_d"], 1)
                    else:
                        dve.sem_inc(m["pT_d"], 1)
                    if u % 2 == 1 and u >= 3:
                        dve.wait_ge(m["yT_ps"], i * PAIRS + p)
                        dve.tensor_copy(naT[:, bass.ds(i, 1), (p - 1) * P:p * P].rearrange("p a t -> p (a t)"), T[:, 768:768 + P]).then_inc(m["yT_sb"], 1)
                    dve.wait_ge(m["o_ps"], i * U + u + 1)
                    dve.tensor_scalar(yt[:, p % 2, hh * HD:(hh + 1) * HD], O[:, u % 2, 0:HD], rinv[:, u % 2], None,
                                      ALU.mult).then_inc(m["y_sb"], 1)
                dve.wait_ge(m["yT_ps"], i * PAIRS + PAIRS)
                dve.tensor_copy(naT[:, bass.ds(i, 1), (PAIRS - 1) * P:].rearrange("p a t -> p (a t)"), T[:, 768:768 + P]).then_inc(m["yT_sb"], 1)
                while st.n < N:
                    dve.sem_inc(m["chain"], 1)
                    st.n += 1


SG, SP_, SI = 32, 64, 16
L = 8
NCH = SEQ // L
GP = SG // 2
Q = 4
PQ = GP // Q
HALF_PI = 1.5707963267948966


def complex_product(op, out, a, b, t1, t2, conj_b=False):
    (orr, oi), (ar, ai), (br, bi) = out, a, b
    op(t1, ar, br, ALU.mult)
    op(t2, ai, bi, ALU.mult)
    op(orr, t1, t2, ALU.add if conj_b else ALU.subtract)
    op(t1, ai, br, ALU.mult)
    op(t2, ar, bi, ALU.mult)
    op(oi, t1, t2, ALU.subtract if conj_b else ALU.add)


def stage_ssm_parameters(nc, I, ident, powers, w8, r8, bbar, ct):
    ND = 2 * GP
    W = lambda n: I[n + "_2"][0]
    with Stage(nc, "ssmpar") as s:
        rows = s.sb("rows", [3 * ND, 2, SP_])
        ldt = s.sb("ldt", [3 * ND, 2])
        names = "lr li dt a b er em e1 r h sh ch cs sn cm Er Ei den cr ci t1 t2".split()
        x = {n: s.sb(n, [P, ND]) for n in names}
        ki = s.sb("ki", [P, ND], I32)
        bre, bim = s.sb("bre", [P, ND, SI]), s.sb("bim", [P, ND, SI])
        u1, u2 = s.sb("u1", [P, ND, SI]), s.sb("u2", [P, ND, SI])
        cl = s.sb("c_rows", [P, 4, 4, 2, SP_])
        ps, pc = s.ps("params", [P, NW]), s.ps("c_turned", [P, 4, 4, P])
        par, exp_rows, turned, chain, a1, a2, c_ps, d1, d2 = (s.sem(n) for n in ("par", "exp_rows", "turned", "chain", "a1", "a2", "c_ps", "d1", "d2"))
        block = s.ctx.enter_context(nc.Block())

        @block.sync
        def _(sp):
            for n, name in enumerate(("ssm_lam_re", "ssm_lam_im")):
                sp.dma_start(rows[n * ND:(n + 1) * ND], W(name).rearrange("d (q g) p -> (d q) g p", g=2)).then_inc(par, 16)
            sp.dma_start(ldt[2 * ND:], W("ssm_log_dt").rearrange("d (q g) -> (d q) g", g=2)).then_inc(par, 16)
            for dst, name in ((bre, "ssm_b_re"), (bim, "ssm_b_im")):
                for d in range(2):
                    for g in range(2):
                        src = W(name)[d].rearrange("(q g) p i -> g p q i", g=2)[g]
                        sp.dma_start(dst[g * 64:(g + 1) * 64, d * GP:(d + 1) * GP], src).then_inc(par, 16)
            for n, name in enumerate(("ssm_c_re", "ssm_c_im")):
                for d in range(2):
                    src = W(name)[d].rearrange("(t g) o p -> (g o) t p", t=4)
                    for dup in range(2):
                        sp.dma_start(cl[:, 2 * n + d, :, dup], src).then_inc(par, 16)
        NPAR = 16 * (3 + 8 + 8)

        @block.tensor
        def _(pe):
            pe.wait_ge(par, NPAR)
            pe.wait_ge(exp_rows, 1)
            pe.matmul(ps[:, 0:3 * ND], rows[:, :, :].rearrange("a g p -> a (g p)"), ident[0:3 * ND, 0:3 * ND], start=True, stop=True).then_inc(turned, 1)
            for n in range(4):
                for t in range(4):
                    mm = pe.transpose(pc[:, n, t], cl[:, n, t, :, :].rearrange("a d p -> a (d p)"), ident)
            mm.then_inc(c_ps, 1)

        @block.scalar
        def _(act):
            act.wait_ge(turned, 1)
            act.wait_ge(d1, 1)
            act.activation(x["dt"][:], x["dt"][:], ACT.Exp).then_inc(a1, 1)
            act.wait_ge(d2, 1)
            act.activation(x["sh"][:], x["h"][:], ACT.Sin)
            act.activation(x["ch"][:], x["t2"][:], ACT.Sin).then_inc(a2, 1)

        @block.vector
        def _(dve):
            st = Steps(dve, chain)
            v = {n: t[:] for n, t in x.items()}
            op = lambda o, a, b, f: st(dve.tensor_tensor(o, a, b, f))
            sc = lambda o, a, s1, f1, s2=None, f2=None: st(dve.tensor_scalar(o, a, s1, s2, f1, *([f2] if f2 else [])))
            dve.wait_ge(par, NPAR)
            dve.tensor_copy(rows[2 * ND:], ldt[2 * ND:].unsqueeze(2).broadcast_to([ND, 2, SP_])).then_inc(exp_rows, 1)
            dve.wait_ge(turned, 1)
            sc(v["lr"], ps[:, 0:ND], -1e-4, ALU.min)
            st(dve.tensor_copy(v["li"], ps[:, ND:2 * ND]))
            dve.tensor_copy(v["dt"], ps[:, 2 * ND:3 * ND]).then_inc(d1, 1)
            dve.wait_ge(a1, 1)
            op(v["a"], v["lr"], v["dt"], ALU.mult)
            op(v["b"], v["li"], v["dt"], ALU.mult)
            sc(v["a"], v["a"], -64.0, ALU.max)
            sc(v["h"], v["a"], 1.0 / 128, ALU.mult)
            st(dve.memset(v["em"], 1.0))
            for n in range(8, 1, -1):
                op(v["t1"], v["em"], v["h"], ALU.mult)
                sc(v["em"], v["t1"], 1.0 / n, ALU.mult, 1.0, ALU.add)
            op(v["em"], v["em"], v["h"], ALU.mult)
            for n in range(7):
                sc(v["t1"], v["em"], 2.0, ALU.add)
                op(v["em"], v["em"], v["t1"], ALU.mult)
            sc(v["er"], v["em"], 1.0, ALU.add)
            sc(v["t1"], v["b"], 1.0 / (4 * HALF_PI), ALU.mult)
            st(dve.tensor_copy(ki[:], v["t1"]))
            st(dve.tensor_copy(v["t1"], ki[:]))
            for part in (-6.28125, -0.0019350051879882812, -3.0199159819e-07):
                st(dve.scalar_tensor_tensor(out=v["b"], in0=v["t1"], scalar=part, in1=v["b"], op0=ALU.mult, op1=ALU.add))
            sc(v["b"], v["b"], 2 * HALF_PI, ALU.min, -2 * HALF_PI, ALU.max)
            sc(v["h"], v["b"], 0.5, ALU.mult)
            st(dve.scalar_tensor_tensor(out=v["t1"], in0=v["h"], scalar=-1.0, in1=v["h"], op0=ALU.mult, op1=ALU.min))
            dve.tensor_scalar(v["t2"], v["t1"], HALF_PI, None, ALU.add).then_inc(d2, 1)
            dve.wait_ge(a2, 1)
            op(v["cm"], v["sh"], v["sh"], ALU.mult)
            sc(v["cm"], v["cm"], -2.0, ALU.mult)
            sc(v["cs"], v["cm"], 1.0, ALU.add)
            op(v["sn"], v["sh"], v["ch"], ALU.mult)
            sc(v["sn"], v["sn"], 2.0, ALU.mult)
            op(v["t1"], v["em"], v["cs"], ALU.mult)
            op(v["Er"], v["t1"], v["cm"], ALU.add)
            op(v["Ei"], v["er"], v["sn"], ALU.mult)
            op(v["t1"], v["lr"], v["lr"], ALU.mult)
            op(v["t2"], v["li"], v["li"], ALU.mult)
            op(v["den"], v["t1"], v["t2"], ALU.add)
            st(dve.reciprocal(v["den"], v["den"]))
            complex_product(op, (v["cr"], v["ci"]), (v["Er"], v["Ei"]), (v["lr"], v["li"]), v["t1"], v["t2"], conj_b=True)
            op(v["cr"], v["cr"], v["den"], ALU.mult)
            op(v["ci"], v["ci"], v["den"], ALU.mult)
            wide = lambda y: y.unsqueeze(2).broadcast_to([P, ND, SI])
            complex_product(op, (bbar[:, 0], bbar[:, 1]), (bre[:], bim[:]), (wide(v["cr"]), wide(v["ci"])), u1[:], u2[:])
            pw = lambda n: (powers[:, 0, n], powers[:, 1, n])
            st(dve.memset(powers[:, 0, 0], 1.0))
            st(dve.memset(powers[:, 1, 0], 0.0))
            op(powers[:, 0, 1], v["er"], v["cs"], ALU.mult)
            op(powers[:, 1, 1], v["er"], v["sn"], ALU.mult)
            for n in range(2, L + 1):
                complex_product(op, pw(n), pw(n // 2), pw(n - n // 2), v["t1"], v["t2"])
            wr, wi = w8[:, 0], w8[:, 1]
            st(dve.tensor_copy(wr, v["cs"]))
            st(dve.tensor_copy(wi, v["sn"]))
            st(dve.tensor_copy(r8, v["er"]))
            for n in range(3):
                op(v["t1"], wr, wr, ALU.mult)
                op(v["t2"], wi, wi, ALU.mult)
                op(v["h"], wr, wi, ALU.mult)
                op(wr, v["t1"], v["t2"], ALU.subtract)
                sc(wi, v["h"], 2.0, ALU.mult)
                op(r8, r8, r8, ALU.mult)
            dve.wait_ge(c_ps, 1)
            for n in range(4):
                for g in range(2):
                    r = slice(64 * g, 64 * g + 64)
                    src = pc[r, n].rearrange("p t (q g o) -> p t q g o", g=2, o=SI)[:, :, :, g]
                    dst = ct[r, n // 2, (n % 2) * GP:(n % 2 + 1) * GP].rearrange("p (t q) o -> p t q o", t=4)
                    for t in range(4):
                        st(dve.tensor_copy(dst[:, t], src[:, t]))


def stage_phasors(nc, w8, wt):
    with Stage(nc, "phasors") as s:
        ND = 2 * GP
        t1, t2 = s.sb("t1", [P, ND, NCH // 2]), s.sb("t2", [P, ND, NCH // 2])
        sq = s.sb("sq", [P, 2, 2, ND])
        chain = s.sem("chain")
        block = s.ctx.enter_context(nc.Block())

        @block.vector
        def _(dve):
            st = Steps(dve, chain)
            op = lambda o, a, b, f: st(dve.tensor_tensor(o, a, b, f))
            st(dve.memset(wt[:, 0, :, 0], 1.0))
            st(dve.memset(wt[:, 1, :, 0], 0.0))
            st(dve.tensor_copy(sq[:, 0], w8[:]))
            n, cur = 1, 0
            while n < NCH:
                b = lambda c: sq[:, cur, c].unsqueeze(2).broadcast_to([P, ND, n])
                complex_product(op, (wt[:, 0, :, n:2 * n], wt[:, 1, :, n:2 * n]), (wt[:, 0, :, 0:n], wt[:, 1, :, 0:n]),
                                (b(0), b(1)), t1[:, :, 0:n], t2[:, :, 0:n])
                a = (sq[:, cur, 0], sq[:, cur, 1])
                complex_product(op, (sq[:, 1 - cur, 0], sq[:, 1 - cur, 1]), a, a, t1[:, :, 0], t2[:, :, 0])
                n, cur = 2 * n, 1 - cur


def stage_ssm(nc, I, M, uT, powers, r8, bbar, ct, wt, yT):
    ident, flip = M["ident"], M["flip"]
    W = lambda n: I[n + "_2"][0]
    G8 = 2 * PQ
    with Stage(nc, "ssm") as s:
        w = s.sb("w", [P, KT, P])
        dcol = s.sb("dcol", [P, SG])
        S2 = s.sb("S2", [P, G8, L, SI])
        U, Ur = s.sb("U", [P, G8, P]), s.sb("Ur", [P, G8, P])
        A = s.sb("A", [P, 2, PQ, L, SI])
        pt1, pt2 = s.sb("pt1", [P, PQ, L + 1, SI]), s.sb("pt2", [P, PQ, L + 1, SI])
        Bq = s.sb("Bq", [P, 2, PQ, SI])
        PT = s.sb("PT", [P, 2, PQ, 2, L + 1, SI])
        Min = s.sb("Min", [P, 2, PQ, P])
        Kt = s.sb("Kt", [SI, PQ, 2, L, SI])
        Tf, Tb, T = (s.sb(n, [P, G8, L * SI]) for n in ("Tf", "Tb", "T"))
        R = s.sb("R", [P, PQ, NCH])
        z = s.sb("z", [P, 2, PQ, NCH])
        pad = s.sb("pad", [P, 2, PQ, NCH + 1])
        Yb, Yg = s.sb("Yb", [P, G8 * P]), s.sb("Yg", [P, L, G8, SI])
        X = [s.ps(f"X{n}", [P, SEQ]) for n in range(4)]
        names = ("w_in d_in s2_ps s2_sb u_ps u_sb ur_sb a_sb min_ps min_sb pt_sb k_ps k_sb t_in v_ps pad_sb yb_ps yb_sb y_ps yg_sb yt_ps yt_sb "
                 "zeroed chain t_ready q_done").split()
        m = {n: s.sem(n) for n in names}
        block = s.ctx.enter_context(nc.Block())
        win = I["w_in_2"][0].rearrange("(k p) n -> p k n", p=P)

        @block.sync
        def _(sp):
            for j in range(L):
                sp.dma_start(dcol[j * SI:(j + 1) * SI], W("ssm_d").rearrange("(g i) -> i g", i=SI)).then_inc(m["d_in"], 16)
            with sp.Fori(0, Q) as i:
                sp.wait_ge(m["s2_ps"], i)
                sp.dma_start(w[:], win[:, :, bass.ds(3 * NW + i * P, P)]).then_inc(m["w_in"], 16)
                for d in range(2):
                    sp.wait_ge(m["k_sb"], i * 2 + d + 1)
                    Td = (Tf, Tb)[d]
                    src = Kt[:, :, :, :, :].rearrange("i q g l o -> i (q g) (l o)")
                    for j in range(L):
                        dst = Td[j * SI:(j + 1) * SI]
                        if d == 0:
                            sp.dma_start(dst[:, :, j * SI:], src[:, :, 0:(L - j) * SI]).then_inc(m["t_in"], 16)
                        else:
                            sp.dma_start(dst[:, :, 0:(j + 1) * SI], src[:, :, (L - 1 - j) * SI:]).then_inc(m["t_in"], 16)

        @block.gpsimd
        def _(pool):
            pool.memset(Tf[:], 0.0)
            pool.memset(Tb[:], 0.0)
            pool.memset(PT[:], 0.0)
            pool.memset(pad[:], 0.0).then_inc(m["zeroed"], 1)

        @block.tensor
        def _(pe):
            pe.wait_ge(m["zeroed"], 1)
            with pe.Fori(0, Q) as i:
                pe.wait_ge(m["w_in"], i * 16 + 16)
                pe.wait_ge(m["q_done"], i)
                for j in range(L):
                    for k in range(KT):
                        mm = pe.matmul(X[0][:, j * P:(j + 1) * P], uT[:, k].rearrange("p (c j) -> p j c", j=L)[:, j], w[:, k],
                                       start=(k == 0), stop=(k == KT - 1), skip_group_check=True)
                mm.then_inc(m["s2_ps"], 1)
                pe.wait_ge(m["s2_sb"], i + 1)
                for g in range(G8):
                    src = S2[:, g, :, :].rearrange("p l i -> p (l i)")
                    pe.matmul(X[1][:, g * P:(g + 1) * P], src, ident, start=True, stop=True, skip_group_check=True)
                    mm = pe.matmul(X[2][:, g * P:(g + 1) * P], src, flip, start=True, stop=True, skip_group_check=True)
                mm.then_inc(m["u_ps"], 1)
                for d in range(2):
                    pe.wait_ge(m["a_sb"], i * 2 + d + 1)
                    for c in range(2):
                        for q in range(PQ):
                            mm = pe.transpose(X[0][:, (c * PQ + q) * P:(c * PQ + q + 1) * P],
                                              A[:, c, q, :, :].rearrange("p l i -> p (l i)"), ident)
                    mm.then_inc(m["min_ps"], 1)
                    pe.wait_ge(m["pt_sb"], i * 2 + d + 1)
                    if d == 0:
                        pe.wait_ge(m["u_sb"], i + 1)
                    else:
                        pe.wait_ge(m["k_sb"], i * 2 + 1)
                    lo = (0, 1)[d]
                    for q in range(PQ):
                        for c in range(2):
                            mm = pe.matmul(X[1][0:SI, q * 256:(q + 1) * 256], Bq[:, c, q], PT[:, c, q, :, lo:lo + L, :],
                                           start=(c == 0), stop=(c == 1), skip_group_check=True)
                    mm.then_inc(m["k_ps"], 1)
                    pe.wait_ge(m["min_sb"], i * 2 + d + 1)
                    if d == 0:
                        pe.wait_ge(m["ur_sb"], i + 1)
                    src = (U, Ur)[d]
                    for c in range(2):
                        for g in range(G8):
                            r = slice(64 * (g % 2), 64 * (g % 2) + 64)
                            mm = pe.matmul(X[2][r, c * NW + (g // 2) * P:c * NW + (g // 2 + 1) * P], Min[:, c, g // 2, r], src[:, g],
                                           start=True, stop=True, skip_group_check=True)
                    mm.then_inc(m["v_ps"], 1)
                    pe.wait_ge(m["pad_sb"], i * 2 + d + 1)
                    out = (X[3], X[0])[d]
                    first = (1, 0)[d]
                    for q in range(PQ):
                        for c in range(2):
                            mm = pe.matmul(out[:, q * 256:(q + 1) * 256], pad[:, c, q, 0:NCH], PT[:, c, q, :, first:first + L, :],
                                           start=(c == 0 and q % 2 == 0), stop=(d == 1 and c == 1), skip_group_check=True)
                    if d == 1:
                        mm.then_inc(m["yb_ps"], 1)
                    else:
                        mm.then_inc(m["y_ps"], 1)
                pe.wait_ge(m["t_ready"], i + 1)
                pe.wait_ge(m["yb_sb"], i + 1)
                for g in range(G8):
                    pe.matmul(X[3][:, g * P:(g + 1) * P], U[:, g], T[:, g], start=False, stop=False, skip_group_check=True)
                for c in range(2):
                    mm = pe.matmul(X[3][:, c * NW:(c + 1) * NW], flip, Yb[:, c * NW:(c + 1) * NW], start=False, stop=True, skip_group_check=True)
                mm.then_inc(m["y_ps"], 1)
                pe.wait_ge(m["yg_sb"], i + 1)
                for j in range(L):
                    mm = pe.matmul(X[0][:, j * P:(j + 1) * P], Yg[:, j, :, :].rearrange("p g o -> p (g o)"), ident, start=True, stop=True, skip_group_check=True)
                mm.then_inc(m["yt_ps"], 1)

        @block.scalar
        def _(act):
            with act.Fori(0, Q) as i:
                act.wait_ge(m["s2_ps"], i + 1)
                for g in range(G8):
                    ins = act.copy(S2[:, g], X[0][:, :].rearrange("p (l g i) -> p g l i", l=L, i=SI)[:, g])
                ins.then_inc(m["s2_sb"], 1)
                act.wait_ge(m["u_ps"], i + 1)
                act.copy(U[:, :, :].rearrange("p g c -> p (g c)"), X[1][:]).then_inc(m["u_sb"], 1)
                act.copy(Ur[:, :, :].rearrange("p g c -> p (g c)"), X[2][:]).then_inc(m["ur_sb"], 1)
                for d in range(2):
                    act.wait_ge(m["min_ps"], i * 2 + d + 1)
                    act.copy(Min[:, :, :, :].rearrange("p c q x -> p (c q x)"), X[0][:]).then_inc(m["min_sb"], 1)
                    act.wait_ge(m["k_ps"], i * 2 + d + 1)
                    act.wait_ge(m["t_in"], (i * 2 + d) * (16 * L))
                    act.copy(Kt[:, :, :, :, :].rearrange("i q g l o -> i (q g l o)"), X[1][0:SI]).then_inc(m["k_sb"], 1)
                act.wait_ge(m["yb_ps"], i + 1)
                act.copy(Yb[:], X[0][:]).then_inc(m["yb_sb"], 1)
                act.wait_ge(m["y_ps"], i * 2 + 2)
                for j in range(L):
                    ins = act.activation(Yg[:, j], X[3][:, :].rearrange("p (g j o) -> p j g o", j=L, o=SI)[:, j], ACT.Gelu_apprx_tanh)
                ins.then_inc(m["yg_sb"], 1)
                act.wait_ge(m["yt_ps"], i + 1)
                dst = yT[:, bass.ds(i, 1), :].rearrange("p a (c j) -> p (a c) j", j=L)
                act.copy(dst, X[0][:, :].rearrange("p (j c) -> p c j", j=L)).then_inc(m["q_done"], 1)

        @block.vector
        def _(dve):
            N = 100
            dve.wait_ge(m["d_in"], 16 * L)
            dve.wait_ge(m["zeroed"], 1)
            with dve.Fori(0, Q) as i:
                st = Steps(dve, m["chain"], at=i * N)
                op = lambda o, a, b, f: st(dve.tensor_tensor(o, a, b, f))
                for d in range(2):
                    at = d * GP + i * PQ
                    if d:
                        dve.wait_ge(m["k_ps"], i * 2 + 1)
                    for c in range(2):
                        st(dve.tensor_copy(Bq[:, c], bbar[:, c, bass.ds(at, PQ)]))
                    pw = lambda c, n: powers[:, c, n, bass.ds(at, PQ)]
                    b4 = lambda c: Bq[:, c]
                    if d:
                        dve.wait_ge(m["min_ps"], i * 2 + 1)
                    for l in range(L):
                        n = (L - 1 - l) if d == 0 else l
                        wide = lambda c: pw(c, n).unsqueeze(2).broadcast_to([P, PQ, SI])
                        t1, t2 = pt1[:, :, l], pt2[:, :, l]
                        dve.tensor_tensor(t1, b4(0), wide(0), ALU.mult)
                        ins = dve.tensor_tensor(t2, b4(1), wide(1), ALU.mult)
                    st(ins)
                    op(A[:, 0], pt1[:, :, 0:L], pt2[:, :, 0:L], ALU.subtract)
                    for l in range(L):
                        n = (L - 1 - l) if d == 0 else l
                        wide = lambda c: pw(c, n).unsqueeze(2).broadcast_to([P, PQ, SI])
                        dve.tensor_tensor(pt1[:, :, l], b4(0), wide(1), ALU.mult)
                        ins = dve.tensor_tensor(pt2[:, :, l], b4(1), wide(0), ALU.mult)
                    st(ins)
                    dve.tensor_tensor(A[:, 1], pt1[:, :, 0:L], pt2[:, :, 0:L], ALU.add).then_inc(m["a_sb"], 1)
                    dve.wait_ge(m["a_sb"], i * 2 + d + 1)
                    c4 = lambda c: ct[:, c, bass.ds(at, PQ)]
                    if d:
                        dve.wait_ge(m["y_ps"], i * 2 + 1)
                    for part in range(2):
                        for n in range(L + 1):
                            l = n if d == 0 else L - n
                            wide = lambda c: pw(c, n).unsqueeze(2).broadcast_to([P, PQ, SI])
                            dve.tensor_tensor(pt1[:, :, l], c4(0), wide(part), ALU.mult)
                            ins = dve.tensor_tensor(pt2[:, :, l], c4(1), wide(1 - part), ALU.mult)
                        st(ins)
                        for g in range(2):
                            r = slice(64 * g, 64 * g + 64)
                            if part == 0:
                                ins = dve.tensor_tensor(PT[r, 0, :, g], pt1[r], pt2[r], ALU.subtract)
                                st(ins)
                            else:
                                ins = dve.scalar_tensor_tensor(out=PT[r, 1, :, g], in0=pt1[r], scalar=-1.0, in1=pt2[r],
                                                               op0=ALU.mult, op1=ALU.subtract)
                                if g == 0:
                                    st(ins)
                    ins.then_inc(m["pt_sb"], 1)
                    for c in range(PQ):
                        st(dve.tensor_copy(R[:, c, 1:], r8[:, bass.ds(at + c, 1)].broadcast_to([P, NCH - 1])))
                    st(dve.memset(R[:, :, 0:1], 0.0))
                    dve.wait_ge(m["v_ps"], i * 2 + d + 1)
                    wv = lambda c: wt[:, c, bass.ds(at, PQ)]
                    V = lambda c: X[2][:, c * NW:(c + 1) * NW].rearrange("p (q n) -> p q n", q=PQ)
                    t1 = pt1[:, :, :, :].rearrange("p q l i -> p q (l i)")[:, :, 0:NCH]
                    t2 = pt2[:, :, :, :].rearrange("p q l i -> p q (l i)")[:, :, 0:NCH]
                    complex_product(op, (z[:, 0], z[:, 1]), (V(0), V(1)), (wv(0), wv(1)), t1, t2, conj_b=True)
                    for c in range(2):
                        fl = lambda y: y.rearrange("p q n -> p (q n)")
                        st(dve.tensor_tensor_scan(fl(z[:, c]), fl(R[:, :, :]), fl(z[:, c]), 0.0, ALU.mult, ALU.add))
                    complex_product(op, (pad[:, 0, :, 1:], pad[:, 1, :, 1:]), (z[:, 0], z[:, 1]), (wv(0), wv(1)), t1, t2)
                    dve.sem_inc(m["pad_sb"], 1)
                dve.wait_ge(m["t_in"], i * (32 * L) + 32 * L)
                dve.wait_ge(m["y_ps"], i * 2 + 1)
                op(T[:], Tf[:], Tb[:], ALU.add)
                for g in range(G8):
                    ins = dve.scalar_tensor_tensor(out=T[:, g], in0=ident, scalar=dcol[:, bass.ds(i * G8 + g, 1)], in1=T[:, g],
                                                   op0=ALU.mult, op1=ALU.add)
                ins.then_inc(m["t_ready"], 1)
                dve.wait_ge(m["t_ready"], i + 1)
                dve.wait_ge(m["q_done"], i + 1)
                assert st.n <= N, st.n
                dve.sem_inc(m["chain"], N - st.n)


def stage_glu(nc, I, yT, oT):
    rows = lambda x: x.rearrange("(k p) n -> p k n", p=P)
    with ExitStack() as a:
        bcol = a.enter_context(nc.sbuf_tensor("glu_b", [P, 4], F32))
        stage_load(nc, "glub", [(bcol[:], I["ssm_glu_b_2"][0].rearrange("(k p) -> p k", p=P))])

        def gate(act, m, j, acc, tmp):
            return act.activation(tmp[:, j], acc[0], ACT.Sigmoid, bias=bcol[:, bass.ds(m, 1)])

        def times(dve, m, j, acc, tmp, st):
            return dve.tensor_tensor(tile_of(oT, m), tile_of(yT, m), tmp[:, j], ALU.mult)

        stage_linear(nc, "glu", [[(rows(I["ssm_glu_w_2"][0]), yT)]], 4, gate, times, scratch=[P, 2, SEQ])


def stage_copy(nc, name, pairs):
    stage_load(nc, name, pairs)


def stage_mixer(nc, I, K, M, hT, uT):
    ident, ones = M["ident"], M["ones"]
    W = lambda n: I[n + "_2"][0]
    rows = lambda x: x.rearrange("(k p) n -> p k n", p=P)
    ND = 2 * GP
    shift_dram = nc.dram_tensor("bias_shifted", [GRID, 8 * (2 * NAH - 1), GRID], F32, kind="Internal").ap()
    h_keep = nc.dram_tensor("h_keep", [P, KT, SEQ], F32, kind="Internal").ap()
    with ExitStack() as a:
        ssmT = a.enter_context(nc.sbuf_tensor("ssmT", [P, 4, SEQ], F32))
        stage_rms_features(nc, "rms2", hT, W("mix_norm"), ones, uT)
        stage_copy(nc, "hkeep", [(h_keep, hT[:])])
        with ExitStack() as b:
            def bb(name, shape):
                return b.enter_context(nc.sbuf_tensor(name, shape, F32))
            yS = bb("yS", [P, 4, SEQ])
            with ExitStack() as c:
                def cb(name, shape):
                    return c.enter_context(nc.sbuf_tensor(name, shape, F32))
                powers, w8, r8 = cb("powers", [P, 2, L + 1, ND]), cb("w8", [P, 2, ND]), cb("r8", [P, ND])
                bbar, ct = cb("bbar", [P, 2, ND, SI]), cb("ct", [P, 2, ND, SI])
                wt = hT[:, :, :].rearrange("p k t -> p (k t)").rearrange("p (c n t) -> p c n t", c=2, t=NCH)
                stage_ssm_parameters(nc, I, ident, powers, w8, r8[:], bbar, ct)
                stage_phasors(nc, w8, wt)
                stage_ssm(nc, I, M, uT, powers, r8, bbar, ct, wt, yS)
            stage_glu(nc, I, yS, ssmT)
        stage_copy(nc, "hback", [(hT[:], h_keep)])
        naT = a.enter_context(nc.sbuf_tensor("naT", [P, 4, SEQ], F32))
        stage_bias_rows(nc, I, shift_dram)
        stage_neighbourhood(nc, I, K, ident, uT, naT, shift_dram)
        mT = a.enter_context(nc.sbuf_tensor("mT", [P, KT, SEQ], F32))

        def gates(act, m, j, acc, tmp):
            act.activation(tmp[:, 0], acc[0], ACT.Sigmoid)
            return act.activation(tmp[:, 1], acc[1], ACT.Sigmoid)

        def blend(dve, m, j, acc, tmp, st):
            st(dve.tensor_tensor(tmp[:, 0], tmp[:, 0], acc[2], ALU.mult))
            st(dve.tensor_tensor(tmp[:, 1], tmp[:, 1], acc[3], ALU.mult))
            return dve.tensor_tensor(tile_of(mT, m), tmp[:, 0], tmp[:, 1], ALU.add)

        wi = rows(W("w_in"))
        stage_linear(nc, "blend", [[(wi[:, :, 2048:3072], uT)], [(wi[:, :, 3072:4096], uT)], [(rows(W("w_attn_out")), naT)],
                                   [(rows(W("w_ssm_out")), ssmT)]], KT, gates, blend, steps=2, bufs=1, scratch=[P, 2, SEQ])

        def add(dve, m, j, acc, tmp, st):
            return dve.tensor_tensor(tile_of(hT, m), tile_of(hT, m), acc[0], ALU.add)

        stage_linear(nc, "mixout2", [[(rows(W("w_out")), mT)]], KT, None, add)


def shape_constants():
    import numpy as np

    j, i = np.meshgrid(np.arange(P), np.arange(P), indexing="ij")
    same = j // 64 == i // 64
    sq = {
        "ident": i == j,
        "cum": same & (j <= i),
        "strict": same & (j < i),
        "same": same,
        "before": j < i,
        "ones": i >= 0,
        "flip": i + j == P - 1,
    }
    for n in range(6):
        w = 1 << n
        sq[f"level{n}"] = (j // (2 * w) == i // (2 * w)) & (i // w % 2 == 1) & (j // w % 2 == 0)
    out = {"squares": np.stack([v.astype(np.float32) for v in sq.values()], 1)}
    inv = np.power(np.float32(10000.0), -np.arange(0, ROPE, 2, dtype=np.float32) / np.float32(ROPE)).astype(np.float32)
    ang = np.arange(SEQ, dtype=np.float32)[:, None] * inv[None, :]
    out["rope"] = np.stack([np.cos(ang), np.sin(ang)], 1).astype(np.float32).reshape(TT, P, 2, 16).transpose(1, 0, 2, 3).copy()
    rc = np.zeros((P, 2, PADW), np.float32)
    for g in range(4):
        r = slice(64 * (g % 2), 64 * (g % 2) + 64)
        rc[r, g // 2] = 1.0 / np.minimum(np.arange(PADW) + 1, 2 << g)
    out["pool_rc"] = rc
    kc, c = np.arange(GRID)[None, :], np.arange(GRID)[:, None]
    start = np.clip(c - NAW // 2, 0, GRID - NAW)
    m = np.where((kc >= start) & (kc < start + NAW), np.float32(0), np.float32(MASKED)).astype(np.float32)
    m = np.repeat(np.concatenate([m, m])[:, None], SLOTS, 1)
    m[:64, SLOTS - 1] = MASKED
    m[64:, EDGE] = MASKED
    out["na_mask"] = m
    out["iota"] = np.tile(np.arange(64, dtype=np.float32), (P, 1))
    out["bstart"] = (P * np.arange(BLOCKS, dtype=np.float32))[None]
    out["tokens"] = np.arange(SEQ, dtype=np.int32).reshape(TT, P).T.copy()
    return out, {k: n for n, k in enumerate(sq)}


def first_block(nc, I, K, M, sq, v, yT):
    with ExitStack() as ctx, nc.allow_non_contiguous_dma(reason="short columns of parameters"):
        def sb(name, shape, dt=F32):
            return ctx.enter_context(nc.sbuf_tensor(name, shape, dt))

        y_dram = nc.dram_tensor("y_rows", [BLOCKS * P, D], F32, kind="Internal").ap()
        ident = M["ident"]
        mod = sb("mod", [P, 6 * D])
        stage_modulation(nc, I, mod)
        nmean, ss = sb("nmean", [P, TT]), sb("ss", [P, TT])
        with ExitStack() as first:
            def fb(name, shape, dt=F32):
                return first.enter_context(nc.sbuf_tensor(name, shape, dt))
            lat, zab, gqkv = fb("lat", [P, TT, LAT]), fb("zab", [P, TT, ZAB]), fb("gqkv", [P, TT, 3 * GW])
            mcol = fb("mcol", [P, 2 * KT])
            stage_columns(nc, "modcol", [(mod[0:1, 0:D], 0), (mod[0:1, D:2 * D], 1)], M["ones"], mcol)
            hT = v
            with ExitStack() as b:
                x = b.enter_context(nc.sbuf_tensor("x", [P, TT, D], F32))
                stage_load(nc, "x", [(x[:], I["x"][0].rearrange("(t p) d -> p t d", p=P))])
                stage_features(nc, "h", x, hT, ident, scale=mcol[:, KT:], bias=mcol[:, 0:KT])
            stage_projections(nc, I, hT, ident, K, lat, zab, gqkv, yT)
            with ExitStack() as a:
                def ab(name, shape):
                    return a.enter_context(nc.sbuf_tensor(name, shape, F32))
                g, beta, gc, egc, kdf = (ab(n, [P, TT, GH]) for n in ("g", "beta", "gc", "egc", "kdf"))
                rs, o_tok, yg = ab("rs", [P, TT * 2 * GH]), ab("o_tok", [P, TT, GW]), ab("yg", [P, TT, GW])
                stage_delta_gates(nc, I, zab, gqkv, M, g, beta, gc, egc, kdf, rs)
                stage_delta_rule(nc, gqkv, M, [M[f"level{n}"] for n in range(6)], g, beta, gc, egc, kdf, rs, o_tok)
                stage_delta_out(nc, I, o_tok, zab, yg)
                stage_features(nc, "yg", yg, yT[:, 4:6], ident)
            with ExitStack() as a:
                def ab(name, shape):
                    return a.enter_context(nc.sbuf_tensor(name, shape, F32))
                rope, kr = ab("rope", [P, TT, 2, HR]), ab("kr", [P, TT, ROPE])
                cT, gains, y_tok = ab("cT", [P, 3, SEQ]), ab("gains", [P, 3]), v[:, :, 0:HEADS * VD]
                stage_load(nc, "rope", [(rope[:], K["rope"]),
                                        (gains[:, 0:2], I["mla_q_norm"][0].rearrange("(k p) -> p k", p=P)),
                                        (gains[:, 2:3], I["mla_kv_norm"][0].rearrange("(k p) -> p k", p=P))])
                stage_latent_norms(nc, lat, rope, kr)
                stage_features(nc, "cT", lat[:, :, 0:3 * P], cT, ident, scale=gains)
                stage_latent_attention(nc, I, cT, rope, kr, ident, y_tok, y_dram,
                                       sq[:, :, :].rearrange("p n c -> p (n c)")[:, 0:D])
                stage_features(nc, "ymla", y_tok, yT, ident)
            stage_mix_out(nc, I, yT, mod[:, 2 * D:3 * D], v, nmean, ss)
        h_dram = nc.dram_tensor("h_rows", [SEQ, D], F32, kind="Internal").ap()
        idx_dram = nc.dram_tensor("place_tokens", [BLOCKS * P, 1], I32, kind="Internal").ap()
        wts, dest, be = sb("wts", [P, 2 * TT]), sb("dest", [P, 2 * TT], I32), sb("be", [1, BLOCKS + 1], I32)
        with ExitStack() as a:
            h2 = a.enter_context(nc.sbuf_tensor("h2", [P, TT, D], F32))
            h2T = yT
            stage_layer_norm(nc, "ln1", I["ln1_g"], I["ln1_b"], v, nmean, ss, factor=mod[:, 4 * D:5 * D], shift=mod[:, 3 * D:4 * D],
                             h=h2, stores=[(h_dram.rearrange("(t p) d -> t p d", p=P), h2)])
            stage_features(nc, "h2T", h2, h2T, ident, spread=True)
            stage_route(nc, I, K, M, h2T, wts, dest, be, idx_dram)
        stage_experts(nc, I, M, h_dram, idx_dram, be, y_dram)
        stage_combine(nc, y_dram, dest, wts, mod[:, 5 * D:6 * D], v, nmean, ss)
        stage_layer_norm(nc, "ln2", I["ln2_g"], I["ln2_b"], v, nmean, ss)


def second_block(nc, I, K, M, hT, out):
    ident, ones = M["ident"], M["ones"]
    W = lambda n: I[n + "_2"][0]
    with ExitStack() as a:
        def ab(name, shape, dt=F32):
            return a.enter_context(nc.sbuf_tensor(name, shape, dt))
        uT = ab("uT", [P, KT, SEQ])
        with ExitStack() as b:
            aT = b.enter_context(nc.sbuf_tensor("aT", [P, FT, SEQ], F32))
            stage_rms_features(nc, "rms1", hT, W("ffn1_norm"), ones, uT)
            stage_ffn(nc, "ffn1", W("ffn1_w_gate"), W("ffn1_w_up"), W("ffn1_w_down"), uT, aT, hT)
        stage_mixer(nc, I, K, M, hT, uT)
        with ExitStack() as b:
            aT = b.enter_context(nc.sbuf_tensor("aT2", [P, FT, SEQ], F32))
            stage_rms_features(nc, "rms3", hT, W("ffn2_norm"), ones, uT)
            stage_ffn(nc, "ffn2", W("ffn2_w_gate"), W("ffn2_w_up"), W("ffn2_w_down"), uT, aT, hT)
        with ExitStack() as b:
            p_tok = b.enter_context(nc.sbuf_tensor("p_tok", [P, TT, PLE], F32))
            pT = b.enter_context(nc.sbuf_tensor("pT", [P, PLE // P, SEQ], F32))
            stage_load(nc, "ple", [(p_tok[:], I["p_2"][0, 0].rearrange("(t p) d -> p t d", p=P))])
            stage_features(nc, "pT", p_tok, pT, ident)
            stage_rms_features(nc, "rms4", hT, W("ple_norm"), ones, uT)
            rows = lambda x: x.rearrange("(k p) n -> p k n", p=P)

            def gate(act, m, j, acc, tmp):
                return act.activation(tmp[:, j], acc[0], ACT.Sigmoid)

            def add(dve, m, j, acc, tmp, st):
                st(dve.tensor_tensor(tmp[:, j], tmp[:, j], acc[1], ALU.mult))
                return dve.tensor_tensor(tile_of(hT, m), tile_of(hT, m), tmp[:, j], ALU.add)

            stage_linear(nc, "ple", [[(rows(W("ple_w_gate")), uT)], [(rows(W("ple_w_proj")), pT)]], KT, gate, add,
                         steps=1, scratch=[P, 2, SEQ])
        stage_rms_features(nc, "rms5", hT, I["final_norm_2"], ones, uT)
        stage_store(nc, uT, ident, out)


def build(nc, I, K, sq_at, out):
    with ExitStack() as ctx, nc.allow_non_contiguous_dma(reason="short columns of parameters"):
        sq = ctx.enter_context(nc.sbuf_tensor("squares", [P, len(sq_at), P], F32))
        M = {k: sq[:, n] for k, n in sq_at.items()}
        stage_load(nc, "consts", [(sq[:], K["squares"])])
        hT = ctx.enter_context(nc.sbuf_tensor("hT", [P, KT, SEQ], F32))
        with ExitStack() as b:
            v = b.enter_context(nc.sbuf_tensor("v", [P, TT, D], F32))
            first_block(nc, I, K, M, sq, v, hT)
            stage_features(nc, "hT", v, hT, M["ident"])
        second_block(nc, I, K, M, hT, out)


_OUTS = [((1, 1024, 1024), 'float32')]


def kernel(**inputs):
    import numpy as _np
    import concourse.bacc as _bacc
    from concourse import mybir as _mybir
    from concourse.bass_utils import run_bass_kernel_spmd as _run

    nc = _bacc.Bacc("TRN2", target_bir_lowering=False, num_devices=1)
    arrays, tensors = {}, {}
    for name, value in inputs.items():
        a = _np.ascontiguousarray(value)
        arrays[f"in_{name}_dram"] = a
        tensors[name] = nc.dram_tensor(f"in_{name}_dram", a.shape, _mybir.dt.from_np(a.dtype), kind="ExternalInput").ap()
    (shape, dtype), = _OUTS
    out = nc.dram_tensor("out_0_dram", shape, _mybir.dt.from_np(_np.dtype(dtype)), kind="ExternalOutput").ap()
    tables, squares = shape_constants()
    K = {}
    for name, a in tables.items():
        arrays[f"table_{name}_dram"] = a
        K[name] = nc.dram_tensor(f"table_{name}_dram", a.shape, _mybir.dt.from_np(a.dtype), kind="ExternalInput").ap()
    build(nc, tensors, K, squares, out)
    r = _run(nc, [arrays], core_ids=[0])
    return r.results[0]["out_0_dram"]
```

```python
import math
from contextlib import ExitStack
import concourse.bass as bass
from concourse import mybir

P = 128
F32 = mybir.dt.float32
F32R = mybir.dt.float32r
I32 = mybir.dt.int32
U32 = mybir.dt.uint32
ALU = mybir.AluOpType
ACT = mybir.ActivationFunctionType
AX = mybir.AxisListType.X

SEQ, D = 1024, 1024
TT = SEQ // P
KT = D // P
NW = 512


class Steps:

    def __init__(self, eng, sem, at=0):
        self.eng, self.sem, self.at, self.n = eng, sem, at, 0

    def __call__(self, ins):
        self.n += 1
        ins.then_inc(self.sem, 1)
        self.eng.wait_ge(self.sem, self.at + self.n)


def in_both_types(nc, ctx, name, shape):
    at = -(-nc.sbuf_base // 32) * 32
    t = ctx.enter_context(nc.sbuf_tensor(name, shape, F32))
    assert nc.sbuf_base == at + 4 * math.prod(shape[1:])
    return t, nc.alloc_sbuf_tensor_at(name + "_halves", shape, F32R, offset=at)


class Stage:

    def __init__(self, nc, name):
        self.nc, self.name, self.ctx, self.sems = nc, name, ExitStack(), []

    def __enter__(self):
        return self

    def __exit__(self, *what):
        self.ctx.close()
        self.nc.clear_and_free_semaphores(self.sems)
        self.nc.all_engine_barrier()

    def sb(self, name, shape, dt=F32):
        return self.ctx.enter_context(self.nc.sbuf_tensor(f"{self.name}_{name}", shape, dt))

    def both(self, name, shape):
        return in_both_types(self.nc, self.ctx, f"{self.name}_{name}", shape)

    def ps(self, name, shape, dt=F32):
        return self.ctx.enter_context(self.nc.psum_tensor(f"{self.name}_{name}", shape, dt))

    def sem(self, name):
        self.sems.append(self.nc.alloc_semaphore(f"{self.name}_{name}"))
        return self.sems[-1]


def stage_modulation(nc, I, mod, x):
    CH = 6 * D // NW
    SL = 4
    with Stage(nc, "mod") as s:
        ccol, cact = s.sb("ccol", [P, KT]), s.sb("cact", [P, KT])
        crep = s.sb("crep", [P, KT, P])
        ones = s.sb("ones", [1, P])
        bias = s.sb("bias", [1, 6 * D])
        w = s.sb("w", [P, SL, KT, NW])
        acc = s.ps("acc", [P, SL, NW])
        c_in, b_in, act_c, rep_c, ones_c = (s.sem(x) for x in ("c_in", "b_in", "act_c", "rep_c", "ones_c"))
        w_in = [s.sem(f"w_in{j}") for j in range(SL)]
        w_free, acc_ready, acc_free = s.sem("w_free"), s.sem("acc_ready"), s.sem("acc_free")
        wv = I["w_mod"][0].rearrange("(k p) n -> p k n", p=P)
        x_in = s.sem("x_in")
        block = s.ctx.enter_context(nc.Block())

        @block.sync
        def _(sp):
            sp.dma_start(ccol[:], I["c"][0].rearrange("(k p) -> p k", p=P)).then_inc(c_in, 16)
            sp.dma_start(bias[:], I["b_mod"]).then_inc(b_in, 16)
            with sp.Fori(0, CH // SL) as i:
                for j in range(SL):
                    sp.wait_ge(w_free, i * SL + j + 1)
                    sp.dma_start(w[:, j], wv[:, :, bass.ds(i * (SL * NW) + j * NW, NW)]).then_inc(w_in[j], 16)

        @block.scalar
        def _(act):
            act.dma_start(x[:], I["x"][0].rearrange("(t p) d -> p t d", p=P)).then_inc(x_in, 16)
            act.wait_ge(c_in, 16)
            act.activation(cact[:], ccol[:], ACT.Silu).then_inc(act_c, 1)
            act.wait_ge(x_in, 16)

        @block.gpsimd
        def _(pool):
            pool.memset(ones[:], 1.0).then_inc(ones_c, 1)
            pool.wait_ge(act_c, 1)
            pool.tensor_copy(crep[:], cact[:].unsqueeze(2).broadcast_to([P, KT, P])).then_inc(rep_c, 1)

        @block.tensor
        def _(pe):
            pe.sem_inc(w_free, SL)
            pe.wait_ge(rep_c, 1)
            pe.wait_ge(ones_c, 1)
            pe.wait_ge(b_in, 16)
            with pe.Fori(0, CH // SL) as i:
                for j in range(SL):
                    pe.wait_ge(acc_free, i * SL + j + 1)
                    pe.wait_ge(w_in[j], i * 16 + 16)
                    for k in range(KT):
                        mm = pe.matmul(acc[:, j], crep[:, k], w[:, j, k], start=(k == 0), stop=False)
                    mm.then_inc(w_free, 1)
                    pe.matmul(acc[:, j], ones[:], bias[:, bass.ds(i * (SL * NW) + j * NW, NW)],
                              start=False, stop=True).then_inc(acc_ready, 1)

        @block.vector
        def _(dve):
            dve.sem_inc(acc_free, SL)
            with dve.Fori(0, CH // SL) as i:
                for j in range(SL):
                    dve.wait_ge(acc_ready, i * SL + j + 1)
                    dve.tensor_copy(mod[:, bass.ds(i * (SL * NW) + j * NW, NW)], acc[:, j]).then_inc(acc_free, 1)


def stage_features(nc, name, src, dst, ident, scale=None, bias=None, spread=False):
    kt = src.shape[2] // P
    n = kt * 2
    with Stage(nc, name) as s:
        turned = s.ps("turned", [P, 4, NW])
        ready, free_a, free_d = s.sem("turned_ready"), s.sem("act_took"), s.sem("dve_took")
        block = s.ctx.enter_context(nc.Block())

        @block.tensor
        def _(pe):
            for g in range(n):
                k, half = g // 2, g % 2
                if g >= 4:
                    pe.wait_ge((free_a, free_d)[g % 2], (g - 4) // 2 + 1)
                for q in range(4):
                    mm = pe.transpose(turned[:, g % 4, q * P:(q + 1) * P],
                                      src[:, 4 * half + q].rearrange("p (c k) -> p k c", k=kt)[:, k] if spread
                                      else src[:, 4 * half + q, k * P:(k + 1) * P], ident)
                mm.then_inc(ready, 1)

        @block.scalar
        def _(act):
            for g in range(0, n, 2):
                act.wait_ge(ready, g + 1)
                k = g // 2
                act.activation(dst[:, k, 0:NW], turned[:, g % 4], ACT.Identity,
                               bias=0.0 if bias is None else bias[:, k:k + 1],
                               scale=1.0 if scale is None else scale[:, k:k + 1]).then_inc(free_a, 1)

        @block.vector
        def _(dve):
            for g in range(1, n, 2):
                dve.wait_ge(ready, g + 1)
                k = g // 2
                o, i = dst[:, k, NW:2 * NW], turned[:, g % 4]
                if scale is None:
                    ins = dve.tensor_copy(o, i)
                elif bias is None:
                    ins = dve.tensor_scalar(o, i, scale[:, k:k + 1], None, ALU.mult)
                else:
                    ins = dve.tensor_scalar(o, i, scale[:, k:k + 1], bias[:, k:k + 1], ALU.mult, ALU.add)
                ins.then_inc(free_d, 1)


def stage_load(nc, name, pairs):
    with Stage(nc, name) as s:
        loaded = s.sem("loaded")
        block = s.ctx.enter_context(nc.Block())

        @block.sync
        def _(sp):
            for dst, src in pairs:
                sp.dma_start(dst, src).then_inc(loaded, 16)
            sp.wait_ge(loaded, 16 * len(pairs))


def stage_columns(nc, name, rows, ones, cols):
    with Stage(nc, name) as s:
        n = sum(r.shape[1] // P for r, _ in rows)
        acc = s.ps("acc", [P, NW])
        turned, done = s.sem("turned"), s.sem("done")
        block = s.ctx.enter_context(nc.Block())

        @block.tensor
        def _(pe):
            c = 0
            for r, _ in rows:
                for k in range(r.shape[1] // P):
                    mm = pe.matmul(acc[:, c:c + 1], r[:, k * P:(k + 1) * P], ones[0:1, 0:1],
                                   start=True, stop=True, skip_group_check=True)
                    c += 1
            mm.then_inc(turned, 1)

        @block.vector
        def _(dve):
            dve.wait_ge(turned, 1)
            c = 0
            for r, one in rows:
                k = r.shape[1] // P
                dve.tensor_scalar(cols[:, c:c + k], acc[:, c:c + k], float(one), None, ALU.add).then_inc(done, 1)
                c += k


Q_RANK, KV_RANK, ROPE = 256, 128, 32
LAT = Q_RANK + KV_RANK + ROPE
GW = 256
GH, GD = 4, 64
CONV = 4
O_G, O_Z, O_P = LAT, LAT + 3 * GW, LAT + 4 * GW + 2 * GH
ZAB = GW + 2 * GH
PADW = 16


def stage_projections(nc, I, hT, ident, kc, lat, zab, gqkv, yT):
    NC = 8
    with Stage(nc, "proj") as s:
        wt = s.sb("w_tokens", [P, KT, LAT + ZAB])
        wf = s.sb("w_features", [P, 2, KT, P])
        cin = s.sb("conv_in", [P, PADW + SEQ])
        cout = s.sb("conv_out", [P, PADW + SEQ])
        cact = s.sb("conv_act", [P, SEQ])
        psum2 = s.sb("pool_sum", [P, PADW + SEQ])
        s_bufs = (cout, psum2)
        cw = s.sb("conv_w", [P, 6, CONV])
        pw = s.sb("pool_w", [P, 2, P])
        psc = s.sb("pool_scale", [P, 2])
        rc = s.sb("rc", [P, 2, PADW])
        tok = s.ps("tok", [P, 2, 2, NW])
        feat = s.ps("feat", [P, 2, NW])
        turn = s.ps("turn", [P, TT, P])
        wt_in, par_in, tok_ready, tok_free = s.sem("wt_in"), s.sem("par_in"), s.sem("tok_ready"), s.sem("tok_free")
        wf_in = [s.sem("wf_in0"), s.sem("wf_in1")]
        feat_ready, feat_free = s.sem("feat_ready"), s.sem("feat_free")
        conv_done, act_done, turn_ready, turn_free = s.sem("conv_done"), s.sem("act_done"), s.sem("turn_ready"), s.sem("turn_free")
        zeroed = s.sem("zeroed")
        cin_ready, dchain, delta_done, mix_ready, mix_free = s.sem("cin_ready"), s.sem("dchain"), s.sem("delta_done"), s.sem("mix_ready"), s.sem("mix_free")
        w = I["w_in"][0].rearrange("(k p) n -> p k n", p=P)
        block = s.ctx.enter_context(nc.Block())
        offs = [O_G + j * P for j in range(6)] + [O_P, O_P + P]

        @block.sync
        def _(sp):
            sp.dma_start(wt[:, :, 0:LAT], w[:, :, 0:LAT]).then_inc(wt_in, 16)
            sp.dma_start(wt[:, :, LAT:], w[:, :, O_Z:O_Z + ZAB]).then_inc(wt_in, 16)
            for i in range(CONV):
                sp.dma_start(cw[:, :, i], I["gdn_conv"][0, i].rearrange("(j p) -> p j", p=P)).then_inc(par_in, 16)
            sp.wait_ge(zeroed, 1)
            for g in range(2):
                r = slice(64 * g, 64 * g + 64)
                sp.dma_start(pw[r, :, r], I["pool_w"][0].rearrange("(j h) c d -> h c j d", h=2)[g]).then_inc(par_in, 16)
            sp.dma_start(psc[:], I["pool_scale"][0].rearrange("(j p) -> p j", p=P)).then_inc(par_in, 16)
            sp.dma_start(rc[:], kc["pool_rc"]).then_inc(par_in, 16)
            for j in range(NC):
                if j >= 2:
                    sp.wait_ge(feat_ready, j - 1)
                sp.dma_start(wf[:, j % 2], w[:, :, offs[j]:offs[j] + P]).then_inc(wf_in[j % 2], 16)

        @block.tensor
        def _(pe):
            def features(j):
                pe.wait_ge(wf_in[j % 2], 16 * (j // 2 + 1))
                if j:
                    pe.wait_ge(feat_free, j)
                for half in range(2):
                    for k in range(KT):
                        mm = pe.matmul(feat[:, half], wf[:, j % 2, k], hT[:, k, half * NW:(half + 1) * NW],
                                       start=(k == 0), stop=(k == KT - 1))
                mm.then_inc(feat_ready, 1)

            def turned(j):
                pe.wait_ge(act_done, j + 1)
                if j:
                    pe.wait_ge(turn_free, j)
                for t in range(TT):
                    mm = pe.transpose(turn[:, t], cact[:, t * P:(t + 1) * P], ident)
                mm.then_inc(turn_ready, 1)

            def tokens(t):
                if t == 0:
                    pe.wait_ge(wt_in, 32)
                if t >= 2:
                    pe.wait_ge(tok_free, t - 1)
                for c, (a, b) in enumerate(((0, LAT), (LAT, LAT + ZAB))):
                    for k in range(KT):
                        mm = pe.matmul(tok[:, t % 2, c, 0:b - a], hT[:, k, t * P:(t + 1) * P], wt[:, k, a:b],
                                       start=(k == 0), stop=(k == KT - 1))
                mm.then_inc(tok_ready, 1)

            def mix(j):
                pe.wait_ge(delta_done, j + 1)
                pe.wait_ge(par_in, 16 * (CONV + 4))
                if j:
                    pe.wait_ge(mix_free, j)
                else:
                    pe.wait_ge(turn_free, 6)
                for half in range(2):
                    mm = pe.matmul(turn[:, :, :].rearrange("p t c -> p (t c)")[:, half * NW:(half + 1) * NW],
                                   pw[:, j], cact[:, half * NW:(half + 1) * NW], start=True, stop=True)
                mm.then_inc(mix_ready, 1)

            for j in range(NC):
                features(j)
                tokens(j)
                if j < 6:
                    turned(j)
                else:
                    mix(j - 6)

        @block.scalar
        def _(act):
            def tokens(t):
                act.wait_ge(tok_ready, t + 1)
                act.copy(lat[:, t], tok[:, t % 2, 0, 0:LAT])
                act.copy(zab[:, t], tok[:, t % 2, 1, 0:ZAB]).then_inc(tok_free, 1)

            act.wait_ge(par_in, 16 * (CONV + 4))
            for j in range(NC):
                act.wait_ge(feat_ready, j + 1)
                if j:
                    act.wait_ge(conv_done, j)
                else:
                    act.wait_ge(cin_ready, 1)
                act.copy(cin[:, PADW:], feat[:, :, :].rearrange("p h c -> p (h c)")).then_inc(feat_free, 1)
                tokens(j)
                if j < 6:
                    act.wait_ge(conv_done, j + 1)
                    if j:
                        act.wait_ge(turn_ready, j)
                    act.activation(cact[:], cout[:, PADW:], ACT.Silu).then_inc(act_done, 1)
                    act.wait_ge(turn_ready, j + 1)
                    act.copy(gqkv[:, :, j * P:(j + 1) * P], turn[:]).then_inc(turn_free, 1)
                else:
                    act.wait_ge(mix_ready, j - 5)
                    act.activation(yT[:, j, :], turn[:, :, :].rearrange("p t c -> p (t c)"), ACT.Copy,
                                   scale=psc[:, j - 6:j - 5]).then_inc(mix_free, 1)

        @block.vector
        def _(dve):
            st = Steps(dve, dchain)
            dve.memset(pw[:], 0.0).then_inc(zeroed, 1)
            st(dve.memset(cout[:, 0:PADW], 0.0))
            dve.memset(cin[:, 0:PADW], 0.0).then_inc(cin_ready, 1)
            dve.wait_ge(par_in, 16 * (CONV + 4))
            for j in range(NC):
                dve.wait_ge(feat_free, j + 1)
                if j < 6:
                    if j:
                        dve.wait_ge(act_done, j)
                    st(dve.tensor_scalar(cout[:, PADW:], cin[:, PADW:], cw[:, j, CONV - 1:CONV], None, ALU.mult))
                    for i in range(CONV - 1):
                        a = PADW - (CONV - 1) + i
                        ins = dve.scalar_tensor_tensor(out=cout[:, PADW:], in0=cin[:, a:a + SEQ], scalar=cw[:, j, i:i + 1],
                                                       in1=cout[:, PADW:], op0=ALU.mult, op1=ALU.add)
                        if i < CONV - 2:
                            st(ins)
                    ins.then_inc(conv_done, 1)
                else:
                    jj = j - 6
                    if jj == 0:
                        dve.wait_ge(act_done, 6)
                        dve.wait_ge(turn_ready, 6)
                    else:
                        dve.wait_ge(mix_ready, 1)
                    lo, hi = slice(0, 64), slice(64, 128)
                    X, Y = cin, cout
                    plan = [(slice(0, 128), 1), (hi, 2)] if jj == 0 else [(slice(0, 128), 1), (slice(0, 128), 2), (slice(0, 128), 4), (hi, 8)]
                    bufs = s_bufs
                    cur = cin
                    for n, (r, sh) in enumerate(plan):
                        nxt = bufs[n % 2]
                        st(dve.memset(nxt[:, 0:PADW], 0.0))
                        st(dve.tensor_tensor(nxt[r, PADW:], cur[r, PADW:], cur[r, PADW - sh:PADW - sh + SEQ], ALU.add))
                        last = nxt
                        prev, cur = cur, nxt
                    for r, src in ((lo, prev), (hi, cur)):
                        g = 2 * jj + (0 if r is lo else 1)
                        win = 2 << g
                        st(dve.tensor_tensor(cact[r, 0:PADW], src[r, PADW:2 * PADW], rc[r, jj], ALU.mult))
                        st(dve.tensor_scalar(cact[r, PADW:], src[r, 2 * PADW:], 1.0 / win, None, ALU.mult))
                    dve.tensor_tensor(cact[:], cact[:], cin[:, PADW:], ALU.subtract).then_inc(delta_done, 1)
                    dve.wait_ge(delta_done, jj + 1)
                    dve.sem_inc(conv_done, 1)


def stage_delta_gates(nc, I, zab, gqkv, M, g, beta, gc, egc, kdf, rs):
    with Stage(nc, "gates") as s:
        alog, dtb, ea = s.sb("alog", [P, GH]), s.sb("dtb", [P, GH]), s.sb("ea", [P, GH])
        xa, nab, e, l = (s.sb(n, [P, TT, GH]) for n in ("xa", "nab", "e", "l"))
        sq = s.sb("sq", [P, TT, 2 * GW])
        diff = s.sb("diff", [P, TT, GH])
        ps = s.ps("sums", [P, 2, TT * GH])
        par_in, x_ready, act_done, g_ready, sums = (s.sem(n) for n in ("par_in", "x_ready", "act_done", "g_ready", "sums"))
        chain, ss_ready, root, diff_ready, achain = (s.sem(n) for n in ("chain", "ss_ready", "root", "diff_ready", "achain"))
        block = s.ctx.enter_context(nc.Block())
        flat = lambda x: x[:, :, :].rearrange("p t h -> p (t h)")

        @block.sync
        def _(sp):
            sp.dma_start(alog[:], I["gdn_a_log"].partition_broadcast(P).rearrange("p a h -> p (a h)")).then_inc(par_in, 16)
            sp.dma_start(dtb[:], I["gdn_dt_bias"].partition_broadcast(P).rearrange("p a h -> p (a h)")).then_inc(par_in, 16)

        @block.scalar
        def _(act):
            a = Steps(act, achain)
            act.activation(sq[:], gqkv[:, :, 0:2 * GW], ACT.Square).then_inc(act_done, 1)
            a(act.activation(beta[:], zab[:, :, GW + GH:], ACT.Sigmoid))
            act.wait_ge(par_in, 32)
            a(act.activation(ea[:], alog[:], ACT.Exp))
            act.wait_ge(x_ready, 1)
            a(act.activation(e[:], nab[:], ACT.Exp))
            act.activation(l[:], e[:], ACT.Ln, bias=1.0).then_inc(act_done, 1)
            act.wait_ge(sums, 1)
            act.activation(flat(egc), ps[:, 0], ACT.Exp).then_inc(act_done, 1)
            act.wait_ge(diff_ready, 1)
            act.activation(flat(kdf), flat(diff), ACT.Exp).then_inc(act_done, 1)
            act.wait_ge(ss_ready, 1)
            act.activation(rs[:], rs[:], ACT.Sqrt).then_inc(root, 1)

        @block.vector
        def _(dve):
            st = Steps(dve, chain)
            dve.wait_ge(par_in, 32)
            st(dve.tensor_tensor(xa[:], zab[:, :, GW:GW + GH], dtb[:].unsqueeze(1).broadcast_to([P, TT, GH]), ALU.add))
            dve.scalar_tensor_tensor(out=nab[:], in0=xa[:], scalar=-1.0, in1=xa[:], op0=ALU.mult, op1=ALU.min).then_inc(x_ready, 1)
            dve.wait_ge(act_done, 2)
            st(dve.scalar_tensor_tensor(out=l[:], in0=xa[:], scalar=0.0, in1=l[:], op0=ALU.max, op1=ALU.add))
            dve.scalar_tensor_tensor(out=g[:], in0=l[:], scalar=-1.0, in1=ea[:].unsqueeze(1).broadcast_to([P, TT, GH]),
                                     op0=ALU.mult, op1=ALU.mult).then_inc(g_ready, 1)
            st(dve.tensor_reduce(rs[:], sq[:, :, :].rearrange("p t (h d) -> p (t h) d", d=GD), AX, ALU.add))
            dve.tensor_scalar(rs[:], rs[:], 1e-6, None, ALU.add).then_inc(ss_ready, 1)
            dve.wait_ge(sums, 1)
            dve.wait_ge(act_done, 3)
            st(dve.tensor_copy(flat(gc), ps[:, 0]))
            dve.tensor_tensor(flat(diff), ps[:, 1], flat(gc), ALU.subtract).then_inc(diff_ready, 1)
            dve.wait_ge(root, 1)
            st(dve.reciprocal(rs[:], rs[:]))
            q = rs[:].rearrange("p (t a) -> p t a", a=2 * GH)[:, :, 0:GH]
            st(dve.tensor_scalar(q, q, GD ** -0.5, None, ALU.mult))

        @block.tensor
        def _(pe):
            pe.wait_ge(g_ready, 1)
            pe.matmul(ps[:, 0], M["cum"], flat(g), start=True, stop=True, skip_group_check=True)
            pe.matmul(ps[:, 1], M["same"], flat(g), start=False, stop=True, skip_group_check=True).then_inc(sums, 1)


def stage_delta_rule(nc, gqkv, M, lv, g, beta, gc, egc, kdf, rs, o_tok):
    W = GH * P
    with Stage(nc, "delta") as s:
        qk, bke, qd = s.sb("qk", [P, 2 * GH, GD]), *(s.sb(n, [P, GH, GD]) for n in ("bke", "qd"))
        bv = s.sb("bv", [P, GH + 1, GD])
        kd = s.sb("kd", [P, 2, GH, GD])
        rsb = s.sb("rsb", [P, 2 * GH])
        bg = s.sb("bg", [P, GH])
        grep, brep = s.sb("g_rep", [P, GH, P]), s.sb("beta_rep", [P, GH, P])
        kT, qT, qdT, wT = (s.sb(n, [P, GH, P]) for n in ("kT", "qT", "qdT", "wT"))
        dec, decI, AT, qkT, X, XT, T1 = (s.sb(n, [P, GH, P]) for n in ("dec", "decI", "AT", "qkT", "X", "XT", "T1"))
        LT = s.sb("LT", [P, 6, GH, P])
        u, vn, o1 = s.sb("u", [P, GH, GD]), s.sb("vn", [P, GH + 1, GD]), s.sb("o1", [P, GH, GD])
        gl = s.sb("gl", [GD, GH, 2])
        S = s.sb("S", [P, GH + 1, GD])
        bank = [s.ps(f"bank{n}", [P, GH, P]) for n in range(8)]
        names = ("staged kT_ps kT_sb rows_ps kk_ps dmin expd at_done t1_ps t1_sb t2_ps t2t_ps x_sb xt_sb masks uw_ps uw_sb gl_sb "
                 "ws_ps vn_sb so_ps s_sb o_sb tile_done prep_done init init_p").split()
        m = {n: s.sem(n) for n in names}
        chain, pchain = s.sem("chain"), s.sem("pchain")
        N_DVE = 30
        block = s.ctx.enter_context(nc.Block())
        bc = lambda x, shape: x.unsqueeze(1).broadcast_to(shape)
        full = [P, GH, P]

        @block.gpsimd
        def _(pool):
            for x in (kT, qT, qdT, wT):
                pool.memset(x[:], 0.0)
            for x in (vn, kd, bv):
                pool.memset(x[:], 0.0)
            pool.memset(S[:], 0.0).then_inc(m["init_p"], 1)
            with pool.Fori(0, TT) as i:
                pool.wait_ge(m["rows_ps"], i + 1)
                gi = g[:, bass.ds(i, 1), :].rearrange("p a h -> p (a h)").unsqueeze(2).broadcast_to(full)
                bi = beta[:, bass.ds(i, 1), :].rearrange("p a h -> p (a h)").unsqueeze(2).broadcast_to(full)
                pool.tensor_copy(grep[:], gi)
                pool.tensor_copy(brep[:], bi).then_inc(m["prep_done"], 1)
                pool.wait_ge(m["at_done"], i + 1)
                for n in range(6):
                    pool.tensor_tensor(LT[:, n], AT[:], bc(lv[n], full), ALU.mult).then_inc(m["masks"], 1)

        @block.tensor
        def _(pe):
            pe.sem_inc(m["rows_ps"], 1)
            pe.wait_ge(m["init_p"], 1)
            with pe.Fori(0, TT) as i:
                pe.wait_ge(m["prep_done"], i + 1)
                for h in range(GH):
                    pe.matmul(bank[3][:, h], grep[:, h], M["cum"], start=True, stop=True, skip_group_check=True)
                    mm = pe.matmul(bank[4][:, h], brep[:, h], M["ident"], start=True, stop=True, skip_group_check=True)
                mm.then_inc(m["rows_ps"], 1)
                pe.wait_ge(m["staged"], i + 1)
                for h in range(GH):
                    pe.matmul(bank[0][0:GD, h], qk[:, GH + h], M["ident"], start=True, stop=True, skip_group_check=True)
                    pe.matmul(bank[1][0:GD, h], qk[:, h], M["ident"], start=True, stop=True, skip_group_check=True)
                    mm = pe.matmul(bank[2][0:GD, h], qd[:, h], M["ident"], start=True, stop=True, skip_group_check=True)
                mm.then_inc(m["kT_ps"], 1)
                pe.wait_ge(m["kT_sb"], i + 1)
                for h in range(GH):
                    pe.matmul(bank[5][:, h], kT[:, h], kT[:, h], start=True, stop=True, skip_group_check=True)
                    mm = pe.matmul(bank[6][:, h], kT[:, h], qT[:, h], start=True, stop=True, skip_group_check=True)
                mm.then_inc(m["kk_ps"], 1)
                for n in range(6):
                    pe.wait_ge(m["masks"], i * 6 + n + 1)
                    if n:
                        pe.wait_ge(m["x_sb"], i * 6 + n)
                    for h in range(GH):
                        mm = pe.matmul(bank[0][:, h], LT[:, n, h], X[:, h] if n else M["ident"], start=True, stop=True, skip_group_check=True)
                    mm.then_inc(m["t1_ps"], 1)
                    if n:
                        pe.wait_ge(m["t1_sb"], i * 5 + n)
                        pe.wait_ge(m["xt_sb"], i * 6 + n)
                        for h in range(GH):
                            mm = pe.matmul(bank[1][:, h], XT[:, h], T1[:, h], start=True, stop=True, skip_group_check=True)
                        mm.then_inc(m["t2_ps"], 1)
                        for h in range(GH):
                            mm = pe.matmul(bank[2][:, h], T1[:, h], XT[:, h], start=True, stop=True, skip_group_check=True)
                        mm.then_inc(m["t2t_ps"], 1)
                pe.wait_ge(m["xt_sb"], i * 6 + 6)
                for h in range(GH):
                    pe.matmul(bank[3][:, h], XT[:, h], bv[:, h:h + 2, :].rearrange("p h d -> p (h d)"), start=True, stop=True, skip_group_check=True)
                    mm = pe.matmul(bank[4][0:GD, h], bke[:, h], XT[:, h], start=True, stop=True, skip_group_check=True)
                mm.then_inc(m["uw_ps"], 1)
                pe.wait_ge(m["uw_sb"], i + 1)
                for c in range(2):
                    r = slice(64 * c, 64 * c + 64)
                    pe.wait_ge(m["s_sb"], i * 2 + c + 1)
                    for h in range(GH):
                        pe.matmul(bank[5][:, h], wT[:, h], S[:, h:h + 2, :].rearrange("p h d -> p (h d)"), start=True, stop=True, skip_group_check=True)
                        mm = pe.matmul(bank[6][:, h], qdT[:, h], S[:, h:h + 2, :].rearrange("p h d -> p (h d)"), start=True, stop=True, skip_group_check=True)
                    mm.then_inc(m["ws_ps"], 1)
                    pe.wait_ge(m["vn_sb"], i * 2 + c + 1)
                    for h in range(GH):
                        pe.matmul(bank[0][:, h], qkT[:, h], vn[:, h:h + 2, :].rearrange("p h d -> p (h d)"), start=True, stop=True, skip_group_check=True)
                    for h in range(GH):
                        mm = pe.matmul(bank[7][0:GD, h], kd[:, c, h], vn[:, h:h + 2, :].rearrange("p h d -> p (h d)"), start=True, stop=True, skip_group_check=True)
                    mm.then_inc(m["so_ps"], 1)

        @block.scalar
        def _(act):
            with act.Fori(0, TT) as i:
                act.wait_ge(m["rows_ps"], i + 2)
                act.wait_ge(m["tile_done"], i + 1)
                act.activation(gl[:], bank[3][0:GD, :, :].rearrange("p h (c j) -> p h c j", c=2)[:, :, :, 63], ACT.Exp).then_inc(m["gl_sb"], 1)
                act.wait_ge(m["dmin"], i + 1)
                act.activation(dec[:], dec[:], ACT.Exp).then_inc(m["expd"], 1)
                act.wait_ge(m["kT_ps"], i + 1)
                act.copy(kT[0:GD], bank[0][0:GD])
                act.copy(qT[0:GD], bank[1][0:GD])
                act.copy(qdT[0:GD], bank[2][0:GD]).then_inc(m["kT_sb"], 1)
                for n in range(1, 6):
                    act.wait_ge(m["t1_ps"], i * 6 + n + 1)
                    act.copy(T1[:], bank[0][:]).then_inc(m["t1_sb"], 1)
                act.wait_ge(m["uw_ps"], i + 1)
                act.copy(wT[0:GD], bank[4][0:GD])
                act.copy(u[:], bank[3][:, :, 0:GD]).then_inc(m["uw_sb"], 1)

        @block.vector
        def _(dve):
            dve.wait_ge(m["init_p"], 1)
            dve.sem_inc(m["s_sb"], 1)
            dve.sem_inc(m["tile_done"], 1)
            with dve.Fori(0, TT) as i:
                st = Steps(dve, chain, at=i * N_DVE)
                row = lambda x: x[:, bass.ds(i, 1), :].rearrange("p a h -> p (a h)")
                wide = lambda x, n=GH: x.unsqueeze(2).broadcast_to([P, n, GD])
                src = gqkv[:, bass.ds(i, 1), :].rearrange("p a (h d) -> p (a h) d", d=GD)
                rsi = rs[:, bass.ds(i * (2 * GH), 2 * GH)]
                st(dve.tensor_tensor(qk[:], src[:, 0:2 * GH], wide(rsi, 2 * GH), ALU.mult))
                st(dve.tensor_tensor(bg[:], row(beta), row(egc), ALU.mult))
                dve.tensor_tensor(bv[:, 0:GH], src[:, 2 * GH:], wide(row(beta)), ALU.mult)
                dve.tensor_tensor(bke[:], qk[:, GH:], wide(bg[:]), ALU.mult)
                for c in range(2):
                    r = slice(64 * c, 64 * c + 64)
                    dve.tensor_tensor(kd[r, c], qk[r, GH:], wide(row(kdf))[r], ALU.mult)
                dve.tensor_tensor(qd[:], qk[:, 0:GH], wide(row(egc)), ALU.mult).then_inc(m["staged"], 1)
                dve.wait_ge(m["rows_ps"], i + 2)
                dve.wait_ge(m["gl_sb"], i + 1)
                for h in range(GH):
                    ins = dve.tensor_scalar(dec[:, h], bank[3][:, h], gc[:, bass.ds(i, 1), h], 0.0, ALU.subtract, ALU.min)
                ins.then_inc(m["dmin"], 1)
                dve.wait_ge(m["expd"], i + 1)
                st(dve.tensor_tensor(AT[:], dec[:], bc(M["strict"], full), ALU.mult))
                st(dve.tensor_tensor(AT[:], AT[:], bank[4][:], ALU.mult))
                dve.wait_ge(m["kk_ps"], i + 1)
                dve.tensor_tensor(AT[:], AT[:], bank[5][:], ALU.mult).then_inc(m["at_done"], 1)
                for n in range(6):
                    dve.wait_ge(m["masks"], i * 6 + n + 1)
                    if n == 0:
                        dve.wait_ge(m["t1_ps"], i * 6 + 1)
                        dve.tensor_tensor(X[:], bc(M["ident"], full), bank[0][:], ALU.subtract).then_inc(m["x_sb"], 1)
                        dve.tensor_tensor(XT[:], bc(M["ident"], full), LT[:, 0], ALU.subtract).then_inc(m["xt_sb"], 1)
                        st(dve.tensor_tensor(decI[:], dec[:], bc(M["cum"], full), ALU.mult))
                        dve.tensor_tensor(qkT[:], decI[:], bank[6][:], ALU.mult)
                    else:
                        dve.wait_ge(m["t2_ps"], i * 5 + n)
                        dve.tensor_tensor(X[:], X[:], bank[1][:], ALU.subtract).then_inc(m["x_sb"], 1)
                        dve.wait_ge(m["t2t_ps"], i * 5 + n)
                        dve.tensor_tensor(XT[:], XT[:], bank[2][:], ALU.subtract).then_inc(m["xt_sb"], 1)
                for c in range(2):
                    r = slice(64 * c, 64 * c + 64)
                    dve.wait_ge(m["ws_ps"], i * 2 + c + 1)
                    dve.wait_ge(m["uw_sb"], i + 1)
                    dve.tensor_tensor(vn[r, 0:GH], u[r], bank[5][r, :, 0:GD], ALU.subtract).then_inc(m["vn_sb"], 1)
                    dve.tensor_copy(o1[r], bank[6][r, :, 0:GD])
                    st(dve.tensor_tensor(S[0:GD, 0:GH], S[0:GD, 0:GH], gl[:, :, c].unsqueeze(2).broadcast_to([GD, GH, GD]), ALU.mult))
                    dve.wait_ge(m["so_ps"], i * 2 + c + 1)
                    dve.tensor_tensor(S[0:GD, 0:GH], S[0:GD, 0:GH], bank[7][0:GD, :, 0:GD], ALU.add).then_inc(m["s_sb"], 1)
                    ot = o_tok[r, bass.ds(i, 1), :].rearrange("p a (h d) -> p (a h) d", d=GD)
                    ins = dve.tensor_tensor(ot, o1[r], bank[0][r, :, 0:GD], ALU.add)
                ins.then_inc(m["tile_done"], 1)
                while st.n < N_DVE:
                    dve.sem_inc(chain, 1)
                    st.n += 1
                dve.wait_ge(m["tile_done"], i + 2)


def stage_delta_out(nc, I, o_tok, zab, yg):
    with Stage(nc, "dout") as s:
        sq, sz = s.sb("sq", [P, TT, GW]), s.sb("sz", [P, TT, GW])
        ss = s.sb("ss", [P, TT * GH])
        gain = s.sb("gain", [P, GD])
        gin, sq_ready, ss_ready, root, chain, silu = (s.sem(n) for n in ("gin", "sq_ready", "ss_ready", "root", "chain", "silu"))
        block = s.ctx.enter_context(nc.Block())
        hd = lambda x: x[:, :, :].rearrange("p t (h d) -> p (t h) d", d=GD)

        @block.sync
        def _(sp):
            sp.dma_start(gain[:], I["gdn_out_norm"].partition_broadcast(P).rearrange("p a h -> p (a h)")).then_inc(gin, 16)

        @block.scalar
        def _(act):
            act.activation(sq[:], o_tok[:], ACT.Square).then_inc(sq_ready, 1)
            act.activation(sz[:], zab[:, :, 0:GW], ACT.Silu).then_inc(silu, 1)
            act.wait_ge(ss_ready, 1)
            act.activation(ss[:], ss[:], ACT.Sqrt).then_inc(root, 1)

        @block.vector
        def _(dve):
            st = Steps(dve, chain)
            dve.wait_ge(sq_ready, 1)
            st(dve.tensor_reduce(ss[:], hd(sq), AX, ALU.add))
            dve.tensor_scalar(ss[:], ss[:], 1.0 / GD, 1e-6, ALU.mult, ALU.add).then_inc(ss_ready, 1)
            dve.wait_ge(root, 1)
            st(dve.reciprocal(ss[:], ss[:]))
            st(dve.tensor_tensor(hd(yg), hd(o_tok), ss[:].unsqueeze(2).broadcast_to([P, TT * GH, GD]), ALU.mult))
            dve.wait_ge(gin, 16)
            st(dve.tensor_tensor(hd(yg), hd(yg), gain[:].unsqueeze(1).broadcast_to([P, TT * GH, GD]), ALU.mult))
            dve.wait_ge(silu, 1)
            st(dve.tensor_tensor(yg[:], yg[:], sz[:], ALU.mult))


HEADS, NOPE, VD = 8, 64, 64
QKD = NOPE + ROPE
HR = ROPE // 2
MASKED = -1.0e30


def stage_latent_norms(nc, lat, rope, kr):
    with Stage(nc, "latent") as s:
        sq = s.sb("sq", [P, TT, Q_RANK + KV_RANK])
        ss = s.sb("ss", [P, 2, TT])
        t1, t2 = s.sb("t1", [P, TT, HR]), s.sb("t2", [P, TT, HR])
        sq_ready, ss_ready, root, chain = (s.sem(n) for n in ("sq_ready", "ss_ready", "root", "chain"))
        block = s.ctx.enter_context(nc.Block())

        @block.scalar
        def _(act):
            act.activation(sq[:], lat[:, :, 0:Q_RANK + KV_RANK], ACT.Square).then_inc(sq_ready, 1)
            act.wait_ge(ss_ready, 1)
            act.activation(ss[:], ss[:], ACT.Sqrt).then_inc(root, 1)

        @block.vector
        def _(dve):
            st = Steps(dve, chain)
            x1, x2 = lat[:, :, LAT - ROPE:LAT - HR], lat[:, :, LAT - HR:LAT]
            cos, sin = rope[:, :, 0], rope[:, :, 1]
            st(dve.tensor_tensor(t1[:], x1, cos, ALU.mult))
            st(dve.tensor_tensor(t2[:], x2, sin, ALU.mult))
            st(dve.tensor_tensor(kr[:, :, 0:HR], t1[:], t2[:], ALU.subtract))
            st(dve.tensor_tensor(t1[:], x2, cos, ALU.mult))
            st(dve.tensor_tensor(t2[:], x1, sin, ALU.mult))
            st(dve.tensor_tensor(kr[:, :, HR:], t1[:], t2[:], ALU.add))
            dve.wait_ge(sq_ready, 1)
            st(dve.tensor_reduce(ss[:, 0], sq[:, :, 0:Q_RANK], AX, ALU.add))
            st(dve.tensor_reduce(ss[:, 1], sq[:, :, Q_RANK:], AX, ALU.add))
            st(dve.tensor_scalar(ss[:, 0], ss[:, 0], 1.0 / Q_RANK, 1e-6, ALU.mult, ALU.add))
            dve.tensor_scalar(ss[:, 1], ss[:, 1], 1.0 / KV_RANK, 1e-6, ALU.mult, ALU.add).then_inc(ss_ready, 1)
            dve.wait_ge(root, 1)
            st(dve.reciprocal(ss[:], ss[:]))
            for a, b, n in ((0, Q_RANK, 0), (Q_RANK, Q_RANK + KV_RANK, 1)):
                st(dve.tensor_tensor(lat[:, :, a:b], lat[:, :, a:b], ss[:, n].unsqueeze(2).broadcast_to([P, TT, b - a]), ALU.mult))


def stage_latent_attention(nc, I, cT, rope, kr, ident, y_tok, y_dram, filler):
    scale = QKD ** -0.5
    with Stage(nc, "mla") as s:
        wq = s.sb("wq", [P, 2, HEADS * QKD])
        wkv = s.sb("wkv", [P, HEADS * (NOPE + VD)])
        qs, ks, vs = s.sb("q_tok", [P, TT, QKD]), s.sb("k_tok", [P, TT, QKD]), s.sb("v_tok", [P, TT, P])
        r1, r2 = s.sb("r1", [P, TT, HR]), s.sb("r2", [P, TT, HR])
        qT, kT = s.sb("qT", [QKD, SEQ]), s.sb("kT", [QKD, SEQ])
        pr, prT = s.sb("probs", [P, 2, SEQ]), s.sb("probsT", [P, 2, SEQ])
        mx, nm, rsum, rinv = (s.sb(n, [P, 2, 1]) for n in ("mx", "nm", "rsum", "rinv"))
        A = [s.ps(f"A{n}", [P, 2 * NW]) for n in range(4)]
        w_in, qkv_ps, kr_set, q_rot, qk_sb, turn_ps, turn_sb = (s.sem(n) for n in ("w_in", "qkv_ps", "kr_set", "q_rot", "qk_sb", "turn_ps", "turn_sb"))
        s_ps, nm_sb, p_sb, pT_ps, pT_a, pT_d, o_ps, y_sb, chain, achain = (s.sem(n) for n in (
            "s_ps", "nm_sb", "p_sb", "pT_ps", "pT_a", "pT_d", "o_ps", "y_sb", "chain", "achain"))
        filled = s.sem("filled")
        tiles = lambda x, w: x[:, :].rearrange("p (t c) -> p t c", t=TT)[:, :, 0:w]
        block = s.ctx.enter_context(nc.Block())

        @block.sync
        def _(sp):
            sp.dma_start(wq[:], I["mla_w_uq"][0].rearrange("(k p) n -> p k n", p=P)).then_inc(w_in, 16)
            sp.dma_start(wkv[:], I["mla_w_ukv"][0]).then_inc(w_in, 16)
            rows = y_dram.rearrange("(b p) d -> p b d", p=P)
            for b in range(0, BLOCKS, 8):
                sp.dma_start(rows[:, b:b + 8], filler.unsqueeze(1).broadcast_to([P, 8, D])).then_inc(filled, 16)
            sp.wait_ge(filled, 16 * (BLOCKS // 8))

        @block.gpsimd
        def _(pool):
            pool.tensor_copy(ks[:, :, NOPE:], kr[:]).then_inc(kr_set, 1)

        @block.tensor
        def _(pe):
            pe.wait_ge(w_in, 32)
            pe.wait_ge(kr_set, 1)
            with pe.Fori(0, HEADS) as h:
                pe.wait_ge(y_sb, h * TT + 1)
                for t in range(TT):
                    for k in range(2):
                        pe.matmul(tiles(A[0], P)[:, t, 0:QKD], cT[:, k, t * P:(t + 1) * P],
                                  wq[:, k, bass.ds(h * QKD, QKD)], start=(k == 0), stop=(k == 1), skip_group_check=True)
                    mm = pe.matmul(tiles(A[1], P)[:, t], cT[:, 2, t * P:(t + 1) * P], wkv[:, bass.ds(h * P, P)],
                                   start=True, stop=True, skip_group_check=True)
                mm.then_inc(qkv_ps, 1)
                pe.wait_ge(qk_sb, h + 1)
                pe.wait_ge(q_rot, h + 1)
                for t in range(TT):
                    pe.transpose(A[2][0:QKD, t * P:(t + 1) * P], qs[:, t], ident)
                    mm = pe.transpose(A[3][0:QKD, t * P:(t + 1) * P], ks[:, t], ident)
                mm.then_inc(turn_ps, 1)
                pe.wait_ge(turn_sb, h * 2 + 2)

                def scores(b):
                    if b >= 2:
                        pe.wait_ge(p_sb, h * TT + b - 1)
                    n = (b + 1) * P
                    for a in range(0, n, NW):
                        mm = pe.matmul(A[b % 2][:, a:min(a + NW, n)], qT[:, b * P:n], kT[:, a:min(a + NW, n)], start=True, stop=True)
                    mm.then_inc(s_ps, 1)

                scores(0)
                scores(1)
                for b in range(TT):
                    pe.wait_ge(p_sb, h * TT + b + 1)
                    if b:
                        pe.wait_ge(pT_a, h * TT + b)
                        pe.wait_ge(pT_d, h * TT + b)
                    for n in range(b + 1):
                        mm = pe.transpose(A[2][:, n * P:(n + 1) * P], pr[:, b % 2, n * P:(n + 1) * P], ident)
                    mm.then_inc(pT_ps, 1)
                    if b + 2 < TT:
                        scores(b + 2)
                    pe.wait_ge(pT_a, h * TT + b + 1)
                    pe.wait_ge(pT_d, h * TT + b + 1)
                    if b >= 2:
                        pe.wait_ge(y_sb, h * TT + b)
                    for n in range(b + 1):
                        mm = pe.matmul(A[3][:, (b % 2) * NW:(b % 2) * NW + P], prT[:, b % 2, n * P:(n + 1) * P], vs[:, n],
                                       start=(n == 0), stop=(n == b))
                    mm.then_inc(o_ps, 1)

        @block.scalar
        def _(act):
            with act.Fori(0, HEADS) as h:
                act.wait_ge(qkv_ps, h + 1)
                act.copy(ks[:, :, 0:NOPE], tiles(A[1], NOPE))
                act.copy(vs[:], A[1][:, :].rearrange("p (t c) -> p t c", t=TT))
                act.copy(qs[:, :, 0:NOPE], tiles(A[0], NOPE)).then_inc(qk_sb, 1)
                act.wait_ge(turn_ps, h + 1)
                act.copy(qT[:], A[2][0:QKD]).then_inc(turn_sb, 1)

                def exps(b):
                    n = (b + 1) * P
                    act.wait_ge(nm_sb, h * TT + b + 1)
                    act.activation(pr[:, b % 2, 0:n], A[b % 2][:, 0:n], ACT.Exp, bias=nm[:, b % 2], scale=scale,
                                   accum_out=rsum[:, b % 2]).then_inc(p_sb, 1)

                exps(0)
                for b in range(TT):
                    n = (b + 1) * P
                    if b + 1 < TT:
                        exps(b + 1)
                    act.wait_ge(pT_ps, h * TT + b + 1)
                    act.copy(prT[:, b % 2, 0:min(n, NW)], A[2][:, 0:min(n, NW)]).then_inc(pT_a, 1)

        @block.vector
        def _(dve):
            dve.sem_inc(y_sb, 1)
            N = 5 + 3 * TT
            with dve.Fori(0, HEADS) as h:
                st = Steps(dve, chain, at=h * N)
                dve.wait_ge(qkv_ps, h + 1)
                dve.wait_ge(qk_sb, h + 1)
                x1, x2 = tiles(A[0], P)[:, :, NOPE:NOPE + HR], tiles(A[0], P)[:, :, NOPE + HR:QKD]
                cos, sin = rope[:, :, 0], rope[:, :, 1]
                st(dve.tensor_tensor(r1[:], x1, cos, ALU.mult))
                st(dve.tensor_tensor(r2[:], x2, sin, ALU.mult))
                st(dve.tensor_tensor(qs[:, :, NOPE:NOPE + HR], r1[:], r2[:], ALU.subtract))
                st(dve.tensor_tensor(r1[:], x2, cos, ALU.mult))
                st(dve.tensor_tensor(r2[:], x1, sin, ALU.mult))
                dve.tensor_tensor(qs[:, :, NOPE + HR:], r1[:], r2[:], ALU.add).then_inc(q_rot, 1)
                dve.wait_ge(turn_ps, h + 1)
                dve.tensor_copy(kT[:], A[3][0:QKD]).then_inc(turn_sb, 1)

                def largest(b):
                    n = (b + 1) * P
                    dve.wait_ge(s_ps, h * TT + b + 1)
                    st(dve.memset(A[b % 2][0:64, n - 64:n], MASKED))
                    st(dve.reduce_max(mx[:, b % 2], A[b % 2][:, 0:n], AX))
                    dve.tensor_scalar(nm[:, b % 2], mx[:, b % 2], -scale, None, ALU.mult).then_inc(nm_sb, 1)

                largest(0)
                largest(1)
                for b in range(TT):
                    dve.wait_ge(p_sb, h * TT + b + 1)
                    st(dve.reciprocal(rinv[:, b % 2], rsum[:, b % 2]))
                    dve.wait_ge(pT_ps, h * TT + b + 1)
                    n = (b + 1) * P
                    if n > NW:
                        dve.tensor_copy(prT[:, b % 2, NW:n], A[2][:, NW:n]).then_inc(pT_d, 1)
                    else:
                        dve.sem_inc(pT_d, 1)
                    if b + 2 < TT:
                        largest(b + 2)
                    dve.wait_ge(o_ps, h * TT + b + 1)
                    dve.tensor_scalar(y_tok[:, b, bass.ds(h * VD, VD)], A[3][:, (b % 2) * NW + NOPE:(b % 2) * NW + P],
                                      rinv[:, b % 2], None, ALU.mult).then_inc(y_sb, 1)
                assert st.n == N, st.n


ALPHA = 2.0 ** 0.25
LN_EPS = 1e-5


def stage_mix_out(nc, I, yT, gate, v, nmean, ss):
    with Stage(nc, "mixout") as s:
        w = s.sb("w", [P, KT, D])
        tmp, junk = s.sb("tmp", [P, 2, D]), s.sb("junk", [P, D])
        sm = s.sb("sum", [P, TT])
        acc = s.ps("acc", [P, 2, D])
        w_in, x_in, acc_ready, acc_free, v_ready, sum_ready, mean_ready, chain, sq_done = (s.sem(n) for n in (
            "w_in", "x_in", "acc_ready", "acc_free", "v_ready", "sum_ready", "mean_ready", "chain", "sq_done"))
        block = s.ctx.enter_context(nc.Block())

        @block.sync
        def _(sp):
            sp.dma_start(w[:], I["w_out"][0].rearrange("(k p) n -> p k n", p=P)).then_inc(w_in, 16)
            sp.dma_start(v[:], I["x"][0].rearrange("(t p) d -> p t d", p=P)).then_inc(x_in, 16)

        @block.tensor
        def _(pe):
            pe.wait_ge(w_in, 16)
            for t in range(TT):
                if t >= 2:
                    pe.wait_ge(acc_free, t - 1)
                for c in range(2):
                    for k in range(KT):
                        mm = pe.matmul(acc[:, t % 2, c * NW:(c + 1) * NW], yT[:, k, t * P:(t + 1) * P],
                                       w[:, k, c * NW:(c + 1) * NW], start=(k == 0), stop=(k == KT - 1))
                mm.then_inc(acc_ready, 1)

        @block.vector
        def _(dve):
            dve.wait_ge(x_in, 16)
            for t in range(TT):
                dve.wait_ge(acc_ready, t + 1)
                dve.scalar_tensor_tensor(out=tmp[:, t % 2], in0=gate, scalar=1.0, in1=acc[:, t % 2],
                                         op0=ALU.add, op1=ALU.mult).then_inc(acc_free, 1)
                dve.wait_ge(acc_free, t + 1)
                dve.scalar_tensor_tensor(out=v[:, t], in0=v[:, t], scalar=ALPHA, in1=tmp[:, t % 2],
                                         op0=ALU.mult, op1=ALU.add).then_inc(v_ready, 1)
                if t:
                    dve.wait_ge(sum_ready, t)
                    dve.tensor_scalar(nmean[:, t - 1:t], sm[:, t - 1:t], -1.0 / D, None, ALU.mult).then_inc(mean_ready, 1)
            dve.wait_ge(sum_ready, TT)
            dve.tensor_scalar(nmean[:, TT - 1:], sm[:, TT - 1:], -1.0 / D, None, ALU.mult).then_inc(mean_ready, 1)

        @block.scalar
        def _(act):
            moments(act, v, v_ready, sm, sum_ready, nmean, mean_ready, junk, chain, ss)


def moments(act, v, v_ready, sm, sum_ready, nmean, mean_ready, junk, chain, ss):
    st = Steps(act, chain)
    for t in range(TT + 1):
        if t < TT:
            act.wait_ge(v_ready, t + 1)
            if t:
                st(act.activation(junk[:], v[:, t], ACT.Copy, accum_out=sm[:, t:t + 1]))
            else:
                act.activation(junk[:], v[:, t], ACT.Copy, accum_out=sm[:, t:t + 1]).then_inc(chain, 1)
                st.n += 1
                act.wait_ge(chain, 1)
            act.sem_inc(sum_ready, 1)
        if t:
            act.wait_ge(mean_ready, t)
            st(act.activation(junk[:], v[:, t - 1], ACT.Square, bias=nmean[:, t - 1:t], accum_out=ss[:, t - 1:t]))


def stage_layer_norm(nc, name, gain, bias, v, nmean, ss, factor=None, shift=None, h=None, stores=()):
    with Stage(nc, name) as s:
        g, b = s.sb("g", [P, D]), s.sb("b", [P, D])
        rstd = s.sb("rstd", [P, TT])
        par, var_ready, root, chain, norm_done, v_done, hm, h_done, stored = (s.sem(n) for n in (
            "par", "var_ready", "root", "chain", "norm_done", "v_done", "hm", "h_done", "stored"))
        block = s.ctx.enter_context(nc.Block())

        @block.sync
        def _(sp):
            sp.dma_start(g[:], gain.partition_broadcast(P).rearrange("p a d -> p (a d)")).then_inc(par, 16)
            sp.dma_start(b[:], bias.partition_broadcast(P).rearrange("p a d -> p (a d)")).then_inc(par, 16)
            for t in range(TT):
                for dram, src in stores:
                    sp.wait_ge(h_done if h is not None and src is h else v_done, t + 1)
                    sp.dma_start(dram[t], src[:, t]).then_inc(stored, 16)
            if stores:
                sp.wait_ge(stored, 16 * TT * len(stores))

        @block.scalar
        def _(act):
            act.wait_ge(var_ready, 1)
            act.activation(rstd[:], rstd[:], ACT.Sqrt).then_inc(root, 1)

        @block.vector
        def _(dve):
            st = Steps(dve, chain)
            dve.tensor_scalar(rstd[:], ss[:], 1.0 / D, LN_EPS, ALU.mult, ALU.add).then_inc(var_ready, 1)
            dve.wait_ge(root, 1)
            st(dve.reciprocal(rstd[:], rstd[:]))
            dve.wait_ge(par, 32)
            for t in range(TT):
                dve.tensor_scalar(v[:, t], v[:, t], nmean[:, t:t + 1], rstd[:, t:t + 1], ALU.add, ALU.mult).then_inc(norm_done, 1)
                dve.wait_ge(norm_done, t + 1)
                st(dve.tensor_tensor(v[:, t], v[:, t], g[:], ALU.mult))
                dve.tensor_tensor(v[:, t], v[:, t], b[:], ALU.add).then_inc(v_done, 1)
                if h is not None:
                    dve.wait_ge(v_done, t + 1)
                    dve.scalar_tensor_tensor(out=h[:, t], in0=factor, scalar=1.0, in1=v[:, t], op0=ALU.add,
                                             op1=ALU.mult).then_inc(hm, 1)

        @block.gpsimd
        def _(pool):
            if h is not None:
                for t in range(TT):
                    pool.wait_ge(hm, t + 1)
                    pool.tensor_tensor(h[:, t], h[:, t], shift, ALU.add).then_inc(h_done, 1)


NG, EG = 4, 8
NE = NG * EG
TOPK = 2
FF = 256
BLOCKS = (SEQ * TOPK + NE * (P - 1) + P - 1) // P
BIG = 1.0e30


def stage_route(nc, I, K, M, h2T, wts, dest, be, idx_dram):
    NR = NG + NE
    with Stage(nc, "route") as s:
        w, bias = s.sb("w", [P, KT, NR]), s.sb("bias", [P, NR])
        iota = s.sb("iota", [P, 64])
        bstart = s.sb("bstart", [1, BLOCKS])
        tok = s.sb("tok", [P, TT], I32)
        zero = s.sb("zero", [P, BLOCKS], I32)
        lg = s.sb("lg", [P, TT, NR])
        gl = s.sb("gl", [P, TT, 8])
        gmax, gidx, gf = s.sb("gmax", [P, TT, 8]), s.sb("gidx", [P, TT, 8], U32), s.sb("gf", [P, TT])
        gm, gmb = s.sb("gm", [P, TT, NG]), s.sb("gmb", [P, TT, NG])
        el = s.sb("el", [P, TT, NE])
        emax, eidx, ef = s.sb("emax", [P, TT, 8]), s.sb("eidx", [P, TT, 8], U32), s.sb("ef", [P, TT, 2])
        ge, gs = s.sb("ge", [P, TT, NG]), s.sb("gs", [P, TT])
        d, de, den = s.sb("d", [P, TT]), s.sb("de", [P, TT]), s.sb("den", [P, TT])
        oh = s.sb("oh", [P, 2, TT, NE])
        both = s.sb("both", [P, TT, NE])
        cf, ci, padded, pend, pstart, one = (s.sb("cf", [P, NE]), s.sb("ci", [P, NE], I32), s.sb("padded", [P, NE]),
                                             s.sb("pend", [P, NE]), s.sb("pstart", [P, NE]), s.sb("one", [P, NE]))
        place, pick = s.sb("place", [P, TT, NE]), s.sb("pick", [P, TT, NE])
        df = s.sb("df", [P, 2, TT])
        bl, bef = s.sb("bl", [1, BLOCKS, NE]), s.sb("bef", [1, BLOCKS + 2])
        ps, ranks = s.ps("logits", [P, TT, 64]), s.ps("ranks", [P, 16, NE])
        par, lg_ps, chain, e_ready, e_done, both_done, rk_ps, placed, zeroed, zstore, scattered = (s.sem(n) for n in (
            "par", "lg_ps", "chain", "e_ready", "e_done", "both_done", "rk_ps", "placed", "zeroed", "zstore", "scattered"))
        block = s.ctx.enter_context(nc.Block())

        @block.sync
        def _(sp):
            kv = lambda a: a.rearrange("(p k) n -> p k n", p=P)
            sp.dma_start(w[:, :, 0:NG], kv(I["router_w_group"][0])).then_inc(par, 16)
            sp.dma_start(w[:, :, NG:], kv(I["router_w_expert"][0])).then_inc(par, 16)
            sp.dma_start(bias[:, 0:NG], I["router_b_group"].partition_broadcast(P).rearrange("p a d -> p (a d)")).then_inc(par, 16)
            sp.dma_start(bias[:, NG:], I["router_b_expert"].partition_broadcast(P).rearrange("p a d -> p (a d)")).then_inc(par, 16)
            sp.dma_start(iota[:], K["iota"]).then_inc(par, 16)
            sp.dma_start(bstart[:], K["bstart"]).then_inc(par, 16)
            sp.dma_start(tok[:], K["tokens"]).then_inc(par, 16)
            sp.wait_ge(zeroed, 1)
            sp.dma_start(idx_dram.rearrange("(p b) a -> p (b a)", p=P), zero[:]).then_inc(zstore, 16)

        @block.tensor
        def _(pe):
            pe.wait_ge(par, 16 * 7)
            for t in range(TT):
                for k in range(KT):
                    mm = pe.matmul(ps[:, t, 0:NR], h2T[:, k, t * P:(t + 1) * P], w[:, k], start=(k == 0), stop=(k == KT - 1),
                                   skip_group_check=True)
            mm.then_inc(lg_ps, 1)
            pe.wait_ge(both_done, 1)
            for t in range(TT + 1):
                for q in range(t):
                    mm = pe.matmul(ranks[:, t], M["ones"], both[:, q], start=(q == 0), stop=(q == t - 1 and t == TT), skip_group_check=True)
                if t < TT:
                    mm = pe.matmul(ranks[:, t], M["before"], both[:, t], start=(t == 0), stop=True, skip_group_check=True)
            mm.then_inc(rk_ps, 1)

        @block.scalar
        def _(act):
            act.wait_ge(e_ready, 1)
            act.activation(ge[:], ge[:], ACT.Exp)
            act.activation(de[:], d[:], ACT.Exp).then_inc(e_done, 1)

        @block.gpsimd
        def _(pool):
            pool.memset(zero[:], 0).then_inc(zeroed, 1)
            pool.wait_ge(zstore, 16)
            pool.wait_ge(placed, 1)
            for c in range(2):
                for t in range(TT):
                    pool.indirect_dma_start(out=idx_dram, out_offset=bass.IndirectOffsetOnAxis(ap=dest[:, c * TT + t:c * TT + t + 1], axis=0),
                                            in_=tok[:, t:t + 1], in_offset=None).then_inc(scattered, 16)
            pool.wait_ge(scattered, 16 * 2 * TT)

        @block.vector
        def _(dve):
            st = Steps(dve, chain)
            wide = lambda x, n: x.unsqueeze(2).broadcast_to([P, TT, n])
            dve.wait_ge(par, 16 * 7)
            st(dve.memset(gl[:], -BIG))
            st(dve.memset(one[:], 1.0))
            dve.wait_ge(lg_ps, 1)
            st(dve.tensor_tensor(lg[:], ps[:, :, 0:NR], bias[:].unsqueeze(1).broadcast_to([P, TT, NR]), ALU.add))
            st(dve.tensor_copy(gl[:, :, 0:NG], lg[:, :, 0:NG]))
            for t in range(TT):
                st(dve.max(gmax[:, t], gl[:, t]))
                st(dve.max_index(gidx[:, t], gmax[:, t], gl[:, t]))
            st(dve.tensor_copy(gf[:], gidx[:, :, 0]))
            st(dve.tensor_tensor(gm[:], iota[:, 0:NG].unsqueeze(1).broadcast_to([P, TT, NG]), wide(gf[:], NG), ALU.is_equal))
            st(dve.tensor_scalar(gmb[:], gm[:], -1.0, BIG, ALU.add, ALU.mult))
            grouped = lambda x: x.rearrange("p t (g e) -> p t g e", g=NG)
            for t in range(TT):
                w3 = lambda x: x[:, t].unsqueeze(2).broadcast_to([P, NG, EG])
                e3 = lambda x: x.rearrange("p (g e) -> p g e", g=NG)
                st(dve.tensor_tensor(e3(el[:, t]), e3(lg[:, t, NG:]), w3(gm), ALU.mult))
                st(dve.tensor_tensor(e3(el[:, t]), e3(el[:, t]), w3(gmb), ALU.add))
                st(dve.max(emax[:, t], el[:, t]))
                st(dve.max_index(eidx[:, t], emax[:, t], el[:, t]))
            st(dve.tensor_copy(ef[:], eidx[:, :, 0:2]))
            st(dve.tensor_tensor(ge[:], lg[:, :, 0:NG], wide(gmax[:, :, 0], NG), ALU.subtract))
            dve.tensor_tensor(d[:], emax[:, :, 1], emax[:, :, 0], ALU.subtract).then_inc(e_ready, 1)
            for c in range(2):
                st(dve.tensor_tensor(oh[:, c], iota[:, 0:NE].unsqueeze(1).broadcast_to([P, TT, NE]), wide(ef[:, :, c], NE), ALU.is_equal))
            dve.tensor_tensor(both[:], oh[:, 0], oh[:, 1], ALU.add).then_inc(both_done, 1)
            dve.wait_ge(e_done, 1)
            st(dve.tensor_reduce(gs[:], ge[:], AX, ALU.add))
            st(dve.tensor_scalar(den[:], de[:], 1.0, None, ALU.add))
            st(dve.tensor_tensor(den[:], den[:], gs[:], ALU.mult))
            st(dve.reciprocal(wts[:, 0:TT], den[:]))
            st(dve.tensor_tensor(wts[:, TT:], wts[:, 0:TT], de[:], ALU.mult))
            dve.wait_ge(rk_ps, 1)
            st(dve.tensor_scalar(cf[:], ranks[:, TT], float(P - 1), None, ALU.add))
            st(dve.tensor_copy(ci[:], cf[:]))
            sh = P.bit_length() - 1
            st(dve.tensor_scalar(ci[:], ci[:], sh, sh, ALU.logical_shift_right, ALU.logical_shift_left))
            st(dve.tensor_copy(padded[:], ci[:]))
            st(dve.tensor_tensor_scan(pend[:], one[:], padded[:], 0.0, ALU.mult, ALU.add))
            st(dve.tensor_tensor(pstart[:], pend[:], padded[:], ALU.subtract))
            st(dve.tensor_tensor(place[:], ranks[:, 0:TT], pstart[:].unsqueeze(1).broadcast_to([P, TT, NE]), ALU.add))
            for c in range(2):
                st(dve.tensor_tensor(pick[:], place[:], oh[:, c], ALU.mult))
                st(dve.tensor_reduce(df[:, c], pick[:], AX, ALU.add))
            dve.tensor_copy(dest[:], df[:, :, :].rearrange("p c t -> p (c t)")).then_inc(placed, 1)
            st(dve.tensor_tensor(bl[:], pend[0:1].unsqueeze(1).broadcast_to([1, BLOCKS, NE]),
                                 bstart[:].unsqueeze(2).broadcast_to([1, BLOCKS, NE]), ALU.is_le))
            st(dve.tensor_reduce(bef[:, 0:BLOCKS], bl[:], AX, ALU.add))
            st(dve.tensor_scalar(bef[:, 0:BLOCKS], bef[:, 0:BLOCKS], float(NE - 1), None, ALU.min))
            st(dve.tensor_scalar(bef[:, BLOCKS:BLOCKS + 1], pend[0:1, NE - 1:], 1.0 / P, 1.0, ALU.mult, ALU.add))
            st(dve.tensor_scalar(bef[:, BLOCKS + 1:], pend[0:1, NE - 1:], 1.0 / P, 1.0, ALU.mult, ALU.subtract))
            st(dve.tensor_copy(be[:], bef[:]))
            st(dve.tensor_scalar(be[:, BLOCKS:], be[:, BLOCKS:], 1, None, ALU.logical_shift_right))


def stage_experts(nc, I, M, h_dram, idx_dram, be, y_dram):
    with Stage(nc, "moe") as s:
        idx = s.sb("idx", [P, BLOCKS], I32)
        one_idx = s.sb("one_idx", [P, 2], I32)
        xg, xT = s.sb("xg", [P, 2, D]), s.sb("xT", [P, 2, KT, P])
        wgu, wd = s.sb("w_gate_up", [P, 2, KT, 2 * FF]), s.sb("w_down", [P, 2, 2, D])
        sg, hh, hT = s.sb("sg", [P, 2, FF]), s.sb("hh", [P, 2, FF]), s.sb("hT", [P, 2, P])
        y = s.sb("y", [P, 2, D])
        turn, gu, th, yo = s.ps("turn", [P, D]), s.ps("gu", [P, 2, NW]), s.ps("th", [P, NW]), s.ps("yo", [P, D])
        idx_in, ix_set, turn_ps, xT_sb, gu_ps, sg_sb, hh_sb, th_ps, hT_sb, y_ps, y_sb = (s.sem(n) for n in (
            "idx_in", "ix_set", "turn_ps", "xT_sb", "gu_ps", "sg_sb", "hh_sb", "th_ps", "hT_sb", "y_ps", "y_sb"))
        gathers = s.sem("gathers")
        gu_in, d_in, x_in, y_out = ([s.sem(f"{n}{j}") for j in range(2)] for n in ("gu_in", "d_in", "x_in", "y_out"))
        block = s.ctx.enter_context(nc.Block())
        pairs = lambda eng: eng.value_load(be[0:1, BLOCKS:BLOCKS + 1], min_val=TT, max_val=BLOCKS // 2)
        last_pair = lambda eng: eng.value_load(be[0:1, BLOCKS + 1:BLOCKS + 2], min_val=TT - 1, max_val=BLOCKS // 2 - 1)
        ident = M["ident"]

        @block.sync
        def _(sp):
            sp.dma_start(idx[:], idx_dram.rearrange("(b p) a -> p (b a)", p=P)).then_inc(idx_in, 16)

            def load_gate_up(b, j):
                e = sp.value_load(be[0:1, bass.ds(b, 1)], min_val=0, max_val=NE - 1)
                sp.wait_ge(gu_ps, b + 1)
                for c, name in enumerate(("moe_w_gate", "moe_w_up")):
                    src = I[name][0][bass.ds(e, 1)].rearrange("a (p k) n -> p (a k) n", p=P)
                    sp.dma_start(wgu[:, j, :, c * FF:(c + 1) * FF], src).then_inc(gu_in[j], 16)

            def load_down(b, j):
                e = sp.value_load(be[0:1, bass.ds(b, 1)], min_val=0, max_val=NE - 1)
                sp.wait_ge(y_ps, b + 1)
                src = I["moe_w_down"][0][bass.ds(e, 1)].rearrange("a (k p) n -> p (a k) n", p=P)
                sp.dma_start(wd[:, j], src).then_inc(d_in[j], 16)

            last = last_pair(sp)
            load_gate_up(0, 0)
            with sp.Fori(0, last) as i:
                for j in range(2):
                    load_gate_up(i * 2 + j + 1, 1 - j)
                    load_down(i * 2 + j, j)
            load_gate_up(last * 2 + 1, 1)
            load_down(last * 2, 0)
            load_down(last * 2 + 1, 1)

        @block.gpsimd
        def _(pool):
            pool.wait_ge(idx_in, 16)
            n = pairs(pool)
            with pool.Fori(0, n) as i:
                for j in range(2):
                    pool.wait_ge(xT_sb, i * 2 + j + 1)
                    pool.tensor_copy(one_idx[:, j:j + 1], idx[:, bass.ds(i * 2 + j, 1)]).then_inc(ix_set, 1)
                    pool.wait_ge(ix_set, i * 2 + j + 1)
                    pool.sem_inc(gathers, 1)
                    pool.indirect_dma_start(out=xg[:, j], out_offset=None, in_=h_dram,
                                            in_offset=bass.IndirectOffsetOnAxis(ap=one_idx[:, j:j + 1], axis=0)).then_inc(x_in[j], 16)

        @block.tensor
        def _(pe):
            pe.sem_inc(gu_ps, 2)
            pe.sem_inc(y_ps, 2)

            def turn_rows(j, times):
                pe.wait_ge(x_in[j], times * 16 + 16)
                for k in range(KT):
                    mm = pe.transpose(turn[:, k * P:(k + 1) * P], xg[:, j].rearrange("p (q k) -> p k q", k=KT)[:, k], ident)
                mm.then_inc(turn_ps, 1)

            def gate_up(b, j, times):
                pe.wait_ge(gu_in[j], times * 32 + 32)
                pe.wait_ge(xT_sb, b + 3)
                for k in range(KT):
                    mm = pe.matmul(gu[:, j], xT[:, j, k], wgu[:, j, k], start=(k == 0), stop=(k == KT - 1))
                mm.then_inc(gu_ps, 1)

            def step(i, j, ahead=2):
                b, after = i * 2 + j, i + j
                if ahead:
                    gate_up(b + 1, 1 - j, after)
                pe.wait_ge(hh_sb, b + 1)
                for k in range(2):
                    mm = pe.transpose(th[:, k * P:(k + 1) * P], hh[:, j, k * P:(k + 1) * P], ident)
                mm.then_inc(th_ps, 1)
                if ahead == 2:
                    turn_rows(j, i + 1)
                pe.wait_ge(d_in[j], i * 16 + 16)
                pe.wait_ge(hT_sb, b + 1)
                pe.wait_ge(y_sb, b * 2 + 1)
                for c in range(2):
                    for k in range(2):
                        mm = pe.matmul(yo[:, c * NW:(c + 1) * NW], hT[:, k], wd[:, j, k, c * NW:(c + 1) * NW], start=(k == 0), stop=(k == 1))
                mm.then_inc(y_ps, 1)

            last = last_pair(pe)
            turn_rows(0, 0)
            gate_up(0, 0, 0)
            turn_rows(1, 0)
            with pe.Fori(0, last) as i:
                step(i, 0)
                step(i, 1)
            step(last, 0, ahead=1)
            step(last, 1, ahead=0)

        @block.scalar
        def _(act):
            for j in range(2):
                act.sem_inc(y_out[j], 1)
            act.sem_inc(y_sb, 1)
            act.sem_inc(xT_sb, 2)

            def take_rows(b, j):
                act.wait_ge(turn_ps, b + 1)
                act.copy(xT[:, j, :, :].rearrange("p k c -> p (k c)"), turn[:]).then_inc(xT_sb, 1)

            def gate(b, j):
                act.wait_ge(gu_ps, b + 3)
                act.activation(sg[:, j], gu[:, j, 0:FF], ACT.Silu).then_inc(sg_sb, 1)

            def step(i, j, ahead=2):
                b = i * 2 + j
                if ahead:
                    gate(b + 1, 1 - j)
                if ahead == 2:
                    take_rows(b + 2, j)
                act.wait_ge(y_ps, b + 3)
                act.wait_ge(y_out[j], i * 16 + 1)
                act.copy(y[:, j, 0:NW], yo[:, 0:NW]).then_inc(y_sb, 1)
                act.wait_ge(y_sb, b * 2 + 3)
                act.dma_start(y_dram[bass.ds(b * P, P)], y[:, j]).then_inc(y_out[j], 16)

            last = last_pair(act)
            take_rows(0, 0)
            gate(0, 0)
            take_rows(1, 1)
            with act.Fori(0, last) as i:
                step(i, 0)
                step(i, 1)
            step(last, 0, ahead=1)
            step(last, 1, ahead=0)
            for j in range(2):
                act.wait_ge(y_out[j], last * 16 + 17)
                act.sem_inc(gathers, 1)

        @block.vector
        def _(dve):
            def times_up(b, j):
                dve.wait_ge(sg_sb, b + 1)
                dve.tensor_tensor(hh[:, j], sg[:, j], gu[:, j, FF:], ALU.mult).then_inc(hh_sb, 1)

            def step(i, j, ahead=True):
                b = i * 2 + j
                dve.wait_ge(th_ps, b + 1)
                dve.tensor_copy(hT[:, :, :].rearrange("p k c -> p (k c)"), th[:, 0:2 * P]).then_inc(hT_sb, 1)
                if ahead:
                    times_up(b + 1, 1 - j)
                dve.wait_ge(y_ps, b + 3)
                dve.wait_ge(y_out[j], i * 16 + 1)
                dve.tensor_copy(y[:, j, NW:], yo[:, NW:]).then_inc(y_sb, 1)

            last = last_pair(dve)
            times_up(0, 0)
            with dve.Fori(0, last) as i:
                step(i, 0)
                step(i, 1)
            step(last, 0)
            step(last, 1, ahead=False)


def stage_combine(nc, y_dram, dest, wts, gate, v, nmean, ss):
    with Stage(nc, "combine") as s:
        a, b = s.sb("a", [P, 2, D]), s.sb("b", [P, 2, D])
        junk, sm = s.sb("junk", [P, D]), s.sb("sum", [P, TT])
        rows = [s.sem("rows0"), s.sem("rows1")]
        chain, v_ready, sum_ready, mean_ready, achain = (s.sem(n) for n in ("chain", "v_ready", "sum_ready", "mean_ready", "achain"))
        block = s.ctx.enter_context(nc.Block())

        @block.gpsimd
        def _(pool):
            for t in range(TT):
                if t >= 2:
                    pool.wait_ge(v_ready, t - 1)
                for c, dst in ((0, a), (1, b)):
                    pool.indirect_dma_start(out=dst[:, t % 2], out_offset=None, in_=y_dram, in_offset=bass.IndirectOffsetOnAxis(
                        ap=dest[:, c * TT + t:c * TT + t + 1], axis=0)).then_inc(rows[t % 2], 16)

        @block.vector
        def _(dve):
            st = Steps(dve, chain)
            for t in range(TT):
                j = t % 2
                dve.wait_ge(rows[j], 32 * (t // 2 + 1))
                st(dve.tensor_scalar(a[:, j], a[:, j], wts[:, t:t + 1], None, ALU.mult))
                st(dve.scalar_tensor_tensor(out=a[:, j], in0=b[:, j], scalar=wts[:, TT + t:TT + t + 1], in1=a[:, j], op0=ALU.mult, op1=ALU.add))
                st(dve.scalar_tensor_tensor(out=a[:, j], in0=gate, scalar=1.0, in1=a[:, j], op0=ALU.add, op1=ALU.mult))
                dve.scalar_tensor_tensor(out=v[:, t], in0=v[:, t], scalar=ALPHA, in1=a[:, j], op0=ALU.mult, op1=ALU.add).then_inc(v_ready, 1)
                if t:
                    dve.wait_ge(sum_ready, t)
                    dve.tensor_scalar(nmean[:, t - 1:t], sm[:, t - 1:t], -1.0 / D, None, ALU.mult).then_inc(mean_ready, 1)
            dve.wait_ge(sum_ready, TT)
            dve.tensor_scalar(nmean[:, TT - 1:], sm[:, TT - 1:], -1.0 / D, None, ALU.mult).then_inc(mean_ready, 1)

        @block.scalar
        def _(act):
            moments(act, v, v_ready, sm, sum_ready, nmean, mean_ready, junk, achain, ss)


RMS_EPS = 1e-6
D_FF = 2816
FT = D_FF // P


def stage_rms_features(nc, name, hT, gain, ones, uT, keep=None, halves=None):
    with Stage(nc, name) as s:
        g = s.sb("gain", [P, KT])
        sq = s.sb("sq", [P, 2, SEQ])
        r = s.sb("rms", [P, SEQ])
        acc = s.ps("acc", [P, SEQ])
        gin, kept, sq_ready, sq_used, var_ready, root, chain, done, up, down = (s.sem(n) for n in (
            "gin", "kept", "sq_ready", "sq_used", "var_ready", "root", "chain", "done", "up", "down"))
        block = s.ctx.enter_context(nc.Block())

        @block.sync
        def _(sp):
            sp.dma_start(g[:], gain.rearrange("(k p) -> p k", p=P)).then_inc(gin, 16)
            if keep is not None:
                sp.dma_start(keep, hT[:]).then_inc(kept, 16)
                sp.wait_ge(kept, 16)

        @block.scalar
        def _(act):
            for k in range(KT):
                if k >= 2:
                    act.wait_ge(sq_used, k - 1)
                act.activation(sq[:, k % 2], hT[:, k], ACT.Square).then_inc(sq_ready, 1)
            act.wait_ge(var_ready, 1)
            act.activation(r[:], r[:], ACT.Sqrt).then_inc(root, 1)
            if halves is not None:
                if keep is not None:
                    act.wait_ge(kept, 16)
                for k in range(KT):
                    act.wait_ge(done, k + 1)
                    act.copy(halves[0][:, k], uT[:, k]).then_inc(up, 1)

        @block.gpsimd
        def _(pool):
            if halves is not None:
                for k in range(KT):
                    pool.wait_ge(up, k + 1)
                    pool.tensor_tensor(halves[1][:, k], uT[:, k], halves[0][:, k], ALU.subtract).then_inc(down, 1)

        @block.tensor
        def _(pe):
            for k in range(KT):
                pe.wait_ge(sq_ready, k + 1)
                for c in range(2):
                    mm = pe.matmul(acc[:, c * NW:(c + 1) * NW], ones, sq[:, k % 2, c * NW:(c + 1) * NW], start=(k == 0), stop=(k == KT - 1))
                mm.then_inc(sq_used, 1)

        @block.vector
        def _(dve):
            dve.wait_ge(sq_used, KT)
            dve.tensor_scalar(r[:], acc[:], 1.0 / D, RMS_EPS, ALU.mult, ALU.add).then_inc(var_ready, 1)
            dve.wait_ge(root, 1)
            dve.reciprocal(r[:], r[:]).then_inc(chain, 1)
            dve.wait_ge(chain, 1)
            dve.wait_ge(gin, 16)
            for k in range(KT):
                dve.scalar_tensor_tensor(out=uT[:, k], in0=hT[:, k], scalar=g[:, k:k + 1], in1=r[:],
                                         op0=ALU.mult, op1=ALU.mult).then_inc(done, 1)


def stage_linear(nc, name, groups, tiles, act_part, dve_part, steps=0, bufs=2, scratch=None):
    kt = sum(src.shape[1] for g in groups for _, src in g)
    n = len(groups)
    with Stage(nc, name) as s:
        w = s.sb("w", [P, 2, kt, P])
        tmp = s.sb("tmp", scratch) if scratch else None
        acc = s.ps("acc", [P, bufs, n, SEQ])
        w_in = [s.sem("w_in0"), s.sem("w_in1")]
        acc_ready, acc_free, act_ready, chain = (s.sem(x) for x in ("acc_ready", "acc_free", "act_ready", "chain"))
        per = sum(len(g) for g in groups)
        block = s.ctx.enter_context(nc.Block())

        @block.sync
        def _(sp):
            with sp.Fori(0, tiles // 2) as i:
                for j in range(2):
                    sp.wait_ge(acc_ready, i * 2 + j + 1)
                    k0 = 0
                    for g in groups:
                        for wd, src in g:
                            k1 = k0 + src.shape[1]
                            sp.dma_start(w[:, j, k0:k1], wd[:, :, bass.ds((i * 2 + j) * P, P)]).then_inc(w_in[j], 16)
                            k0 = k1

        @block.tensor
        def _(pe):
            pe.sem_inc(acc_ready, 2)
            with pe.Fori(0, tiles // 2) as i:
                for j in range(2):
                    b = j % bufs
                    pe.wait_ge(acc_free, i * 2 + j + 2)
                    pe.wait_ge(w_in[j], i * (16 * per) + 16 * per)
                    k0 = 0
                    for q, g in enumerate(groups):
                        kg = sum(src.shape[1] for _, src in g)
                        for c in range(2):
                            k = k0
                            for wd, src in g:
                                for kk in range(src.shape[1]):
                                    mm = pe.matmul(acc[:, b, q, c * NW:(c + 1) * NW], w[:, j, k], src[:, kk, c * NW:(c + 1) * NW],
                                                   start=(k == k0), stop=(k == k0 + kg - 1))
                                    k += 1
                        k0 += kg
                    mm.then_inc(acc_ready, 1)

        @block.scalar
        def _(act):
            if act_part is not None:
                with act.Fori(0, tiles // 2) as i:
                    for j in range(2):
                        act.wait_ge(acc_ready, i * 2 + j + 3)
                        act.wait_ge(acc_free, i * 2 + j + bufs)
                        act_part(act, i * 2 + j, j, [acc[:, j % bufs, q] for q in range(n)], tmp).then_inc(act_ready, 1)

        @block.vector
        def _(dve):
            dve.sem_inc(acc_free, bufs + 1)
            with dve.Fori(0, tiles // 2) as i:
                for j in range(2):
                    st = Steps(dve, chain, at=(i * 2 + j) * steps)
                    dve.wait_ge(acc_ready, i * 2 + j + 3)
                    if act_part is not None:
                        dve.wait_ge(act_ready, i * 2 + j + 1)
                    dve_part(dve, i * 2 + j, j, [acc[:, j % bufs, q] for q in range(n)], tmp, st).then_inc(acc_free, 1)
                    assert st.n == steps


def tile_of(x, m):
    return x[:, bass.ds(m, 1), :].rearrange("p a t -> p (a t)")


def stage_split(nc, name, src, high, low, load=None):
    kt = src.shape[1]
    with Stage(nc, name) as s:
        up, low_a, low_b, loaded = s.sem("up"), s.sem("low_a"), s.sem("low_b"), s.sem("loaded")
        block = s.ctx.enter_context(nc.Block())

        @block.sync
        def _(sp):
            if load is not None:
                sp.dma_start(load[0], load[1]).then_inc(loaded, 16)
                sp.wait_ge(loaded, 16)

        @block.scalar
        def _(act):
            for k in range(kt):
                act.copy(high[:, k], src[:, k]).then_inc(up, 1)

        def rest(eng, first, done):
            for k in range(first, kt, 2):
                eng.wait_ge(up, k + 1)
                eng.tensor_tensor(low[:, k], src[:, k], high[:, k], ALU.subtract).then_inc(done, 1)

        @block.vector
        def _(dve):
            rest(dve, 0, low_a)

        @block.gpsimd
        def _(pool):
            rest(pool, 1, low_b)


def stage_split_linear(nc, name, groups, tiles, act_part, dve_part, steps=0, bufs=2, scratch=None, early=0):
    terms = [t for g in groups for t in g]
    kt = sum(t[1].shape[1] for t in terms)
    kh = sum(t[1].shape[1] for t in terms if len(t) == 3)
    n = len(groups)
    with Stage(nc, name) as s:
        (w, wl), wh = s.both("w", [P, 2, kt, P]), s.sb("w_high", [P, 2, kh, P], F32R)
        tmp = s.sb("tmp", scratch) if scratch else None
        acc = s.ps("acc", [P, bufs, n, SEQ])
        w_in = [s.sem("w_in0"), s.sem("w_in1")]
        w_high, w_ready, acc_ready, acc_free, act_ready, chain = (s.sem(x) for x in (
            "w_high", "w_ready", "acc_ready", "acc_free", "act_ready", "chain"))
        begun, early_ready = s.sem("begun"), s.sem("early_ready")
        per = sum(len(g) for g in groups)
        block = s.ctx.enter_context(nc.Block())

        @block.sync
        def _(sp):
            with sp.Fori(0, tiles // 2) as i:
                for j in range(2):
                    sp.wait_ge(acc_ready, i * 2 + j + 1)
                    k0 = 0
                    for g in groups:
                        for wd, src, *_ in g:
                            k1 = k0 + src.shape[1]
                            sp.dma_start(w[:, j, k0:k1], wd[:, :, bass.ds((i * 2 + j) * P, P)]).then_inc(w_in[j], 16)
                            k0 = k1

        @block.gpsimd
        def _(pool):
            with pool.Fori(0, tiles // 2) as i:
                for j in range(2):
                    pool.wait_ge(w_in[j], i * (16 * per) + 16 * per)
                    pool.sem_inc(begun, 1)
                    pool.tensor_copy(wh[:, j], w[:, j, 0:kh]).then_inc(w_high, 1)
                    pool.wait_ge(w_high, i * 2 + j + 1)
                    pool.tensor_tensor(wl[:, j, 0:kh], w[:, j, 0:kh], wh[:, j], ALU.subtract).then_inc(w_ready, 1)

        @block.tensor
        def _(pe):
            pe.sem_inc(acc_ready, 2)
            with pe.Fori(0, tiles // 2) as i:
                for j in range(2):
                    b = j % bufs
                    if early:
                        pe.wait_ge(act_ready, i * 2 + j + 1)
                    else:
                        pe.wait_ge(acc_free, i * 2 + j + 2)
                    pe.wait_ge(w_ready, i * 2 + j + 1)
                    k0 = 0
                    for q, g in enumerate(groups):
                        if early and q == early:
                            mm.then_inc(early_ready, 1)
                            pe.wait_ge(acc_free, i * 2 + j + 2)
                        kg, k = sum(t[1].shape[1] for t in g), k0
                        for _, high, *low in g:
                            for kk in range(high.shape[1]):
                                if not low:
                                    for c in range(2):
                                        cols = slice(c * NW, (c + 1) * NW)
                                        mm = pe.matmul(acc[:, b, q, cols], w[:, j, k], high[:, kk, cols], start=(k == k0), stop=(k == k0 + kg - 1))
                                    k += 1
                                    continue
                                for c in range(2):
                                    cols = slice(c * NW, (c + 1) * NW)
                                    pe.matmul(acc[:, b, q, cols], wh[:, j, k], high[:, kk, cols], start=(k == k0), stop=False)
                                    pe.matmul(acc[:, b, q, cols], wh[:, j, k], low[0][:, kk, cols], start=False, stop=False)
                                for c in range(2):
                                    cols = slice(c * NW, (c + 1) * NW)
                                    mm = pe.matmul(acc[:, b, q, cols], wl[:, j, k], high[:, kk, cols],
                                                   start=False, stop=(k == k0 + kg - 1))
                                k += 1
                        k0 += kg
                    mm.then_inc(acc_ready, 1)

        @block.scalar
        def _(act):
            if act_part is not None:
                act.sem_inc(act_ready, 1)
                with act.Fori(0, tiles // 2) as i:
                    for j in range(2):
                        if early:
                            act.wait_ge(early_ready, i * 2 + j + 1)
                        else:
                            act.wait_ge(acc_ready, i * 2 + j + 3)
                        act.wait_ge(acc_free, i * 2 + j + bufs)
                        act_part(act, i * 2 + j, j, [acc[:, j % bufs, q] for q in range(n)], tmp).then_inc(act_ready, 1)

        @block.vector
        def _(dve):
            dve.sem_inc(acc_free, bufs + 1)
            with dve.Fori(0, tiles // 2) as i:
                for j in range(2):
                    st = Steps(dve, chain, at=(i * 2 + j) * steps)
                    dve.wait_ge(acc_ready, i * 2 + j + 3)
                    if act_part is not None:
                        dve.wait_ge(act_ready, i * 2 + j + 2)
                    dve_part(dve, i * 2 + j, j, [acc[:, j % bufs, q] for q in range(n)], tmp, st).then_inc(acc_free, 1)
                    assert st.n == steps


def stage_ffn(nc, name, wg, wu, wd, low, aT, hT, uh, h_keep):
    rows = lambda x: x.rearrange("(k p) n -> p k n", p=P)

    def silu_gate(act, m, j, acc, tmp):
        return act.activation(tile_of(aT, m), acc[0], ACT.Silu)

    def times_up(dve, m, j, acc, tmp, st):
        return dve.tensor_tensor(tile_of(aT, m), tile_of(aT, m), acc[1], ALU.mult)

    stage_split_linear(nc, name + "_in", [[(rows(wg), uh, low)], [(rows(wu), uh, low)]], FT, silu_gate, times_up)
    UN = FT // 2
    with Stage(nc, name + "_out") as s:
        (w, wl), wh = s.both("w", [P, 2, 2, NW]), s.sb("w_high", [P, 2, 2, NW], F32R)
        acc = s.ps("acc", [P, 4, SEQ])
        w_in = [s.sem("w_in0"), s.sem("w_in1")]
        w_high, w_ready, a_high, a_ready, used, acc_free, h_in = (s.sem(x) for x in (
            "w_high", "w_ready", "a_high", "a_ready", "used", "acc_free", "h_in"))
        begun = s.sem("begun")
        block = s.ctx.enter_context(nc.Block())
        down = rows(wd)
        pair = lambda x, u: x[:, bass.ds(u * 2, 2)]
        ah = [low[:, 2 * j + 4:2 * j + 6] for j in range(2)]
        al = [low[:, 2 * j:2 * j + 2] for j in range(2)]

        def units(eng, c, unit):
            unit(0, c * UN, c * UN // 2, c, True)
            with eng.Fori(0, UN // 2) as i:
                for at in (c * UN + 1, c * UN + 2):
                    unit(i * 2 + (at - c * UN), i * 2 + at, i + at // 2, at % 2, False)

        @block.sync
        def _(sp):
            for c in range(2):
                def load(u, n, turn, j, first):
                    sp.wait_ge(used, n + 1)
                    sp.dma_start(w[:, j], down[:, bass.ds(u * 2, 2), c * NW:(c + 1) * NW]).then_inc(w_in[j], 16)
                units(sp, c, load)

        @block.gpsimd
        def _(pool):
            pool.dma_start(hT[:], h_keep).then_inc(h_in, 16)
            for c in range(2):
                def halve(u, n, turn, j, first):
                    pool.wait_ge(w_in[j], turn * 16 + 16)
                    pool.sem_inc(begun, 1)
                    pool.tensor_copy(wh[:, j], w[:, j]).then_inc(w_high, 1)
                    pool.wait_ge(w_high, n + 1)
                    pool.tensor_tensor(wl[:, j], w[:, j], wh[:, j], ALU.subtract).then_inc(w_ready, 1)
                units(pool, c, halve)

        @block.scalar
        def _(act):
            for c in range(2):
                def high(u, n, turn, j, first):
                    act.wait_ge(used, n + 1)
                    act.copy(ah[j], pair(aT, u)).then_inc(a_high, 1)
                units(act, c, high)

        @block.vector
        def _(dve):
            def rest(u, n, turn, j, first):
                dve.wait_ge(a_high, n + 1)
                dve.tensor_tensor(al[j], pair(aT, u), ah[j], ALU.subtract).then_inc(a_ready, 1)

            def leave(c):
                dve.wait_ge(used, UN * (c + 1) + 2)
                dve.wait_ge(h_in, 16)
                for q in range(4):
                    k = 4 * c + q
                    dve.scalar_tensor_tensor(out=hT[:, k], in0=acc[:, q], scalar=0.5, in1=hT[:, k],
                                             op0=ALU.mult, op1=ALU.add).then_inc(acc_free, 1)

            units(dve, 0, rest)
            leave(0)
            units(dve, 1, rest)
            leave(1)

        @block.tensor
        def _(pe):
            pe.sem_inc(used, 2)
            for c in range(2):
                def products(u, n, turn, j, first):
                    pe.wait_ge(w_ready, n + 1)
                    pe.wait_ge(a_ready, n + 1)
                    for q in range(4):
                        if c and first:
                            pe.wait_ge(acc_free, q + 1)
                        o = slice(q * P, (q + 1) * P)
                        for f in range(2):
                            for t in range(2):
                                cols = slice(t * NW, (t + 1) * NW)
                                pe.matmul(acc[:, q, cols], wh[:, j, f, o], ah[j][:, f, cols], start=first and f == 0, stop=False, skip_group_check=True)
                                pe.matmul(acc[:, q, cols], wh[:, j, f, o], al[j][:, f, cols], start=False, stop=False, skip_group_check=True)
                            for t in range(2):
                                cols = slice(t * NW, (t + 1) * NW)
                                mm = pe.matmul(acc[:, q, cols], wl[:, j, f, o], ah[j][:, f, cols], start=False, stop=False,
                                               skip_group_check=True)
                    mm.then_inc(used, 1)
                units(pe, c, products)


def stage_store(nc, uT, ident, out):
    with Stage(nc, "store") as s:
        o = s.sb("o", [P, 4, D])
        turned = s.ps("turned", [P, 4, D])
        ready, free_a, free_d = (s.sem(n) for n in ("ready", "free_a", "free_d"))
        stored = [s.sem(f"stored{n}") for n in range(4)]
        view = out[0].rearrange("(t p) d -> t p d", p=P)
        block = s.ctx.enter_context(nc.Block())

        @block.tensor
        def _(pe):
            for t in range(TT):
                if t >= 4:
                    pe.wait_ge(free_a, t - 3)
                    pe.wait_ge(free_d, t - 3)
                for k in range(KT):
                    mm = pe.transpose(turned[:, t % 4, k * P:(k + 1) * P], uT[:, k, t * P:(t + 1) * P], ident)
                mm.then_inc(ready, 1)

        def take(eng, copy, half, free):
            for t in range(TT):
                eng.wait_ge(ready, t + 1)
                if t >= 4:
                    eng.wait_ge(stored[t % 4], 16 * (t // 4))
                c = slice(half * NW, half * NW + NW)
                copy(o[:, t % 4, c], turned[:, t % 4, c]).then_inc(free, 1)

        @block.scalar
        def _(act):
            take(act, act.copy, 0, free_a)

        @block.vector
        def _(dve):
            take(dve, dve.tensor_copy, 1, free_d)

        @block.sync
        def _(sp):
            for t in range(TT):
                sp.wait_ge(free_a, t + 1)
                sp.wait_ge(free_d, t + 1)
                sp.dma_start(view[t], o[:, t % 4]).then_inc(stored[t % 4], 16)
            for n in range(4):
                sp.wait_ge(stored[n], 16 * (TT // 4))


PLE = 256
GRID = 64
NAH, NAW = 8, 16
HD = 64
PAIRS = SEQ // (2 * GRID)
PADR = 128
EDGE, INNER = 14, 9
SLOTS = EDGE + INNER


def pair_window(p):
    rows = SEQ // GRID
    clip = lambda r: min(max(r - NAH // 2, 0), rows - NAH)
    a, b = clip(2 * p), clip(2 * p + 1)
    if a == b:
        return a, NAH * GRID, NAH - 1 + a - 2 * p - 1
    return a, (NAH + 1) * GRID, EDGE


def stage_neighbourhood(nc, I, K, ident, uh, ul, naT, shift_dram):
    R = 2 * NAH - 1
    scale = HD ** -0.5
    U = PAIRS * 2
    with Stage(nc, "na") as s:
        (w, wl), wh = s.both("w", [P, 3, KT, P]), s.sb("w_high", [P, 3, KT, P], F32R)
        mask = s.sb("mask", [P, SLOTS, GRID])
        tb = s.sb("bias", [P, 2, SLOTS, GRID])
        qT, kT, V = s.sb("qT", [P, 2, SEQ]), s.sb("kT", [P, SEQ]), s.sb("V", [P, TT, P])
        KW = (NAH + 1) * GRID
        pr, prT = s.sb("probs", [P, 2, KW]), s.sb("probsT", [P, 2, 5, P])
        yt = s.sb("y_tok", [P, 2, P])
        mx, nm, rsum, rinv = (s.sb(n, [P, 2, 1]) for n in ("mx", "nm", "rsum", "rinv"))
        S = [s.ps("S0", [P, SEQ]), s.ps("S1", [P, SEQ])]
        T, O = s.ps("T", [P, SEQ]), s.ps("O", [P, 2, NW])
        names = ("mask_in w_in w_used b_in zeroed tb_ready qkv_ps q_sb k_sb v_sb s_ps m_set nm_set p_sb pT_ps pT_a pT_d o_ps y_sb yT_ps yT_sb "
                 "chain units w_high w_ready begun").split()
        m = {n: s.sem(n) for n in names}
        win = I["w_in_2"][0].rearrange("(k p) n -> p k n", p=P)
        block = s.ctx.enter_context(nc.Block())

        def shifted(i, hh, dr, n):
            return shift_dram[:, bass.ds((i * 2 + hh) * R + dr, n)]

        @block.sync
        def _(sp):
            sp.dma_start(mask[:], K["na_mask"]).then_inc(m["mask_in"], 16)
            sp.wait_ge(m["zeroed"], 1)
            with sp.Fori(0, 4) as i:
                sp.wait_ge(m["w_used"], i + 1)
                for c in range(3):
                    sp.dma_start(w[:, c], win[:, :, bass.ds(i * P + c * NW, P)]).then_inc(m["w_in"], 16)
                sp.wait_ge(m["y_sb"], i * U + 1)
                for hh in range(2):
                    for r, dr, n, at in ((0, 1, EDGE, 0), (64, 0, EDGE, 0), (0, 3, NAH, EDGE), (64, 3, NAH, EDGE + 1)):
                        sp.dma_start(tb[r:r + GRID, hh, at:at + n], shifted(i, hh, dr, n)).then_inc(m["b_in"], 16)

        @block.gpsimd
        def _(pool):
            pool.memset(qT[0:64, 1], 0.0)
            pool.memset(qT[64:128, 0], 0.0)
            pool.memset(prT[64:128, :, 4], 0.0)
            pool.memset(tb[0:64, :, SLOTS - 1], 0.0)
            pool.memset(tb[64:128, :, EDGE], 0.0).then_inc(m["zeroed"], 1)
            pool.wait_ge(m["zeroed"], 1)
            with pool.Fori(0, 4) as i:
                pool.wait_ge(m["w_in"], i * 48 + 48)
                pool.sem_inc(m["begun"], 1)
                pool.tensor_copy(wh[:], w[:]).then_inc(m["w_high"], 1)
                pool.wait_ge(m["w_high"], i + 1)
                pool.tensor_tensor(wl[:], w[:], wh[:], ALU.subtract).then_inc(m["w_ready"], 1)

        def window(u):
            p, hh = u // 2, u % 2
            row, n, slot = pair_window(p)
            return p, hh, row, n, slot

        @block.tensor
        def _(pe):
            pe.sem_inc(m["w_used"], 1)
            with pe.Fori(0, 4) as i:
                pe.wait_ge(m["w_ready"], i + 1)
                pe.wait_ge(m["yT_sb"], i * PAIRS + 1)
                for c, dst in ((0, S[0]), (1, S[1])):
                    for k in range(KT):
                        for a, b in ((wh, uh), (wh, ul), (wl, uh)):
                            for t in range(2):
                                cols = slice(t * NW, (t + 1) * NW)
                                pe.matmul(dst[:, cols], a[:, c, k], b[:, k, cols], start=(k == 0 and a is wh and b is uh),
                                          stop=(k == KT - 1 and a is wl))
                for t in range(TT):
                    for k in range(KT):
                        for a, b in ((uh, wh), (uh, wl), (ul, wh)):
                            mm = pe.matmul(T[:, t * P:(t + 1) * P], a[:, k, t * P:(t + 1) * P], b[:, 2, k], start=(k == 0 and a is uh and b is wh),
                                           stop=(k == KT - 1 and a is ul), skip_group_check=True)
                mm.then_inc(m["qkv_ps"], 1)
                pe.wait_ge(m["qkv_ps"], i + 1)
                pe.sem_inc(m["w_used"], 1)
                pe.wait_ge(m["q_sb"], i + 1)
                pe.wait_ge(m["k_sb"], i + 1)
                pe.wait_ge(m["v_sb"], i + 1)

                def scores(u):
                    p, hh, row, n, slot = window(u)
                    if u >= 2:
                        pe.wait_ge(m["m_set"], i * U + u - 1)
                    for a in range(0, n, NW):
                        b = min(n, a + NW)
                        mm = pe.matmul(S[hh][:, a:b], qT[:, hh, p * P:(p + 1) * P], kT[:, row * GRID + a:row * GRID + b], start=True, stop=True)
                    mm.then_inc(m["s_ps"], 1)

                def turn_out(p):
                    pe.wait_ge(m["y_sb"], i * U + 2 * p + 3)
                    if p:
                        pe.wait_ge(m["yT_sb"], i * PAIRS + p + 1)
                    pe.transpose(T[:, 768:768 + P], yt[:, p % 2], ident).then_inc(m["yT_ps"], 1)

                scores(0)
                scores(1)
                for u in range(U):
                    p, hh, row, n, slot = window(u)
                    pe.wait_ge(m["p_sb"], i * U + u + 1)
                    if u:
                        pe.wait_ge(m["pT_a"], i * U + u)
                        pe.wait_ge(m["pT_d"], i * U + u)
                    if u % 2 == 0 and u >= 4:
                        pe.wait_ge(m["yT_sb"], i * PAIRS + p)
                    if u % 2 == 1 and u >= 3:
                        turn_out(p - 1)
                    for q in range(4):
                        mm = pe.transpose(T[:, q * P:(q + 1) * P], pr[:, u % 2, q * P:(q + 1) * P], ident)
                    if n > NW:
                        mm = pe.matmul(T[0:64, NW:NW + P], pr[:, u % 2, NW:n], ident, start=True, stop=True, skip_group_check=True)
                    mm.then_inc(m["pT_ps"], 1)
                    if u + 2 < U:
                        scores(u + 2)
                    pe.wait_ge(m["pT_a"], i * U + u + 1)
                    pe.wait_ge(m["pT_d"], i * U + u + 1)
                    if u >= 2:
                        pe.wait_ge(m["y_sb"], i * U + u)
                    t0 = row * GRID // P
                    for q in range(4):
                        mm = pe.matmul(O[:, u % 2, 0:P], prT[:, u % 2, q], V[:, t0 + q],
                                       start=(q == 0), stop=(q == 3 and n == NW))
                    if n > NW:
                        mm = pe.matmul(O[:, u % 2, 0:P], prT[:, u % 2, 4], V[:, t0 + 4], start=False, stop=True)
                    mm.then_inc(m["o_ps"], 1)
                turn_out(PAIRS - 1)

        @block.scalar
        def _(act):
            with act.Fori(0, 4) as i:
                act.wait_ge(m["qkv_ps"], i + 1)
                for hh in range(2):
                    r = slice(64 * hh, 64 * hh + 64)
                    ins = act.copy(qT[r, hh], S[0][r])
                ins.then_inc(m["q_sb"], 1)
                act.copy(V[:, :, :].rearrange("p t c -> p (t c)"), T[:]).then_inc(m["v_sb"], 1)

                def exps(u):
                    p, hh, row, n, slot = window(u)
                    act.wait_ge(m["nm_set"], i * U + u + 1)
                    act.activation(pr[:, u % 2, 0:n], pr[:, u % 2, 0:n], ACT.Exp, bias=nm[:, u % 2], scale=scale,
                                   accum_out=rsum[:, u % 2]).then_inc(m["p_sb"], 1)

                exps(0)
                for u in range(U):
                    if u + 1 < U:
                        exps(u + 1)
                    act.wait_ge(m["pT_ps"], i * U + u + 1)
                    act.copy(prT[:, u % 2, 0:4, :].rearrange("p q c -> p (q c)"), T[:, 0:NW]).then_inc(m["pT_a"], 1)

        @block.vector
        def _(dve):
            dve.sem_inc(m["yT_sb"], 1)
            dve.sem_inc(m["y_sb"], 1)
            N = 1 + 2 * U - U + U
            dve.wait_ge(m["mask_in"], 16)
            with dve.Fori(0, 4) as i:
                st = Steps(dve, m["chain"], at=i * N)
                dve.wait_ge(m["b_in"], i * 128 + 128)
                for hh in range(2):
                    ins = dve.scalar_tensor_tensor(out=tb[:, hh], in0=tb[:, hh], scalar=1.0 / scale, in1=mask[:],
                                                   op0=ALU.mult, op1=ALU.add)
                st(ins)
                dve.wait_ge(m["qkv_ps"], i + 1)
                dve.tensor_copy(kT[:], S[1][:]).then_inc(m["k_sb"], 1)

                def largest(u):
                    p, hh, row, n, slot = window(u)
                    dve.wait_ge(m["s_ps"], i * U + u + 1)
                    if u >= 2:
                        dve.wait_ge(m["pT_ps"], i * U + u - 1)
                    dve.sem_inc(m["units"], 1)
                    dve.tensor_tensor_reduce(out=pr[:, u % 2, 0:n], in0=S[hh][:, 0:n],
                                             in1=tb[:, hh, slot:slot + n // GRID, :].rearrange("p s c -> p (s c)"),
                                             scale=1.0, scalar=-3.0e38, op0=ALU.add, op1=ALU.max,
                                             accum_out=mx[:, u % 2]).then_inc(m["m_set"], 1)
                    dve.wait_ge(m["m_set"], i * U + u + 1)
                    dve.tensor_scalar(nm[:, u % 2], mx[:, u % 2], -scale, None, ALU.mult).then_inc(m["nm_set"], 1)

                largest(0)
                largest(1)
                for u in range(U):
                    p, hh, row, n, slot = window(u)
                    dve.wait_ge(m["p_sb"], i * U + u + 1)
                    st(dve.reciprocal(rinv[:, u % 2], rsum[:, u % 2]))
                    dve.wait_ge(m["pT_ps"], i * U + u + 1)
                    if n > NW:
                        dve.tensor_copy(prT[0:64, u % 2, 4], T[0:64, NW:NW + P]).then_inc(m["pT_d"], 1)
                    else:
                        dve.sem_inc(m["pT_d"], 1)
                    if u % 2 == 1 and u >= 3:
                        dve.wait_ge(m["yT_ps"], i * PAIRS + p)
                        dve.tensor_copy(naT[:, bass.ds(i, 1), (p - 1) * P:p * P].rearrange("p a t -> p (a t)"), T[:, 768:768 + P]).then_inc(m["yT_sb"], 1)
                    if u + 2 < U:
                        largest(u + 2)
                    dve.wait_ge(m["o_ps"], i * U + u + 1)
                    dve.tensor_scalar(yt[:, p % 2, hh * HD:(hh + 1) * HD], O[:, u % 2, hh * HD:(hh + 1) * HD], rinv[:, u % 2], None,
                                      ALU.mult).then_inc(m["y_sb"], 1)
                dve.wait_ge(m["yT_ps"], i * PAIRS + PAIRS)
                dve.tensor_copy(naT[:, bass.ds(i, 1), (PAIRS - 1) * P:].rearrange("p a t -> p (a t)"), T[:, 768:768 + P]).then_inc(m["yT_sb"], 1)
                while st.n < N:
                    dve.sem_inc(m["chain"], 1)
                    st.n += 1


SG, SP_, SI = 32, 64, 16
L = 8
NCH = SEQ // L
GP = SG // 2
Q = 4
PQ = GP // Q
HALF_PI = 1.5707963267948966


def complex_product(op, out, a, b, t1, t2, conj_b=False):
    (orr, oi), (ar, ai), (br, bi) = out, a, b
    op(t1, ar, br, ALU.mult)
    op(t2, ai, bi, ALU.mult)
    op(orr, t1, t2, ALU.add if conj_b else ALU.subtract)
    op(t1, ai, br, ALU.mult)
    op(t2, ar, bi, ALU.mult)
    op(oi, t1, t2, ALU.subtract if conj_b else ALU.add)


def stage_ssm_parameters(nc, I, ident, powers, w8, r8, bbar, ct):
    ND = 2 * GP
    W = lambda n: I[n + "_2"][0]
    with Stage(nc, "ssmpar") as s:
        rows = s.sb("rows", [3 * ND, 2, SP_])
        ldt = s.sb("ldt", [3 * ND, 2])
        names = "lr li dt a b er em e1 r h sh ch cs sn cm Er Ei den cr ci t1 t2".split()
        x = {n: s.sb(n, [P, ND]) for n in names}
        ki = s.sb("ki", [P, ND], I32)
        bre, bim = s.sb("bre", [P, ND, SI]), s.sb("bim", [P, ND, SI])
        u1, u2 = s.sb("u1", [P, ND, SI]), s.sb("u2", [P, ND, SI])
        cl = s.sb("c_rows", [P, 4, 4, 2, SP_])
        ps, pc = s.ps("params", [P, NW]), s.ps("c_turned", [P, 4, 4, P])
        par, exp_rows, turned, chain, a1, a2, c_ps, d1, d2 = (s.sem(n) for n in ("par", "exp_rows", "turned", "chain", "a1", "a2", "c_ps", "d1", "d2"))
        block = s.ctx.enter_context(nc.Block())

        @block.sync
        def _(sp):
            for n, name in enumerate(("ssm_lam_re", "ssm_lam_im")):
                sp.dma_start(rows[n * ND:(n + 1) * ND], W(name).rearrange("d (q g) p -> (d q) g p", g=2)).then_inc(par, 16)
            sp.dma_start(ldt[2 * ND:], W("ssm_log_dt").rearrange("d (q g) -> (d q) g", g=2)).then_inc(par, 16)
            for dst, name in ((bre, "ssm_b_re"), (bim, "ssm_b_im")):
                for d in range(2):
                    for g in range(2):
                        src = W(name)[d].rearrange("(q g) p i -> g p q i", g=2)[g]
                        sp.dma_start(dst[g * 64:(g + 1) * 64, d * GP:(d + 1) * GP], src).then_inc(par, 16)
            for n, name in enumerate(("ssm_c_re", "ssm_c_im")):
                for d in range(2):
                    src = W(name)[d].rearrange("(t g) o p -> (g o) t p", t=4)
                    for dup in range(2):
                        sp.dma_start(cl[:, 2 * n + d, :, dup], src).then_inc(par, 16)
        NPAR = 16 * (3 + 8 + 8)

        @block.tensor
        def _(pe):
            pe.wait_ge(par, NPAR)
            pe.wait_ge(exp_rows, 1)
            pe.matmul(ps[:, 0:3 * ND], rows[:, :, :].rearrange("a g p -> a (g p)"), ident[0:3 * ND, 0:3 * ND], start=True, stop=True).then_inc(turned, 1)
            for n in range(4):
                for t in range(4):
                    mm = pe.transpose(pc[:, n, t], cl[:, n, t, :, :].rearrange("a d p -> a (d p)"), ident)
            mm.then_inc(c_ps, 1)

        @block.scalar
        def _(act):
            act.wait_ge(turned, 1)
            act.wait_ge(d1, 1)
            act.activation(x["dt"][:], x["dt"][:], ACT.Exp).then_inc(a1, 1)
            act.wait_ge(d2, 1)
            act.activation(x["sh"][:], x["h"][:], ACT.Sin)
            act.activation(x["ch"][:], x["t2"][:], ACT.Sin).then_inc(a2, 1)

        @block.vector
        def _(dve):
            st = Steps(dve, chain)
            v = {n: t[:] for n, t in x.items()}
            op = lambda o, a, b, f: st(dve.tensor_tensor(o, a, b, f))
            sc = lambda o, a, s1, f1, s2=None, f2=None: st(dve.tensor_scalar(o, a, s1, s2, f1, *([f2] if f2 else [])))
            dve.wait_ge(par, NPAR)
            dve.tensor_copy(rows[2 * ND:], ldt[2 * ND:].unsqueeze(2).broadcast_to([ND, 2, SP_])).then_inc(exp_rows, 1)
            dve.wait_ge(turned, 1)
            sc(v["lr"], ps[:, 0:ND], -1e-4, ALU.min)
            st(dve.tensor_copy(v["li"], ps[:, ND:2 * ND]))
            dve.tensor_copy(v["dt"], ps[:, 2 * ND:3 * ND]).then_inc(d1, 1)
            dve.wait_ge(a1, 1)
            op(v["a"], v["lr"], v["dt"], ALU.mult)
            op(v["b"], v["li"], v["dt"], ALU.mult)
            sc(v["a"], v["a"], -64.0, ALU.max)
            sc(v["h"], v["a"], 1.0 / 128, ALU.mult)
            st(dve.memset(v["em"], 1.0))
            for n in range(8, 1, -1):
                op(v["t1"], v["em"], v["h"], ALU.mult)
                sc(v["em"], v["t1"], 1.0 / n, ALU.mult, 1.0, ALU.add)
            op(v["em"], v["em"], v["h"], ALU.mult)
            for n in range(7):
                sc(v["t1"], v["em"], 2.0, ALU.add)
                op(v["em"], v["em"], v["t1"], ALU.mult)
            sc(v["er"], v["em"], 1.0, ALU.add)
            sc(v["t1"], v["b"], 1.0 / (4 * HALF_PI), ALU.mult)
            st(dve.tensor_copy(ki[:], v["t1"]))
            st(dve.tensor_copy(v["t1"], ki[:]))
            for part in (-6.28125, -0.0019350051879882812, -3.0199159819e-07):
                st(dve.scalar_tensor_tensor(out=v["b"], in0=v["t1"], scalar=part, in1=v["b"], op0=ALU.mult, op1=ALU.add))
            sc(v["b"], v["b"], 2 * HALF_PI, ALU.min, -2 * HALF_PI, ALU.max)
            sc(v["h"], v["b"], 0.5, ALU.mult)
            st(dve.scalar_tensor_tensor(out=v["t1"], in0=v["h"], scalar=-1.0, in1=v["h"], op0=ALU.mult, op1=ALU.min))
            dve.tensor_scalar(v["t2"], v["t1"], HALF_PI, None, ALU.add).then_inc(d2, 1)
            dve.wait_ge(a2, 1)
            op(v["cm"], v["sh"], v["sh"], ALU.mult)
            sc(v["cm"], v["cm"], -2.0, ALU.mult)
            sc(v["cs"], v["cm"], 1.0, ALU.add)
            op(v["sn"], v["sh"], v["ch"], ALU.mult)
            sc(v["sn"], v["sn"], 2.0, ALU.mult)
            op(v["t1"], v["em"], v["cs"], ALU.mult)
            op(v["Er"], v["t1"], v["cm"], ALU.add)
            op(v["Ei"], v["er"], v["sn"], ALU.mult)
            op(v["t1"], v["lr"], v["lr"], ALU.mult)
            op(v["t2"], v["li"], v["li"], ALU.mult)
            op(v["den"], v["t1"], v["t2"], ALU.add)
            st(dve.reciprocal(v["den"], v["den"]))
            complex_product(op, (v["cr"], v["ci"]), (v["Er"], v["Ei"]), (v["lr"], v["li"]), v["t1"], v["t2"], conj_b=True)
            op(v["cr"], v["cr"], v["den"], ALU.mult)
            op(v["ci"], v["ci"], v["den"], ALU.mult)
            wide = lambda y: y.unsqueeze(2).broadcast_to([P, ND, SI])
            complex_product(op, (bbar[:, 0], bbar[:, 1]), (bre[:], bim[:]), (wide(v["cr"]), wide(v["ci"])), u1[:], u2[:])
            pw = lambda n: (powers[:, 0, n], powers[:, 1, n])
            st(dve.memset(powers[:, 0, 0], 1.0))
            st(dve.memset(powers[:, 1, 0], 0.0))
            op(powers[:, 0, 1], v["er"], v["cs"], ALU.mult)
            op(powers[:, 1, 1], v["er"], v["sn"], ALU.mult)
            for n in range(2, L + 1):
                complex_product(op, pw(n), pw(n // 2), pw(n - n // 2), v["t1"], v["t2"])
            wr, wi = w8[:, 0], w8[:, 1]
            st(dve.tensor_copy(wr, v["cs"]))
            st(dve.tensor_copy(wi, v["sn"]))
            st(dve.tensor_copy(r8, v["er"]))
            for n in range(3):
                op(v["t1"], wr, wr, ALU.mult)
                op(v["t2"], wi, wi, ALU.mult)
                op(v["h"], wr, wi, ALU.mult)
                op(wr, v["t1"], v["t2"], ALU.subtract)
                sc(wi, v["h"], 2.0, ALU.mult)
                op(r8, r8, r8, ALU.mult)
            dve.wait_ge(c_ps, 1)
            for n in range(4):
                for g in range(2):
                    r = slice(64 * g, 64 * g + 64)
                    src = pc[r, n].rearrange("p t (q g o) -> p t q g o", g=2, o=SI)[:, :, :, g]
                    dst = ct[r, n // 2, (n % 2) * GP:(n % 2 + 1) * GP].rearrange("p (t q) o -> p t q o", t=4)
                    for t in range(4):
                        st(dve.tensor_copy(dst[:, t], src[:, t]))


def stage_phasors(nc, w8, wt):
    with Stage(nc, "phasors") as s:
        ND = 2 * GP
        t1, t2 = s.sb("t1", [P, ND, NCH // 2]), s.sb("t2", [P, ND, NCH // 2])
        sq = s.sb("sq", [P, 2, 2, ND])
        chain = s.sem("chain")
        block = s.ctx.enter_context(nc.Block())

        @block.vector
        def _(dve):
            st = Steps(dve, chain)
            op = lambda o, a, b, f: st(dve.tensor_tensor(o, a, b, f))
            st(dve.memset(wt[:, 0, :, 0], 1.0))
            st(dve.memset(wt[:, 1, :, 0], 0.0))
            st(dve.tensor_copy(sq[:, 0], w8[:]))
            n, cur = 1, 0
            while n < NCH:
                b = lambda c: sq[:, cur, c].unsqueeze(2).broadcast_to([P, ND, n])
                complex_product(op, (wt[:, 0, :, n:2 * n], wt[:, 1, :, n:2 * n]), (wt[:, 0, :, 0:n], wt[:, 1, :, 0:n]),
                                (b(0), b(1)), t1[:, :, 0:n], t2[:, :, 0:n])
                a = (sq[:, cur, 0], sq[:, cur, 1])
                complex_product(op, (sq[:, 1 - cur, 0], sq[:, 1 - cur, 1]), a, a, t1[:, :, 0], t2[:, :, 0])
                n, cur = 2 * n, 1 - cur


def stage_ssm(nc, I, M, uT, powers, r8, bbar, ct, wt, yT, shift_dram):
    ident, flip = M["ident"], M["flip"]
    W = lambda n: I[n + "_2"][0]
    G8 = 2 * PQ
    with Stage(nc, "ssm") as s:
        w = s.sb("w", [P, KT, P])
        dcol = s.sb("dcol", [P, SG])
        S2 = s.sb("S2", [P, G8, L, SI])
        U, Ur = s.sb("U", [P, G8, P]), s.sb("Ur", [P, G8, P])
        A = [s.sb(f"A{d}", [P, 2, PQ, L, SI]) for d in range(2)]
        pt1, pt2 = s.sb("pt1", [P, PQ, L + 1, SI]), s.sb("pt2", [P, PQ, L + 1, SI])
        Bq = [s.sb(f"Bq{d}", [P, 2, PQ, SI]) for d in range(2)]
        PT = [s.sb(f"PT{d}", [P, 2, PQ, 2, L + 1, SI]) for d in range(2)]
        Min = s.sb("Min", [P, 2, PQ, P])
        Kt = s.sb("Kt", [SI, PQ, 2, L, SI])
        Tf, Tb, T = (s.sb(n, [P, G8, L * SI]) for n in ("Tf", "Tb", "T"))
        R = [s.sb(f"R{d}", [P, PQ, NCH]) for d in range(2)]
        z = s.sb("z", [P, 2, PQ, NCH])
        rows = s.sb("bias_rows", [8 * (2 * NAH - 1), PADR])
        pad = s.sb("pad", [P, 2, PQ, NCH + 1])
        Yb, Yg = s.sb("Yb", [P, G8 * P]), s.sb("Yg", [P, L, G8, SI])
        X = [s.ps(f"X{n}", [P, SEQ]) for n in range(4)]
        names = ("w_in d_in s2_ps s2_sb u_ps u_sb ur_sb a_sb min_ps min_sb pt_sb k_ps k_sb t_in v_ps pad_sb yb_ps yb_sb y_ps yg_sb yt_ps yt_sb "
                 "zeroed chain t_ready q_done rows_set rows_in shifted").split()
        m = {n: s.sem(n) for n in names}
        block = s.ctx.enter_context(nc.Block())
        win = I["w_in_2"][0].rearrange("(k p) n -> p k n", p=P)

        @block.sync
        def _(sp):
            sp.sem_inc(m["t_in"], 1)
            for j in range(L):
                sp.dma_start(dcol[j * SI:(j + 1) * SI], W("ssm_d").rearrange("(g i) -> i g", i=SI)).then_inc(m["d_in"], 16)
            with sp.Fori(0, Q) as i:
                sp.wait_ge(m["s2_ps"], i + 1)
                sp.dma_start(w[:], win[:, :, bass.ds(3 * NW + i * P, P)]).then_inc(m["w_in"], 16)
                for d in range(2):
                    sp.wait_ge(m["k_sb"], i * 2 + d + 1)
                    Td = (Tf, Tb)[d]
                    src = Kt[:, :, :, :, :].rearrange("i q g l o -> i (q g) (l o)")
                    for j in range(L):
                        dst = Td[j * SI:(j + 1) * SI]
                        if d == 0:
                            sp.dma_start(dst[:, :, j * SI:], src[:, :, 0:(L - j) * SI]).then_inc(m["t_in"], 16)
                        else:
                            sp.dma_start(dst[:, :, 0:(j + 1) * SI], src[:, :, (L - 1 - j) * SI:]).then_inc(m["t_in"], 16)

        @block.gpsimd
        def _(pool):
            pool.memset(Tf[:], 0.0)
            pool.memset(Tb[:], 0.0)
            pool.memset(PT[0][:], 0.0)
            pool.memset(PT[1][:], 0.0)
            pool.memset(pad[:], 0.0).then_inc(m["zeroed"], 1)
            pool.memset(rows[:], 0.0).then_inc(m["rows_set"], 1)
            pool.wait_ge(m["rows_set"], 1)
            lo = GRID - NAW
            pool.dma_start(rows[:, lo:lo + 2 * NAW - 1], I["na_rpb_2"][0].rearrange("h r c -> (h r) c")).then_inc(m["rows_in"], 16)
            pool.wait_ge(m["rows_in"], 16)
            with pool.Fori(0, GRID) as i:
                pool.dma_start(shift_dram[bass.ds(GRID - 1 - i, 1)].rearrange("c r k -> (c r) k"),
                               rows[:, bass.ds(i, GRID)]).then_inc(m["shifted"], 16)
            pool.wait_ge(m["shifted"], 16 * GRID)

        @block.tensor
        def _(pe):
            pe.sem_inc(m["s2_ps"], 1)
            pe.wait_ge(m["zeroed"], 1)
            with pe.Fori(0, Q) as i:
                pe.wait_ge(m["w_in"], i * 16 + 16)
                pe.wait_ge(m["q_done"], i + 1)
                for j in range(L):
                    for k in range(KT):
                        mm = pe.matmul(X[0][:, j * P:(j + 1) * P], uT[:, k].rearrange("p (c j) -> p j c", j=L)[:, j], w[:, k],
                                       start=(k == 0), stop=(k == KT - 1), skip_group_check=True)
                mm.then_inc(m["s2_ps"], 1)
                pe.wait_ge(m["s2_sb"], i + 1)
                for g in range(G8):
                    src = S2[:, g, :, :].rearrange("p l i -> p (l i)")
                    pe.matmul(X[1][:, g * P:(g + 1) * P], src, ident, start=True, stop=True, skip_group_check=True)
                    mm = pe.matmul(X[2][:, g * P:(g + 1) * P], src, flip, start=True, stop=True, skip_group_check=True)
                mm.then_inc(m["u_ps"], 1)

                def maps(d):
                    pe.wait_ge(m["a_sb"], i * 2 + d + 1)
                    for c in range(2):
                        for q in range(PQ):
                            mm = pe.transpose(X[0][:, (c * PQ + q) * P:(c * PQ + q + 1) * P],
                                              A[d][:, c, q, :, :].rearrange("p l i -> p (l i)"), ident)
                    mm.then_inc(m["min_ps"], 1)
                    pe.wait_ge(m["pt_sb"], i * 2 + d + 1)
                    if d == 0:
                        pe.wait_ge(m["u_sb"], i + 1)
                    else:
                        pe.wait_ge(m["k_sb"], i * 2 + 1)
                    lo = (0, 1)[d]
                    for q in range(PQ):
                        for c in range(2):
                            mm = pe.matmul(X[1][0:SI, q * 256:(q + 1) * 256], Bq[d][:, c, q], PT[d][:, c, q, :, lo:lo + L, :],
                                           start=(c == 0), stop=(c == 1), skip_group_check=True)
                    mm.then_inc(m["k_ps"], 1)
                    pe.wait_ge(m["min_sb"], i * 2 + d + 1)

                def into_states(d):
                    src = (U, Ur)[d]
                    for c in range(2):
                        for g in range(G8):
                            r = slice(64 * (g % 2), 64 * (g % 2) + 64)
                            mm = pe.matmul(X[2][r, c * NW + (g // 2) * P:c * NW + (g // 2 + 1) * P], Min[:, c, g // 2, r], src[:, g],
                                           start=True, stop=True, skip_group_check=True)
                    mm.then_inc(m["v_ps"], 1)

                def out_of_states(d):
                    pe.wait_ge(m["pad_sb"], i * 2 + d + 1)
                    out = (X[3], X[0])[d]
                    first = (1, 0)[d]
                    for q in range(PQ):
                        for c in range(2):
                            mm = pe.matmul(out[:, q * 256:(q + 1) * 256], pad[:, c, q, 0:NCH], PT[d][:, c, q, :, first:first + L, :],
                                           start=(c == 0 and q % 2 == 0), stop=(d == 1 and c == 1), skip_group_check=True)
                    mm.then_inc((m["y_ps"], m["yb_ps"])[d], 1)

                maps(0)
                pe.wait_ge(m["ur_sb"], i + 1)
                into_states(0)
                maps(1)
                out_of_states(0)
                into_states(1)
                out_of_states(1)
                pe.wait_ge(m["t_ready"], i + 1)
                pe.wait_ge(m["yb_sb"], i + 1)
                for g in range(G8):
                    pe.matmul(X[3][:, g * P:(g + 1) * P], U[:, g], T[:, g], start=False, stop=False, skip_group_check=True)
                for c in range(2):
                    mm = pe.matmul(X[3][:, c * NW:(c + 1) * NW], flip, Yb[:, c * NW:(c + 1) * NW], start=False, stop=True, skip_group_check=True)
                mm.then_inc(m["y_ps"], 1)
                pe.wait_ge(m["yg_sb"], i + 1)
                for j in range(L):
                    mm = pe.matmul(X[0][:, j * P:(j + 1) * P], Yg[:, j, :, :].rearrange("p g o -> p (g o)"), ident, start=True, stop=True, skip_group_check=True)
                mm.then_inc(m["yt_ps"], 1)

        @block.scalar
        def _(act):
            act.sem_inc(m["q_done"], 1)
            with act.Fori(0, Q) as i:
                act.wait_ge(m["s2_ps"], i + 2)
                for g in range(G8):
                    ins = act.copy(S2[:, g], X[0][:, :].rearrange("p (l g i) -> p g l i", l=L, i=SI)[:, g])
                ins.then_inc(m["s2_sb"], 1)
                act.wait_ge(m["u_ps"], i + 1)
                act.copy(U[:, :, :].rearrange("p g c -> p (g c)"), X[1][:]).then_inc(m["u_sb"], 1)
                act.copy(Ur[:, :, :].rearrange("p g c -> p (g c)"), X[2][:]).then_inc(m["ur_sb"], 1)
                for d in range(2):
                    act.wait_ge(m["min_ps"], i * 2 + d + 1)
                    act.copy(Min[:, :, :, :].rearrange("p c q x -> p (c q x)"), X[0][:]).then_inc(m["min_sb"], 1)
                    act.wait_ge(m["k_ps"], i * 2 + d + 1)
                    act.wait_ge(m["t_in"], (i * 2 + d) * (16 * L) + 1)
                    act.copy(Kt[:, :, :, :, :].rearrange("i q g l o -> i (q g l o)"), X[1][0:SI]).then_inc(m["k_sb"], 1)
                act.wait_ge(m["yb_ps"], i + 1)
                act.copy(Yb[:], X[0][:]).then_inc(m["yb_sb"], 1)
                act.wait_ge(m["y_ps"], i * 2 + 2)
                for j in range(L):
                    ins = act.activation(Yg[:, j], X[3][:, :].rearrange("p (g j o) -> p j g o", j=L, o=SI)[:, j], ACT.Gelu_apprx_tanh)
                ins.then_inc(m["yg_sb"], 1)
                act.wait_ge(m["yt_ps"], i + 1)
                dst = yT[:, bass.ds(i, 1), :].rearrange("p a (c j) -> p (a c) j", j=L)
                act.copy(dst, X[0][:, :].rearrange("p (j c) -> p c j", j=L)).then_inc(m["q_done"], 1)

        @block.vector
        def _(dve):
            N = 100
            dve.wait_ge(m["d_in"], 16 * L)
            dve.wait_ge(m["zeroed"], 1)
            with dve.Fori(0, Q) as i:
                st = Steps(dve, m["chain"], at=i * N)
                op = lambda o, a, b, f: st(dve.tensor_tensor(o, a, b, f))
                for d in range(2):
                    at = d * GP + i * PQ
                    for c in range(2):
                        st(dve.tensor_copy(Bq[d][:, c], bbar[:, c, bass.ds(at, PQ)]))
                    pw = lambda c, n: powers[:, c, n, bass.ds(at, PQ)]
                    b4 = lambda c: Bq[d][:, c]
                    for l in range(L):
                        n = (L - 1 - l) if d == 0 else l
                        wide = lambda c: pw(c, n).unsqueeze(2).broadcast_to([P, PQ, SI])
                        t1, t2 = pt1[:, :, l], pt2[:, :, l]
                        dve.tensor_tensor(t1, b4(0), wide(0), ALU.mult)
                        ins = dve.tensor_tensor(t2, b4(1), wide(1), ALU.mult)
                    st(ins)
                    op(A[d][:, 0], pt1[:, :, 0:L], pt2[:, :, 0:L], ALU.subtract)
                    for l in range(L):
                        n = (L - 1 - l) if d == 0 else l
                        wide = lambda c: pw(c, n).unsqueeze(2).broadcast_to([P, PQ, SI])
                        dve.tensor_tensor(pt1[:, :, l], b4(0), wide(1), ALU.mult)
                        ins = dve.tensor_tensor(pt2[:, :, l], b4(1), wide(0), ALU.mult)
                    st(ins)
                    dve.tensor_tensor(A[d][:, 1], pt1[:, :, 0:L], pt2[:, :, 0:L], ALU.add).then_inc(m["a_sb"], 1)
                    dve.wait_ge(m["a_sb"], i * 2 + d + 1)
                    c4 = lambda c: ct[:, c, bass.ds(at, PQ)]
                    for part in range(2):
                        for n in range(L + 1):
                            l = n if d == 0 else L - n
                            wide = lambda c: pw(c, n).unsqueeze(2).broadcast_to([P, PQ, SI])
                            dve.tensor_tensor(pt1[:, :, l], c4(0), wide(part), ALU.mult)
                            ins = dve.tensor_tensor(pt2[:, :, l], c4(1), wide(1 - part), ALU.mult)
                        st(ins)
                        for g in range(2):
                            r = slice(64 * g, 64 * g + 64)
                            if part == 0:
                                ins = dve.tensor_tensor(PT[d][r, 0, :, g], pt1[r], pt2[r], ALU.subtract)
                                st(ins)
                            else:
                                ins = dve.scalar_tensor_tensor(out=PT[d][r, 1, :, g], in0=pt1[r], scalar=-1.0, in1=pt2[r],
                                                               op0=ALU.mult, op1=ALU.subtract)
                                if g == 0:
                                    st(ins)
                    ins.then_inc(m["pt_sb"], 1)
                    for c in range(PQ):
                        st(dve.tensor_copy(R[d][:, c, 1:], r8[:, bass.ds(at + c, 1)].broadcast_to([P, NCH - 1])))
                    st(dve.memset(R[d][:, :, 0:1], 0.0))
                for d in range(2):
                    at = d * GP + i * PQ
                    dve.wait_ge(m["v_ps"], i * 2 + d + 1)
                    wv = lambda c: wt[:, c, bass.ds(at, PQ)]
                    V = lambda c: X[2][:, c * NW:(c + 1) * NW].rearrange("p (q n) -> p q n", q=PQ)
                    t1 = pt1[:, :, :, :].rearrange("p q l i -> p q (l i)")[:, :, 0:NCH]
                    t2 = pt2[:, :, :, :].rearrange("p q l i -> p q (l i)")[:, :, 0:NCH]
                    complex_product(op, (z[:, 0], z[:, 1]), (V(0), V(1)), (wv(0), wv(1)), t1, t2, conj_b=True)
                    for c in range(2):
                        fl = lambda y: y.rearrange("p q n -> p (q n)")
                        st(dve.tensor_tensor_scan(fl(z[:, c]), fl(R[d][:, :, :]), fl(z[:, c]), 0.0, ALU.mult, ALU.add))
                    if d:
                        dve.wait_ge(m["y_ps"], i * 2 + 1)
                    complex_product(op, (pad[:, 0, :, 1:], pad[:, 1, :, 1:]), (z[:, 0], z[:, 1]), (wv(0), wv(1)), t1, t2)
                    dve.sem_inc(m["pad_sb"], 1)
                dve.wait_ge(m["t_in"], i * (32 * L) + 32 * L + 1)
                dve.wait_ge(m["y_ps"], i * 2 + 1)
                op(T[:], Tf[:], Tb[:], ALU.add)
                for g in range(G8):
                    ins = dve.scalar_tensor_tensor(out=T[:, g], in0=ident, scalar=dcol[:, bass.ds(i * G8 + g, 1)], in1=T[:, g],
                                                   op0=ALU.mult, op1=ALU.add)
                ins.then_inc(m["t_ready"], 1)
                dve.wait_ge(m["t_ready"], i + 1)
                dve.wait_ge(m["q_done"], i + 2)
                assert st.n <= N, st.n
                dve.sem_inc(m["chain"], N - st.n)


def stage_glu(nc, I, yT, oT):
    rows = lambda x: x.rearrange("(k p) n -> p k n", p=P)
    with ExitStack() as a:
        bcol = a.enter_context(nc.sbuf_tensor("glu_b", [P, 4], F32))
        stage_load(nc, "glub", [(bcol[:], I["ssm_glu_b_2"][0].rearrange("(k p) -> p k", p=P))])

        def gate(act, m, j, acc, tmp):
            return act.activation(tmp[:, j], acc[0], ACT.Sigmoid, bias=bcol[:, bass.ds(m, 1)])

        def times(dve, m, j, acc, tmp, st):
            return dve.tensor_tensor(tile_of(oT, m), tile_of(yT, m), tmp[:, j], ALU.mult)

        stage_linear(nc, "glu", [[(rows(I["ssm_glu_w_2"][0]), yT)]], 4, gate, times, scratch=[P, 2, SEQ])


def stage_copy(nc, name, pairs):
    stage_load(nc, name, pairs)


def stage_mixer(nc, I, K, M, hT, hh, uT, ul, h_keep):
    ident, ones = M["ident"], M["ones"]
    W = lambda n: I[n + "_2"][0]
    rows = lambda x: x.rearrange("(k p) n -> p k n", p=P)
    ND = 2 * GP
    shift_dram = nc.dram_tensor("bias_shifted", [GRID, 8 * (2 * NAH - 1), GRID], F32, kind="Internal").ap()
    with ExitStack() as a:
        ssmT = a.enter_context(nc.sbuf_tensor("ssmT", [P, 4, SEQ], F32))
        stage_rms_features(nc, "rms2", hT, W("mix_norm"), ones, uT, keep=h_keep)
        with ExitStack() as b:
            def bb(name, shape):
                return b.enter_context(nc.sbuf_tensor(name, shape, F32))
            yS = bb("yS", [P, 4, SEQ])
            with ExitStack() as c:
                def cb(name, shape):
                    return c.enter_context(nc.sbuf_tensor(name, shape, F32))
                powers, w8, r8 = cb("powers", [P, 2, L + 1, ND]), cb("w8", [P, 2, ND]), cb("r8", [P, ND])
                bbar, ct = cb("bbar", [P, 2, ND, SI]), cb("ct", [P, 2, ND, SI])
                wt = hT[:, :, :].rearrange("p k t -> p (k t)").rearrange("p (c n t) -> p c n t", c=2, t=NCH)
                stage_ssm_parameters(nc, I, ident, powers, w8, r8[:], bbar, ct)
                stage_phasors(nc, w8, wt)
                stage_ssm(nc, I, M, uT, powers, r8, bbar, ct, wt, yS, shift_dram)
            stage_glu(nc, I, yS, ssmT)
        naT = a.enter_context(nc.sbuf_tensor("naT", [P, 4, SEQ], F32))
        stage_split(nc, "split2", uT, hh, ul)
        stage_neighbourhood(nc, I, K, ident, hh, ul, naT, shift_dram)
        mT, ml = in_both_types(nc, a, "mT", [P, KT, SEQ])

        def gates(act, m, j, acc, tmp):
            act.activation(tmp[:, j, 0], acc[0], ACT.Sigmoid)
            return act.activation(tmp[:, j, 1], acc[1], ACT.Sigmoid)

        def blend(dve, m, j, acc, tmp, st):
            st(dve.tensor_tensor(tmp[:, j, 0], tmp[:, j, 0], acc[2], ALU.mult))
            st(dve.tensor_tensor(tmp[:, j, 1], tmp[:, j, 1], acc[3], ALU.mult))
            return dve.tensor_tensor(tile_of(mT, m), tmp[:, j, 0], tmp[:, j, 1], ALU.add)

        wi = rows(W("w_in"))
        stage_split_linear(nc, "blend", [[(wi[:, :, 2048:3072], hh, ul)], [(wi[:, :, 3072:4096], hh, ul)], [(rows(W("w_attn_out")), naT)],
                                   [(rows(W("w_ssm_out")), ssmT)]], KT, gates, blend, steps=2, bufs=1, scratch=[P, 2, 2, SEQ], early=2)

        def add(dve, m, j, acc, tmp, st):
            return dve.tensor_tensor(tile_of(hT, m), tile_of(hT, m), acc[0], ALU.add)

        stage_split(nc, "splitm", mT, ul, ml, load=(hT[:], h_keep))
        stage_split_linear(nc, "mixout2", [[(rows(W("w_out")), ul, ml)]], KT, None, add)


def shape_constants():
    import numpy as np

    j, i = np.meshgrid(np.arange(P), np.arange(P), indexing="ij")
    same = j // 64 == i // 64
    sq = {
        "ident": i == j,
        "cum": same & (j <= i),
        "strict": same & (j < i),
        "same": same,
        "before": j < i,
        "ones": i >= 0,
        "flip": i + j == P - 1,
    }
    for n in range(6):
        w = 1 << n
        sq[f"level{n}"] = (j // (2 * w) == i // (2 * w)) & (i // w % 2 == 1) & (j // w % 2 == 0)
    out = {"squares": np.stack([v.astype(np.float32) for v in sq.values()], 1)}
    inv = np.power(np.float32(10000.0), -np.arange(0, ROPE, 2, dtype=np.float32) / np.float32(ROPE)).astype(np.float32)
    ang = np.arange(SEQ, dtype=np.float32)[:, None] * inv[None, :]
    out["rope"] = np.stack([np.cos(ang), np.sin(ang)], 1).astype(np.float32).reshape(TT, P, 2, 16).transpose(1, 0, 2, 3).copy()
    rc = np.zeros((P, 2, PADW), np.float32)
    for g in range(4):
        r = slice(64 * (g % 2), 64 * (g % 2) + 64)
        rc[r, g // 2] = 1.0 / np.minimum(np.arange(PADW) + 1, 2 << g)
    out["pool_rc"] = rc
    kc, c = np.arange(GRID)[None, :], np.arange(GRID)[:, None]
    start = np.clip(c - NAW // 2, 0, GRID - NAW)
    m = np.where((kc >= start) & (kc < start + NAW), np.float32(0), np.float32(MASKED)).astype(np.float32)
    m = np.repeat(np.concatenate([m, m])[:, None], SLOTS, 1)
    m[:64, SLOTS - 1] = MASKED
    m[64:, EDGE] = MASKED
    out["na_mask"] = m
    out["iota"] = np.tile(np.arange(64, dtype=np.float32), (P, 1))
    out["bstart"] = (P * np.arange(BLOCKS, dtype=np.float32))[None]
    out["tokens"] = np.arange(SEQ, dtype=np.int32).reshape(TT, P).T.copy()
    return out, {k: n for n, k in enumerate(sq)}


def first_block(nc, I, K, M, sq, v, yT):
    with ExitStack() as ctx, nc.allow_non_contiguous_dma(reason="short columns of parameters"):
        def sb(name, shape, dt=F32):
            return ctx.enter_context(nc.sbuf_tensor(name, shape, dt))

        y_dram = nc.dram_tensor("y_rows", [BLOCKS * P, D], F32, kind="Internal").ap()
        ident = M["ident"]
        mod = sb("mod", [P, 6 * D])
        x = yT[:, :, :].rearrange("p k t -> p (k t)").rearrange("p (t d) -> p t d", d=D)
        stage_modulation(nc, I, mod, x)
        nmean, ss = sb("nmean", [P, TT]), sb("ss", [P, TT])
        with ExitStack() as first:
            def fb(name, shape, dt=F32):
                return first.enter_context(nc.sbuf_tensor(name, shape, dt))
            lat, zab, gqkv = fb("lat", [P, TT, LAT]), fb("zab", [P, TT, ZAB]), fb("gqkv", [P, TT, 3 * GW])
            mcol = fb("mcol", [P, 2 * KT])
            stage_columns(nc, "modcol", [(mod[0:1, 0:D], 0), (mod[0:1, D:2 * D], 1)], M["ones"], mcol)
            hT = v
            stage_features(nc, "h", x, hT, ident, scale=mcol[:, KT:], bias=mcol[:, 0:KT])
            stage_projections(nc, I, hT, ident, K, lat, zab, gqkv, yT)
            with ExitStack() as a:
                def ab(name, shape):
                    return a.enter_context(nc.sbuf_tensor(name, shape, F32))
                g, beta, gc, egc, kdf = (ab(n, [P, TT, GH]) for n in ("g", "beta", "gc", "egc", "kdf"))
                rs, o_tok, yg = ab("rs", [P, TT * 2 * GH]), ab("o_tok", [P, TT, GW]), ab("yg", [P, TT, GW])
                stage_delta_gates(nc, I, zab, gqkv, M, g, beta, gc, egc, kdf, rs)
                stage_delta_rule(nc, gqkv, M, [M[f"level{n}"] for n in range(6)], g, beta, gc, egc, kdf, rs, o_tok)
                stage_delta_out(nc, I, o_tok, zab, yg)
                stage_features(nc, "yg", yg, yT[:, 4:6], ident)
            with ExitStack() as a:
                def ab(name, shape):
                    return a.enter_context(nc.sbuf_tensor(name, shape, F32))
                rope, kr = ab("rope", [P, TT, 2, HR]), ab("kr", [P, TT, ROPE])
                cT, gains, y_tok = ab("cT", [P, 3, SEQ]), ab("gains", [P, 3]), v[:, :, 0:HEADS * VD]
                stage_load(nc, "rope", [(rope[:], K["rope"]),
                                        (gains[:, 0:2], I["mla_q_norm"][0].rearrange("(k p) -> p k", p=P)),
                                        (gains[:, 2:3], I["mla_kv_norm"][0].rearrange("(k p) -> p k", p=P))])
                stage_latent_norms(nc, lat, rope, kr)
                stage_features(nc, "cT", lat[:, :, 0:3 * P], cT, ident, scale=gains)
                stage_latent_attention(nc, I, cT, rope, kr, ident, y_tok, y_dram,
                                       sq[:, :, :].rearrange("p n c -> p (n c)")[:, 0:D])
                stage_features(nc, "ymla", y_tok, yT, ident)
            stage_mix_out(nc, I, yT, mod[:, 2 * D:3 * D], v, nmean, ss)
        h_dram = nc.dram_tensor("h_rows", [SEQ, D], F32, kind="Internal").ap()
        idx_dram = nc.dram_tensor("place_tokens", [BLOCKS * P, 1], I32, kind="Internal").ap()
        wts, dest, be = sb("wts", [P, 2 * TT]), sb("dest", [P, 2 * TT], I32), sb("be", [1, BLOCKS + 2], I32)
        with ExitStack() as a:
            h2 = a.enter_context(nc.sbuf_tensor("h2", [P, TT, D], F32))
            h2T = yT
            stage_layer_norm(nc, "ln1", I["ln1_g"], I["ln1_b"], v, nmean, ss, factor=mod[:, 4 * D:5 * D], shift=mod[:, 3 * D:4 * D],
                             h=h2, stores=[(h_dram.rearrange("(t p) d -> t p d", p=P), h2)])
            stage_features(nc, "h2T", h2, h2T, ident, spread=True)
            stage_route(nc, I, K, M, h2T, wts, dest, be, idx_dram)
        stage_experts(nc, I, M, h_dram, idx_dram, be, y_dram)
        stage_combine(nc, y_dram, dest, wts, mod[:, 5 * D:6 * D], v, nmean, ss)
        stage_layer_norm(nc, "ln2", I["ln2_g"], I["ln2_b"], v, nmean, ss)


def second_block(nc, I, K, M, hT, hh, out):
    ident, ones = M["ident"], M["ones"]
    W = lambda n: I[n + "_2"][0]
    with ExitStack() as a:
        def ab(name, shape, dt=F32):
            return a.enter_context(nc.sbuf_tensor(name, shape, dt))
        uT, ul = in_both_types(nc, a, "uT", [P, KT, SEQ])
        h_keep = nc.dram_tensor("h_keep", [P, KT, SEQ], F32, kind="Internal").ap()
        with ExitStack() as b:
            aT = b.enter_context(nc.sbuf_tensor("aT", [P, FT, SEQ], F32))
            stage_rms_features(nc, "rms1", hT, W("ffn1_norm"), ones, uT, keep=h_keep, halves=(hh, ul))
            stage_ffn(nc, "ffn1", W("ffn1_w_gate"), W("ffn1_w_up"), W("ffn1_w_down"), ul, aT, hT, hh, h_keep)
        stage_mixer(nc, I, K, M, hT, hh, uT, ul, h_keep)
        with ExitStack() as b:
            aT = b.enter_context(nc.sbuf_tensor("aT2", [P, FT, SEQ], F32))
            stage_rms_features(nc, "rms3", hT, W("ffn2_norm"), ones, uT, keep=h_keep, halves=(hh, ul))
            stage_ffn(nc, "ffn2", W("ffn2_w_gate"), W("ffn2_w_up"), W("ffn2_w_down"), ul, aT, hT, hh, h_keep)
        with ExitStack() as b:
            p_tok = b.enter_context(nc.sbuf_tensor("p_tok", [P, TT, PLE], F32))
            pT = b.enter_context(nc.sbuf_tensor("pT", [P, PLE // P, SEQ], F32))
            stage_load(nc, "ple", [(p_tok[:], I["p_2"][0, 0].rearrange("(t p) d -> p t d", p=P))])
            stage_features(nc, "pT", p_tok, pT, ident)
            uh = b.enter_context(nc.sbuf_tensor("uh", [P, KT, SEQ], F32R))
            stage_rms_features(nc, "rms4", hT, W("ple_norm"), ones, uT, halves=(uh, ul))
            rows = lambda x: x.rearrange("(k p) n -> p k n", p=P)

            def gate(act, m, j, acc, tmp):
                return act.activation(tmp[:, j], acc[0], ACT.Sigmoid)

            def add(dve, m, j, acc, tmp, st):
                st(dve.tensor_tensor(tmp[:, j], tmp[:, j], acc[1], ALU.mult))
                return dve.tensor_tensor(tile_of(hT, m), tile_of(hT, m), tmp[:, j], ALU.add)

            stage_split_linear(nc, "ple", [[(rows(W("ple_w_gate")), uh, ul)], [(rows(W("ple_w_proj")), pT)]], KT, gate, add,
                         steps=1, scratch=[P, 2, SEQ])
        stage_rms_features(nc, "rms5", hT, I["final_norm_2"], ones, uT)
        stage_store(nc, uT, ident, out)


def build(nc, I, K, sq_at, out):
    with ExitStack() as ctx, nc.allow_non_contiguous_dma(reason="short columns of parameters"):
        sq = ctx.enter_context(nc.sbuf_tensor("squares", [P, len(sq_at), P], F32))
        M = {k: sq[:, n] for k, n in sq_at.items()}
        stage_load(nc, "consts", [(sq[:], K["squares"])])
        hT, hh = in_both_types(nc, ctx, "hT", [P, KT, SEQ])
        with ExitStack() as b:
            v = b.enter_context(nc.sbuf_tensor("v", [P, TT, D], F32))
            first_block(nc, I, K, M, sq, v, hT)
            stage_features(nc, "hT", v, hT, M["ident"])
        second_block(nc, I, K, M, hT, hh, out)


_OUTS = [((1, 1024, 1024), 'float32')]


def kernel(**inputs):
    import numpy as _np
    import concourse.bacc as _bacc
    from concourse import mybir as _mybir
    from concourse.bass_utils import run_bass_kernel_spmd as _run

    nc = _bacc.Bacc("TRN2", target_bir_lowering=False, num_devices=1)
    arrays, tensors = {}, {}
    for name, value in inputs.items():
        a = _np.ascontiguousarray(value)
        arrays[f"in_{name}_dram"] = a
        tensors[name] = nc.dram_tensor(f"in_{name}_dram", a.shape, _mybir.dt.from_np(a.dtype), kind="ExternalInput").ap()
    (shape, dtype), = _OUTS
    out = nc.dram_tensor("out_0_dram", shape, _mybir.dt.from_np(_np.dtype(dtype)), kind="ExternalOutput").ap()
    tables, squares = shape_constants()
    K = {}
    for name, a in tables.items():
        arrays[f"table_{name}_dram"] = a
        K[name] = nc.dram_tensor(f"table_{name}_dram", a.shape, _mybir.dt.from_np(a.dtype), kind="ExternalInput").ap()
    build(nc, tensors, K, squares, out)
    r = _run(nc, [arrays], core_ids=[0])
    return r.results[0]["out_0_dram"]
```
